# Optimizing a Trainium2 kernel written in Bass

```python
import jax, jax.numpy as jnp
from jax import lax
import numpy as np

D_MODEL = 1024
BATCH = 1
SEQ = 1024
DEPTH = 1

D_MIX = D_MODEL
C_CONV = D_MIX // 2
V_HEAD = 64
N_HEADS = (D_MIX - C_CONV) // V_HEAD
QK_NOPE = 64
QK_ROPE = 32
QK_HEAD = QK_NOPE + QK_ROPE
Q_LORA = D_MODEL // 4
KV_LORA = D_MODEL // 8
CONV_K = 31
CONV_PAD = CONV_K // 2
D_FF = 256 * ((8 * D_MODEL // 3 + 255) // 256)
N_MOD = 9
W_IN_COLS = 2 * C_CONV + Q_LORA + KV_LORA + QK_ROPE
ROPE_THETA = 10000.0
Q_BLOCK = 128
EPS = 1e-6

kernel_name = "hybrid_conv_mla_macaron_adaln_encoder"

def _rms(x):
    xf = x.astype(jnp.float32)
    return (xf * lax.rsqrt(jnp.mean(xf * xf, axis=-1, keepdims=True) + EPS)).astype(x.dtype)

def _layernorm(x, g, b):
    xf = x.astype(jnp.float32)
    mu = jnp.mean(xf, axis=-1, keepdims=True)
    var = jnp.mean(jnp.square(xf - mu), axis=-1, keepdims=True)
    return ((xf - mu) * lax.rsqrt(var + 1e-5)).astype(x.dtype) * g + b

def _modulate(x, shift, scale):
    return _rms(x) * (1 + scale[:, None, :]) + shift[:, None, :]

def _swiglu(x, w_gate, w_up, w_down):
    return (jax.nn.silu(x @ w_gate) * (x @ w_up)) @ w_down

def _rope(x, cos, sin):
    half = x.shape[-1] // 2
    x1, x2 = x[..., :half], x[..., half:]
    return jnp.concatenate([x1 * cos - x2 * sin, x2 * cos + x1 * sin], axis=-1)

def _attention(q, k, v):
    B, S, H, Dq = q.shape
    nb = S // Q_BLOCK
    qb = q.reshape(B, nb, Q_BLOCK, H, Dq).transpose(1, 0, 2, 3, 4)
    scale = Dq ** -0.5

    def one_block(qblk):
        s = jnp.einsum('bqhd,bkhd->bhqk', qblk, k, preferred_element_type=jnp.float32) * scale
        p = jax.nn.softmax(s, axis=-1).astype(v.dtype)
        return jnp.einsum('bhqk,bkhd->bqhd', p, v)

    o = lax.map(one_block, qb)
    return o.transpose(1, 0, 2, 3, 4).reshape(B, S, H * v.shape[-1])

def setup_inputs(seed: int = 0) -> dict:
    key = jax.random.key(seed)
    ks = jax.random.split(key, 24)

    def w(k, shape, fan_in):
        return jax.random.normal(k, shape, jnp.float32) * (fan_in ** -0.5)

    def gain(k, shape):
        return 1.0 + 0.01 * jax.random.normal(k, shape, jnp.float32)

    def bias(k, shape):
        return 0.01 * jax.random.normal(k, shape, jnp.float32)

    L = DEPTH
    return {
        "x": jax.random.normal(ks[0], (BATCH, SEQ, D_MODEL), jnp.float32),
        "c": jax.random.normal(ks[1], (BATCH, D_MODEL), jnp.float32),
        "positions": jnp.broadcast_to(jnp.arange(SEQ, dtype=jnp.int32), (BATCH, SEQ)),
        "w_ada": w(ks[2], (L, D_MODEL, N_MOD * D_MODEL), D_MODEL),
        "b_ada": bias(ks[3], (L, N_MOD * D_MODEL)),
        "ffn1_wg": w(ks[4], (L, D_MODEL, D_FF), D_MODEL),
        "ffn1_wu": w(ks[5], (L, D_MODEL, D_FF), D_MODEL),
        "ffn1_wd": w(ks[6], (L, D_FF, D_MODEL), D_FF),
        "w_in": w(ks[7], (L, D_MODEL, W_IN_COLS), D_MODEL),
        "g_q_lat": gain(ks[8], (L, Q_LORA)),
        "g_kv_lat": gain(ks[9], (L, KV_LORA)),
        "w_q_up": w(ks[10], (L, Q_LORA, N_HEADS * QK_HEAD), Q_LORA),
        "w_kv_up": w(ks[11], (L, KV_LORA, N_HEADS * (QK_NOPE + V_HEAD)), KV_LORA),
        "g_q_head": gain(ks[12], (L, QK_HEAD)),
        "g_k_head": gain(ks[13], (L, QK_HEAD)),
        "conv_w": w(ks[14], (L, CONV_K, 1, C_CONV), CONV_K),
        "conv_b": bias(ks[15], (L, C_CONV)),
        "g_conv_ln": gain(ks[16], (L, C_CONV)),
        "b_conv_ln": bias(ks[17], (L, C_CONV)),
        "w_out": w(ks[18], (L, D_MIX, D_MODEL), D_MIX),
        "ffn2_wg": w(ks[19], (L, D_MODEL, D_FF), D_MODEL),
        "ffn2_wu": w(ks[20], (L, D_MODEL, D_FF), D_MODEL),
        "ffn2_wd": w(ks[21], (L, D_FF, D_MODEL), D_FF),
        "g_final": gain(ks[22], (L, D_MODEL)),
    }

def reference(x, c, positions, w_ada, b_ada, ffn1_wg, ffn1_wu, ffn1_wd, w_in,
              g_q_lat, g_kv_lat, w_q_up, w_kv_up, g_q_head, g_k_head,
              conv_w, conv_b, g_conv_ln, b_conv_ln, w_out,
              ffn2_wg, ffn2_wu, ffn2_wd, g_final):
    B, S, _ = x.shape
    inv_freq = 1.0 / (ROPE_THETA ** (jnp.arange(0, QK_ROPE, 2, dtype=jnp.float32) / QK_ROPE))
    ang = positions.astype(jnp.float32)[..., None] * inv_freq
    cos = jnp.cos(ang)[:, :, None, :].astype(x.dtype)
    sin = jnp.sin(ang)[:, :, None, :].astype(x.dtype)
    sc = jax.nn.silu(c)

    h = x
    for i in range(DEPTH):
        mod = sc @ w_ada[i] + b_ada[i]
        (sh1, s1, g1, shm, smx, gm, sh2, s2, g2) = jnp.split(mod, N_MOD, axis=-1)

        h = h + 0.5 * g1[:, None, :] * _swiglu(_modulate(h, sh1, s1), ffn1_wg[i], ffn1_wu[i], ffn1_wd[i])

        n = _modulate(h, shm, smx)
        z = n @ w_in[i]
        o1 = 2 * C_CONV
        o2 = o1 + Q_LORA
        o3 = o2 + KV_LORA
        u, cq, ckv, kr = z[..., :o1], z[..., o1:o2], z[..., o2:o3], z[..., o3:]

        a = u[..., :C_CONV] * jax.nn.sigmoid(u[..., C_CONV:])
        a = lax.conv_general_dilated(a, conv_w[i], window_strides=(1,),
                                     padding=[(CONV_PAD, CONV_PAD)],
                                     dimension_numbers=('NWC', 'WIO', 'NWC'),
                                     feature_group_count=C_CONV) + conv_b[i]
        a = jax.nn.silu(_layernorm(a, g_conv_ln[i], b_conv_ln[i]))

        q = ((_rms(cq) * g_q_lat[i]) @ w_q_up[i]).reshape(B, S, N_HEADS, QK_HEAD)
        kv = ((_rms(ckv) * g_kv_lat[i]) @ w_kv_up[i]).reshape(B, S, N_HEADS, QK_NOPE + V_HEAD)
        k_nope, v = kv[..., :QK_NOPE], kv[..., QK_NOPE:]
        k_rope = jnp.broadcast_to(kr[:, :, None, :], (B, S, N_HEADS, QK_ROPE))
        k = jnp.concatenate([k_nope, k_rope], axis=-1)
        q = _rms(q) * g_q_head[i]
        k = _rms(k) * g_k_head[i]
        q = jnp.concatenate([q[..., :QK_NOPE], _rope(q[..., QK_NOPE:], cos, sin)], axis=-1)
        k = jnp.concatenate([k[..., :QK_NOPE], _rope(k[..., QK_NOPE:], cos, sin)], axis=-1)
        att = _attention(q, k, v)

        mix = jnp.concatenate([a, att], axis=-1) @ w_out[i]
        h = h + gm[:, None, :] * mix

        h = h + 0.5 * g2[:, None, :] * _swiglu(_modulate(h, sh2, s2), ffn2_wg[i], ffn2_wu[i], ffn2_wd[i])

        h = _rms(h) * g_final[i]
    return h


_drawn_inputs = setup_inputs


def setup_inputs(seed=0):
    import zlib

    import numpy as np

    out = dict(_drawn_inputs(seed))
    spreads = {}
    factors = {'b_ada': 4.855,
     'g_q_lat': 8.0,
     'g_kv_lat': 8.0,
     'g_q_head': 8.0,
     'g_k_head': 8.0,
     'conv_b': 8.0,
     'g_conv_ln': 8.0,
     'b_conv_ln': 8.0,
     'g_final': 5.628}
    for name, (base, spread) in spreads.items():
        noise = np.random.default_rng([zlib.crc32(name.encode()), seed]).standard_normal(out[name].shape)
        drawn = base * np.exp(spread * noise) if base else spread * noise
        out[name] = __import__('jax').numpy.asarray(drawn.astype(out[name].dtype))
    for name, factor in factors.items():
        out[name] = (out[name] * factor).astype(out[name].dtype)
    return out
```

```python
from contextlib import ExitStack

import numpy as np

import concourse.bass as bass
from concourse import mybir
from concourse.alu_op_type import AluOpType as ALU

ACT = mybir.ActivationFunctionType
AX_X = mybir.AxisListType.X
F32 = mybir.dt.float32
F32R = mybir.dt.float32r
I32 = mybir.dt.int32

P = 128
HALF = 512
EPS = 1e-6

HI, LO = 0, 1
PASSES = ((HI, HI), (HI, LO), (LO, HI))


def build(nc, A, out, dump=None, stop=99):
    D = A["x"].shape[2]
    S = A["x"].shape[1]
    FF = A["ffn1_wg"].shape[2]
    KC = D // P
    NT = S // P
    NH = S // HALF
    THALF = NT // NH
    CPG = 2
    GROUPS = FF // (CPG * P)
    GW = CPG * P
    CH = A["conv_b"].shape[1]
    CONV_K = A["conv_w"].shape[1]
    QL, KVL = A["g_q_lat"].shape[1], A["g_kv_lat"].shape[1]
    QK = A["g_q_head"].shape[1]
    NHD = A["w_q_up"].shape[2] // QK
    VH = (D - CH) // NHD
    NOPE = A["w_kv_up"].shape[2] // NHD - VH
    ROPE = QK - NOPE
    W_IN_L = QL + KVL + ROPE
    N_MOD = A["w_ada"].shape[2] // D
    SH1, S1, G1, SHM, SMX, GM, SH2, S2, G2 = range(N_MOD)

    x_d = A["x"][0].rearrange("(t p) d -> p t d", p=P)
    out_d = out[0].rearrange("(t p) d -> p t d", p=P)
    ada_d = A["w_ada"][0].rearrange("(k p) n -> p k n", p=P)
    ffn_w = []
    for n in (1, 2):
        ffn_w.append(tuple(A[f"ffn{n}_{w}"][0].rearrange("(k p) n -> p k n", p=P) for w in ("wg", "wu", "wd")))

    win_d = A["w_in"][0].rearrange("(k p) n -> p k n", p=P)
    glu_w = (win_d[:, :, CH:2 * CH], win_d[:, :, 0:CH])
    CONV_PAD = CONV_K // 2
    LN_VAR = 11
    INV_FREQ = [float(np.float32(1) / np.float32(np.float32(10000.0) ** np.float32(j / ROPE))) for j in range(0, ROPE, 2)]
    ROUND = 12582912.0
    TWO_PI = (6.28125, 0.0019354820251464844, 2 * np.pi - 6.28125 - 0.0019354820251464844)
    PI_IN = 3.1415925

    with ExitStack() as ctx:
        def sem(name):
            return ctx.enter_context(nc.semaphore(name))

        def region(size, *variants):
            made = []
            for v in variants:
                with ExitStack() as inner:
                    used = 0
                    for name, shape, dt in v:
                        used += int(np.prod(shape[1:])) * 4
                        made.append(inner.enter_context(nc.sbuf_tensor(name, shape, dt)))
                    assert used <= size, (v, used, size)
            ctx.enter_context(nc.sbuf_tensor(f"region_{made[0].name}", [P, size // 4], F32))
            return made

        def sb(name, shape, dt=F32):
            return ctx.enter_context(nc.sbuf_tensor(name, shape, dt))

        KB = 1024
        ident = sb("ident", [P, P])
        ones = sb("ones", [P, P])
        CC = CH // P
        V_BADA, V_C = 0, N_MOD * KC
        V_CB = V_C + KC
        V_LG, V_LB = V_CB + CC, V_CB + 2 * CC
        V_GQ, V_GKV = V_CB + 3 * CC, V_CB + 3 * CC + QL // P
        NV = V_GKV + KVL // P
        vect = sb("vect", [P, NV])
        silu_c = sb("silu_c", [P, KC])
        half_b = sb("half_b", [P, N_MOD * KC])
        modc = sb("modc", [P, N_MOD * KC])
        stat = sb("stat", [P, 4 * NT])
        zstat = sb("zstat", [P, 6 * NT])
        mhalf = sb("mhalf", [P, 2 * NT])
        gains = sb("gains", [P, 2])
        soft = sb("soft", [P, 12])
        NZ = W_IN_L // 2
        ACW = S + CONV_K + 1
        H, ac, wq, kr, cs, cw, grot, rqk, _ac2, prod = region(
            32 * KB, [("H", [P, NT, D], F32)],
            [("ac", [P, CC, ACW], F32), ("wq", [P, 2, QL // P, NHD * QK], F32R), ("kr", [P, NT, ROPE], F32),
             ("cs", [P, NT, ROPE], F32), ("cw", [P, CC, CONV_K + 2], F32), ("grot", [P, 2, ROPE], F32),
             ("rqk", [P, NT, 2 * NHD], F32)],
            [("_ac2", [P, CC, ACW], F32), ("prod", [P, 2, S], F32)])
        xh, xl, ada01, qn, kn, vn, vs, wo = region(
            64 * KB, [("xh", [P, KC, S], F32R), ("xl", [P, KC, S], F32R)],
            [("ada01", [P, 2, KC, D], F32)],
            [("qn", [P, NT, NHD, QK], F32), ("kn", [P, NT, NHD, NOPE], F32), ("vn", [P, NT, NHD, VH], F32),
             ("vs", [P, 2, NT, 2 * VH], F32R)],
            [("wo", [P, KC, 2, D], F32R)])
        X = (xh, xl)
        W1, pth, ptl, sq, rt, qs, qh = region(
            32 * KB, [("W1", [P, CPG, 2, 2, KC, P], F32R)],
            [("pth", [P, NT, HALF], F32R), ("ptl", [P, NT, HALF], F32R)],
            [("sq", [P, 2, NHD * (QK + NOPE)], F32), ("rt", [P, 4, NT, NHD, ROPE // 2], F32),
             ("qs", [P, NT, 2 * NHD], F32), ("qh", [P, NT, 2 * NHD], F32)])
        PT = (pth, ptl)
        AT, XS, wl, czh, czl, qkT, _x4, mixT = region(
            32 * KB, [("AT", [P, 2, CPG, 2, S], F32R)], [("XS", [P, NT, D], F32)],
            [("wl", [P, 2, KC, W_IN_L], F32R)],
            [("czh", [P, 3, S], F32R), ("czl", [P, 3, S], F32R)],
            [("qkT", [P, 2, 2, 2, S], F32R)],
            [("_x4", [P, NT // 2, D], F32), ("mixT", [P, 2, 2, KC, P], F32R)])
        CZ = (czh, czl)
        rawg, rawu, rawd, vec, wqr, _u2, latb, _g3, _u3, wkv, slot, _s2, att, wor = region(
            24 * KB, [("rawg", [P, KC, GW], F32), ("rawu", [P, KC, GW], F32), ("rawd", [P, CPG, D], F32)],
            [("vec", [NV, P], F32)],
            [("wqr", [P, QL // P, 1024], F32), ("_u2", [P, KC, GW], F32), ("latb", [P, KC, NZ], F32)],
            [("_g3", [P, KC, GW], F32), ("_u3", [P, KC, GW], F32), ("wkv", [P, 2, NHD * 2 * NOPE], F32R)],
            [("slot", [P, 2, NT, QK], F32), ("_s2", [P, 512], F32), ("att", [P, CC, S], F32)],
            [("wor", [P, 2, D], F32)])
        wkr = rawu[:].rearrange("p k n -> p (k n)")[:, 0:NHD * 2 * NOPE]
        WD, cv, trig = region(16 * KB, [("WD", [P, CPG, 2, D], F32R)], [("cv", [P, CC, S], F32)],
                              [("trig", [P, 4, NT, ROPE], F32)])
        ada_raw, ada_acc, lata, cwr, posr, posf, posc, zz, pp = region(
            12 * KB, [("ada_raw", [P, 2, D], F32), ("ada_acc", [P, D], F32)],
            [("lata", [P, KC, NZ], F32), ("cwr", [P, CH], F32), ("posr", [NT, P], I32), ("posf", [NT, P], F32),
             ("posc", [P, NT], F32)],
            [("zz", [P, NT, QL + KVL], F32)],
            [("pp", [P, 2, S], F32)])
        tmp = sb("tmp", [P, 2, HALF])
        grow = sb("grow", [P, D])
        ps = ctx.enter_context(nc.psum_tensor("ps", [P, 8, HALF], F32))
        MISC = 7

        vec_in = sem("vec_in")
        x_in = [sem(f"x_in{t}") for t in range(NT)]
        ada_in = [sem(f"ada_in{n}") for n in range(2)]
        consts = sem("consts")
        vec_tr = sem("vec_tr")
        vec_ok = sem("vec_ok")
        silu_ok = sem("silu_ok")
        ada01_in = [[sem(f"ada{v}_in{k}") for k in range(KC // 2)] for v in range(2)]
        acc_ok = sem("acc_ok")
        acc_used = sem("acc_used")
        mod_ok = sem("mod_ok")
        ada_step = sem("ada_step")
        row_src = sem("row_src")
        row_mm = sem("row_mm")
        row_ok = sem("row_ok")
        final_out = sem("final_out")
        h_dram = nc.dram_tensor("h_saved_rows", (P, NT, D), F32).ap()

        class Sems:
            pass

        sumsq, mean_sq, rms_inv = sem("sumsq"), sem("mean_sq"), sem("rms_inv")

        def norm_sems(n, before):
            g = Sems()
            g.base = before * NT
            g.scaled, g.turned, g.modulated, g.x_hi, g.x_lo = (sem(f"{n}_{what}") for what in (
                "scaled", "turned", "modulated", "x_hi", "x_lo"))
            return g

        def gate_up_sems(n):
            g = Sems()
            g.g_in, g.u_in, g.gu_hi, g.gu_lo, g.gu_mm, g.silu, g.mul = (sem(f"{n}_{what}") for what in (
                "g_in", "u_in", "gu_hi", "gu_lo", "gu_mm", "silu", "mul"))
            return g

        def ffn_sems(n):
            g = gate_up_sems(n)
            g.d_in, g.d_scaled, g.d_hi, g.d_lo, g.a_hi, g.a_lo, g.down_mm, g.added = (sem(f"{n}_{what}") for what in (
                "d_in", "d_scaled", "d_hi", "d_lo", "a_hi", "a_lo", "down_mm", "added"))
            return g

        ns = [norm_sems("norm1", 0), norm_sems("norm_mix", 1), norm_sems("norm2", 2)]
        FINAL = 3 * NT
        fs = [ffn_sems("ffn1"), ffn_sems("ffn2")]
        U = gate_up_sems("glu")
        h_saved, h_back = sem("h_saved"), [sem(f"h_back{n}") for n in range(2)]
        small_in, lat_in = sem("small_in"), [sem("lat_in0"), sem("lat_in1")]
        up_in = [sem("wq_in"), sem("wkv_in")]
        pads, pos_ok, trig_ok, cw_ok = sem("pads"), sem("pos_ok"), sem("trig_ok"), sem("cw_ok")
        wl_hi, wl_lo, lat_mm, z_ok, z_sq, z_rstd = (sem(n) for n in (
            "wl_hi", "wl_lo", "lat_mm", "z_ok", "z_sq", "z_rstd"))
        z_turned, z_hi, z_lo = sem("z_turned"), sem("z_hi"), sem("z_lo")
        up_scaled, up_hi, up_lo, up_mm, up_out = (sem(n) for n in ("up_scaled", "up_hi", "up_lo", "up_mm", "up_out"))
        qk_sq, qk_sum_t, qk_sum, qk_rstd, rope = (sem(n) for n in ("qk_sq", "qk_sum_t", "qk_sum", "qk_rstd", "rope"))
        grot_in, dve_step, cs_ok, tap0 = sem("grot_in"), sem("dve_step"), sem("cs_ok"), sem("tap0")
        conv = sem("conv")
        prod_ok, conv_add = sem("prod_ok"), sem("conv_add")
        slot_q, slot_k, v_cut = sem("slot_q"), sem("slot_k"), sem("v_cut")
        qk_turned, qk_y, qk_hi, qk_lo = sem("qk_turned"), sem("qk_y"), sem("qk_hi"), sem("qk_lo")
        s_mm, s_max, s_exp, s_rec, s_norm = (sem(n) for n in ("s_mm", "s_max", "s_exp", "s_rec", "s_norm"))
        p_turned, p_hi, p_lo, pv_mm, pv_low, pv_out = (sem(n) for n in (
            "p_turned", "p_hi", "p_lo", "pv_mm", "pv_low", "pv_out"))
        ln_step, ln_mm, ln_act, ln_pool = sem("ln_step"), sem("ln_mm"), sem("ln_act"), sem("ln_pool")
        wo_in, wo_scaled, wo_hi, wo_lo = [sem("wo_in0"), sem("wo_in1")], sem("wo_scaled"), sem("wo_hi"), sem("wo_lo")
        mix_hi, mix_lo, mix_mm, mix_added = sem("mix_hi"), sem("mix_lo"), sem("mix_mm"), sem("mix_added")
        gfin_in, o_ok = sem("gfin_in"), sem("o_ok")

        def sp_load_gu(e, f, w, g):
            if isinstance(g, int) and g == 0:
                pass
            else:
                e.wait_ge(f.gu_lo, g * (2 * CPG))
            e.dma_start(rawg[:], w[0][:, :, bass.ds(g * GW, GW)]).then_inc(f.g_in, 16)
            e.dma_start(rawu[:], w[1][:, :, bass.ds(g * GW, GW)]).then_inc(f.u_in, 16)

        def sp_load_d(e, f, w, g):
            if not (isinstance(g, int) and g == 0):
                e.wait_ge(f.d_lo, g * CPG)
            e.dma_start(rawd[:], w[2][:, bass.ds(g * CPG, CPG), :]).then_inc(f.d_in, 16)

        def act_hi_gu(e, f, g, c, gate_free):
            for m, (raw, arrived) in enumerate(((rawg, f.g_in), (rawu, f.u_in))):
                e.wait_ge(arrived, g * 16 + 16)
                if m == 0 and gate_free is not None:
                    e.wait_ge(f.gu_mm, gate_free)
                e.activation(W1[:, c, m, HI], raw[:, :, c * P:(c + 1) * P], ACT.Copy).then_inc(f.gu_hi, 1)

        def dve_lo_gu(e, f, g, c, m):
            raw = (rawg, rawu)[m]
            e.wait_ge(f.gu_hi, g * (2 * CPG) + (2 * c + m + 1))
            e.tensor_tensor(W1[:, c, m, LO], raw[:, :, c * P:(c + 1) * P], W1[:, c, m, HI].bitcast(F32),
                            ALU.subtract).then_inc(f.gu_lo, 1)

        def dve_scale_d(e, f, g):
            e.wait_ge(f.d_in, g * 16 + 16)
            for c in range(CPG):
                e.tensor_tensor(rawd[:, c], rawd[:, c], grow[:], ALU.mult).then_inc(f.d_scaled, 1)

        def act_hi_d(e, f, g):
            for c in range(CPG):
                e.wait_ge(f.d_scaled, g * CPG + c + 1)
                e.activation(WD[:, c, HI], rawd[:, c], ACT.Copy).then_inc(f.d_hi, 1)

        def dve_lo_d(e, f, g):
            for c in range(CPG):
                e.wait_ge(f.d_hi, g * CPG + c + 1)
                e.tensor_tensor(WD[:, c, LO], rawd[:, c], WD[:, c, HI].bitcast(F32), ALU.subtract).then_inc(f.d_lo, 1)

        STEPS = [(0, 0), (0, 1), (1, 0), (1, 1)]
        FIRST_STEPS = [(0, 0), (1, 0), (0, 1), (1, 1)]

        def pe_gateup(e, f, n, g, first=False, after={}):
            for s, (c, h) in enumerate(FIRST_STEPS if first else STEPS):
                if first and s in (0, 2):
                    e.wait_ge(n.x_lo, KC * (h + 1))
                e.wait_ge(f.gu_lo, g * (2 * CPG) + 2 * c + 2)
                if not (first and s < 2):
                    e.wait_ge(f.mul, g * 4 + s - 1)
                for m in range(2):
                    bank = 2 * (s % 2) + m
                    k = 0
                    for kc in range(KC):
                        for wx, xx in PASSES:
                            mm = e.matmul(ps[:, bank], W1[:, c, m, wx, kc], X[xx][:, kc, h * HALF:(h + 1) * HALF],
                                          start=(k == 0), stop=(k == 3 * KC - 1))
                            k += 1
                mm.then_inc(f.gu_mm, 1)
                if s in after:
                    after[s]()

        def act_silu(e, f, n, g, s):
            e.wait_ge(f.gu_mm, g * 4 + s + 1)
            if not (isinstance(g, int) and g == 0 and s < 2):
                e.wait_ge(f.a_lo, g * 4 + s - 1)
            else:
                e.wait_ge(n.x_lo, NH * KC)
            e.activation(tmp[:, s % 2], ps[:, 2 * (s % 2)], ACT.Silu).then_inc(f.silu, 1)

        def dve_hidden(e, f, g, par, s, steps=STEPS):
            c, h = steps[s]
            tok = slice(h * HALF, (h + 1) * HALF)
            e.wait_ge(f.silu, g * 4 + s + 1)
            e.tensor_tensor(tmp[:, s % 2], ps[:, 2 * (s % 2) + 1], tmp[:, s % 2], ALU.mult).then_inc(f.mul, 1)
            e.wait_ge(f.mul, g * 4 + s + 1)
            e.tensor_copy(AT[:, par, c, HI, tok], tmp[:, s % 2]).then_inc(f.a_hi, 1)
            e.wait_ge(f.a_hi, g * 4 + s + 1)
            e.tensor_tensor(AT[:, par, c, LO, tok], tmp[:, s % 2], AT[:, par, c, HI, tok].bitcast(F32),
                            ALU.subtract).then_inc(f.a_lo, 1)

        DB = 3

        def pe_down(e, f, g, par, ks):
            for k in ks:
                t, h = divmod(k, 2)
                if k == 0:
                    e.wait_ge(f.a_lo, g * 4 + 4)
                    e.wait_ge(f.d_lo, g * CPG + CPG)
                if k >= DB:
                    e.wait_ge(f.added, g * (2 * NT) + k - DB + 1)
                n = 0
                for c in range(CPG):
                    for wx, ax in PASSES:
                        mm = e.matmul(ps[:, 4 + k % DB], AT[:, par, c, ax, t * P:(t + 1) * P],
                                      WD[:, c, wx, h * HALF:(h + 1) * HALF], start=(n == 0), stop=(n == 3 * CPG - 1))
                        n += 1
                mm.then_inc(f.down_mm, 1)

        def dve_add(e, f, g, ks):
            for k in ks:
                t, h = divmod(k, 2)
                e.wait_ge(f.down_mm, g * (2 * NT) + k + 1)
                dst = H[:, t, h * HALF:(h + 1) * HALF]
                e.tensor_tensor(dst, ps[:, 4 + k % DB], dst, ALU.add).then_inc(f.added, 1)

        def act_norm_tiles(e, n, tiles, ready):
            def square(t):
                ready(e, t)
                e.activation(XS[:, t], H[:, t], ACT.Square, accum_out=stat[:, t:t + 1]).then_inc(sumsq, 1)

            def scale(t):
                e.wait_ge(rms_inv, n.base + t + 1)
                e.activation(XS[:, t], H[:, t], ACT.Copy, scale=stat[:, 2 * NT + t:2 * NT + t + 1]).then_inc(n.scaled, 1)

            square(tiles[0])
            for t in tiles[1:]:
                square(t)
                scale(t - 1)
            scale(tiles[-1])

        def pool_rstd(e, base):
            for t in range(NT):
                e.wait_ge(sumsq, base + t + 1)
                e.tensor_scalar(stat[:, NT + t:NT + t + 1], stat[:, t:t + 1], 1.0 / D, EPS, ALU.mult, ALU.add)\
                    .then_inc(mean_sq, 1)
                e.wait_ge(mean_sq, base + t + 1)
                e.tensor_tensor(stat[:, 2 * NT + t:2 * NT + t + 1], stat[:, NT + t:NT + t + 1], mhalf[:, t:t + 1],
                                ALU.pow).then_inc(rms_inv, 1)

        TB = 4

        def pe_turn(e, n, h):
            e.wait_ge(n.scaled, THALF * (h + 1))
            for kc in range(KC):
                u = h * KC + kc
                if kc >= TB:
                    e.wait_ge(n.modulated, u - TB + 1)
                for j in range(THALF):
                    mm = e.transpose(ps[:, h * TB + kc % TB, j * P:(j + 1) * P],
                                     XS[:, h * THALF + j, kc * P:(kc + 1) * P], ident[:])
                mm.then_inc(n.turned, 1)

        def act_modulate(e, n, shift, scale, h):
            for kc in range(KC):
                u = h * KC + kc
                e.wait_ge(n.turned, u + 1)
                if u >= 2:
                    e.wait_ge(n.x_lo, u - 1)
                e.activation(tmp[:, u % 2], ps[:, h * TB + kc % TB], ACT.Identity, bias=modc[:, shift * KC + kc:shift * KC + kc + 1],
                             scale=modc[:, scale * KC + kc:scale * KC + kc + 1]).then_inc(n.modulated, 1)

        def dve_cut_x(e, n, h, kcs=range(KC)):
            for kc in kcs:
                u = h * KC + kc
                tok = slice(h * HALF, (h + 1) * HALF)
                e.wait_ge(n.modulated, u + 1)
                e.tensor_copy(xh[:, kc, tok], tmp[:, u % 2]).then_inc(n.x_hi, 1)
                e.wait_ge(n.x_hi, u + 1)
                e.tensor_tensor(xl[:, kc, tok], tmp[:, u % 2], xh[:, kc, tok].bitcast(F32), ALU.subtract)\
                    .then_inc(n.x_lo, 1)

        def sp_ada_piece(e, v, kc):
            j = (v - 2) * KC + kc
            if not (isinstance(v, int) and v == 2 and kc < 2):
                e.wait_ge(ada_step, v * KC + kc - 1)
            e.dma_start(ada_raw[:, kc % 2], ada_d[:, kc, bass.ds(v * D, D)]).then_inc(ada_in[kc % 2], 16)

        def dve_ada_piece(e, v, kc, src=None):
            if src is None:
                src = ada_raw[:, kc % 2]
                e.wait_ge(ada_in[kc % 2], (v - 2) * (16 * KC // 2) + (kc // 2) * 16 + 16)
            if kc == 0:
                if not (isinstance(v, int) and v == 0):
                    e.wait_ge(acc_used, v)
                e.tensor_scalar(ada_acc[:], src, silu_c[:, kc:kc + 1], None, ALU.mult).then_inc(ada_step, 1)
            else:
                e.wait_ge(ada_step, v * KC + kc)
                e.scalar_tensor_tensor(out=ada_acc[:], in0=src, scalar=silu_c[:, kc:kc + 1], in1=ada_acc[:],
                                       op0=ALU.mult, op1=ALU.add).then_inc(ada_step, 1)

        def pe_ada_sum(e, v):
            e.wait_ge(ada_step, v * KC + KC)
            if not (isinstance(v, int) and v == 0):
                e.wait_ge(mod_ok, v)
            for j in range(KC):
                mm = e.matmul(ps[:, MISC, j:j + 1], ada_acc[:, j * P:(j + 1) * P], ones[:, 0:1], start=True, stop=True)
            mm.then_inc(acc_used, 1)

        def dve_ada_column(e, v, kind):
            e.wait_ge(acc_used, v + 1)
            cols = bass.ds(v * KC, KC)
            src = ps[:, MISC, 0:KC]
            if kind == "scale":
                e.scalar_tensor_tensor(out=modc[:, cols], in0=src, scalar=1.0, in1=vect[:, cols], op0=ALU.add,
                                       op1=ALU.add).then_inc(mod_ok, 1)
            elif kind == "half":
                e.scalar_tensor_tensor(out=modc[:, cols], in0=src, scalar=0.5, in1=half_b[:, cols], op0=ALU.mult,
                                       op1=ALU.add).then_inc(mod_ok, 1)
            else:
                e.tensor_tensor(modc[:, cols], src, vect[:, cols], ALU.add).then_inc(mod_ok, 1)

        KIND = {S1: "scale", SMX: "scale", S2: "scale", G1: "half", G2: "half"}

        def dve_row_diag(e, r, v):
            e.tensor_tensor(grow[:].rearrange("p (k j) -> p k j", k=KC), ident[:].unsqueeze(1).broadcast_to([P, KC, P]),
                            modc[:, v * KC:(v + 1) * KC].unsqueeze(2).broadcast_to([P, KC, P]), ALU.mult).then_inc(row_src, 1)

        ROW_BANKS = (MISC, 4)

        def pe_row(e, r):
            e.wait_ge(row_src, r + 1)
            for h in range(2):
                mm = e.matmul(ps[:, ROW_BANKS[h]], ones[:], grow[:, h * HALF:(h + 1) * HALF], start=True, stop=True)
            mm.then_inc(row_mm, 1)

        def dve_row_copy(e, r):
            e.wait_ge(row_mm, r + 1)
            for h in range(2):
                e.tensor_copy(grow[:, h * HALF:(h + 1) * HALF], ps[:, ROW_BANKS[h]]).then_inc(row_ok, 1)

        LAST = (GROUPS - 1) // 2 - 1

        def sp_ffn(e, f, w, ada):
            def turn(i, last):
                for j in (1, 2):
                    g = i * 2 + j
                    sp_load_d(e, f, w, g)
                    if ada:
                        for kc in range(KC // 2 * (j - 1), KC // 2 * j):
                            sp_ada_piece(e, i + SMX, kc)
                    if not (last and j == 2):
                        sp_load_gu(e, f, w, g + 1)

            with e.Fori(0, LAST) as i:
                turn(i, False)
            turn(LAST, True)

        def act_ffn(e, f, n):
            def period(g, first, last):
                if not first:
                    act_hi_d(e, f, g - 1)
                act_silu(e, f, n, g, 0)
                act_silu(e, f, n, g, 1)
                if not last and not first:
                    act_hi_gu(e, f, g + 1, 0, g * 4 + 2)
                act_silu(e, f, n, g, 2)
                act_silu(e, f, n, g, 3)
                if not last:
                    if first:
                        act_hi_gu(e, f, g + 1, 0, g * 4 + 3)
                    act_hi_gu(e, f, g + 1, 1, g * 4 + 4)

            period(0, True, False)
            with e.Fori(0, LAST) as i:
                period(i * 2 + 1, False, False)
                period(i * 2 + 2, False, False)
            period(2 * LAST + 1, False, False)
            period(2 * LAST + 2, False, True)
            act_hi_d(e, f, GROUPS - 1)

        def dve_period(e, f, g, par, last, pieces):
            pieces = list(pieces)

            def some(k):
                for _ in range(min(k, len(pieces))):
                    dve_ada_piece(e, *pieces.pop(0))

            dve_scale_d(e, f, g - 1)
            dve_lo_d(e, f, g - 1)
            dve_hidden(e, f, g, par, 0)
            some(2)
            dve_hidden(e, f, g, par, 1)
            if not last:
                dve_lo_gu(e, f, g + 1, 0, 0)
                dve_lo_gu(e, f, g + 1, 0, 1)
            dve_hidden(e, f, g, par, 2)
            some(2)
            dve_hidden(e, f, g, par, 3)
            dve_add(e, f, g - 1, range(0, 4))
            if not last:
                dve_lo_gu(e, f, g + 1, 1, 0)
            dve_add(e, f, g - 1, range(4, 8))
            if not last:
                dve_lo_gu(e, f, g + 1, 1, 1)
            dve_add(e, f, g - 1, range(8, 2 * NT))

        def dve_first(e, f, row, before_row, after_row):
            dve_hidden(e, f, 0, 0, 0, FIRST_STEPS)
            dve_hidden(e, f, 0, 0, 1, FIRST_STEPS)
            before_row()
            dve_hidden(e, f, 0, 0, 2, FIRST_STEPS)
            after_row()
            for m in range(2):
                dve_lo_gu(e, f, 1, 0, m)
            dve_hidden(e, f, 0, 0, 3, FIRST_STEPS)
            for m in range(2):
                dve_lo_gu(e, f, 1, 1, m)

        def dve_turns(e, f, ada):
            def turn(i, last):
                for j, par in ((1, 1), (2, 0)):
                    half = range(KC // 2 * (j - 1), KC // 2 * j)
                    dve_period(e, f, i * 2 + j, par, last and j == 2, [(i + SMX, kc) for kc in half] if ada else [])
                if ada:
                    dve_ada_column(e, i + SMX, None)

            with e.Fori(0, LAST) as i:
                turn(i, False)
            turn(LAST, True)
            dve_scale_d(e, f, GROUPS - 1)
            dve_lo_d(e, f, GROUPS - 1)

        def pe_turns(e, f, n, ada):
            def turn(i):
                for j, par in ((1, 1), (2, 0)):
                    g = i * 2 + j
                    pe_gateup(e, f, n, g)
                    pe_down(e, f, g - 1, 1 - par, range(2 * NT))
                if ada:
                    pe_ada_sum(e, i + SMX)

            with e.Fori(0, LAST) as i:
                turn(i)
            turn(LAST)

        def dve_last_adds_and_cut(e, f, n):
            dve_add(e, f, GROUPS - 1, range(0, 12))
            for k in range(4):
                dve_cut_x(e, n, 0, range(2 * k, 2 * k + 2))
                dve_add(e, f, GROUPS - 1, [12 + k])

        NJ = 2 * NT
        TURNS = NHD // 2

        def at(i, j):
            return (i + 1, j - NJ) if j >= NJ else (i, j)

        def pe_scores(e, i, j):
            i, j = at(i, j)
            hp, t = divmod(j, NT)
            if t == 0:
                e.wait_ge(qk_lo, i * 8 + (hp * 4 + 4))
            if not (isinstance(i, int) and i == 0 and j < 2):
                e.wait_ge(s_exp, i * NJ + (j - 1))
            for h in range(NH):
                for k, (a, b) in enumerate(PASSES):
                    mm = e.matmul(ps[:, 2 * (j % 2) + h], qkT[0:QK, hp, 0, a, t * P:(t + 1) * P],
                                  qkT[0:QK, hp, 1, b, h * HALF:(h + 1) * HALF], start=(k == 0), stop=(k == 2))
            mm.then_inc(s_mm, 1)

        def pe_turn_p(e, i, j, first):
            e.wait_ge(s_norm, i * NJ + (j + 1))
            for b in range(2):
                if not (first and j == 0):
                    e.wait_ge(p_lo, i * (2 * NJ) + (2 * j + b - 1))
                for k in range(THALF):
                    mm = e.transpose(ps[:, 4 + b, k * P:(k + 1) * P],
                                     pp[:, j % 2, (b * THALF + k) * P:(b * THALF + k + 1) * P], ident[:])
                mm.then_inc(p_turned, 1)

        def pe_pv(e, i, j):
            hp = ((j - 1) % NJ) // NT
            e.wait_ge(p_lo, i * (2 * NJ) + 2 * j)
            if not (isinstance(i, int) and i == 0 and j == THALF):
                e.wait_ge(pv_out, i * 4 + (j // THALF - 1))
            if j % NT == THALF:
                e.wait_ge(v_cut, i * 4 + (hp * 2 + 2))
            for kt in range(NT):
                for a in (HI, LO):
                    mm = e.matmul(ps[:, 6], vs[:, hp, kt], PT[a][:, kt], start=(kt == 0 and a == HI),
                                  stop=(kt == NT - 1 and a == LO))
            mm.then_inc(pv_mm, 1)

        def pe_turn_head(e, i, hp, u, first=False):
            e.wait_ge((slot_q, slot_k)[u // 2], i * 2 + (hp + 1))
            if not (first and u == 0):
                e.wait_ge(qk_y, i * 8 + (hp * 4 + u))
            for k in range(THALF):
                mm = e.transpose(ps[0:QK, 7, k * P:(k + 1) * P], slot[:, u // 2, (u % 2) * THALF + k], ident[:])
            mm.then_inc(qk_turned, 1)

        def act_head_unit(e, i, hp, u, first=False):
            e.wait_ge(qk_turned, i * 8 + (hp * 4 + u + 1))
            if not (first and u < 2):
                e.wait_ge(qk_lo, i * 8 + (hp * 4 + u - 1))
            e.activation(tmp[0:QK, u % 2], ps[0:QK, 7], ACT.Copy, scale=gains[0:QK, u // 2:u // 2 + 1]).then_inc(qk_y, 1)

        def dve_head_unit(e, i, hp, u):
            qk, h = divmod(u, 2)
            tok = slice(h * HALF, (h + 1) * HALF)
            e.wait_ge(qk_y, i * 8 + (hp * 4 + u + 1))
            e.tensor_copy(qkT[0:QK, hp, qk, HI, tok], tmp[0:QK, u % 2]).then_inc(qk_hi, 1)
            e.wait_ge(qk_hi, i * 8 + (hp * 4 + u + 1))
            e.tensor_tensor(qkT[0:QK, hp, qk, LO, tok], tmp[0:QK, u % 2], qkT[0:QK, hp, qk, HI, tok].bitcast(F32),
                            ALU.subtract).then_inc(qk_lo, 1)

        def pool_slots(e, i, hp, first=False):
            hd = i * 2 + hp
            r = rqk[:, :, bass.ds(hd, 1)]
            if not first:
                e.wait_ge(qk_turned, hd * 4 - 2)
            e.tensor_tensor(slot[:, 0], qn[:, :, bass.ds(hd, 1), :].rearrange("p t a d -> p t (a d)"),
                            r.broadcast_to([P, NT, QK]), ALU.mult).then_inc(slot_q, 1)
            if not first:
                e.wait_ge(qk_turned, hd * 4)
            r = rqk[:, :, bass.ds(hd + NHD, 1)]
            e.tensor_tensor(slot[:, 1, :, 0:NOPE], kn[:, :, bass.ds(hd, 1), :].rearrange("p t a d -> p t (a d)"),
                            r.broadcast_to([P, NT, NOPE]), ALU.mult)
            e.tensor_tensor(slot[:, 1, :, NOPE:QK], kr[:], r.broadcast_to([P, NT, ROPE]), ALU.mult).then_inc(slot_k, 1)

        def dve_v(e, i, hp, first=False):
            hd = i * 2 + hp
            src = vn[:, :, bass.ds(hd, 1), :].rearrange("p t a d -> p t (a d)")
            if not first:
                e.wait_ge(pv_mm, hd * 2 - 2)
            e.tensor_copy(vs[:, hp, :, 0:VH], src).then_inc(v_cut, 1)
            e.wait_ge(v_cut, hd * 2 + 1)
            e.tensor_tensor(vs[:, hp, :, VH:2 * VH], src, vs[:, hp, :, 0:VH].bitcast(F32), ALU.subtract)\
                .then_inc(v_cut, 1)

        def dve_max(e, i, j):
            i, j = at(i, j)
            e.wait_ge(s_mm, i * NJ + (j + 1))
            e.tensor_reduce(soft[:, j % 4:j % 4 + 1], ps[:, 2 * (j % 2):2 * (j % 2) + 2].rearrange("p b k -> p (b k)"),
                            AX_X, ALU.max, negate=True).then_inc(s_max, 1)

        def act_exp(e, i, j):
            i, j = at(i, j)
            e.wait_ge(s_max, i * NJ + (j + 1))
            if not (isinstance(i, int) and i == 0 and j < 2):
                e.wait_ge(p_turned, i * (2 * NJ) + (2 * j - 2))
            e.activation(pp[:, j % 2], ps[:, 2 * (j % 2):2 * (j % 2) + 2].rearrange("p b k -> p (b k)"), ACT.Exp,
                         bias=soft[:, j % 4:j % 4 + 1], accum_out=soft[:, 4 + j % 4:5 + j % 4]).then_inc(s_exp, 1)

        def dve_norm_p(e, i, j):
            e.wait_ge(s_exp, i * NJ + (j + 1))
            e.reciprocal(soft[:, 8 + j % 4:9 + j % 4], soft[:, 4 + j % 4:5 + j % 4]).then_inc(s_rec, 1)
            e.wait_ge(s_rec, i * NJ + (j + 1))
            e.tensor_scalar(pp[:, j % 2], pp[:, j % 2], soft[:, 8 + j % 4:9 + j % 4], None, ALU.mult).then_inc(s_norm, 1)

        def p_place(a, b, j):
            q = j % THALF
            return PT[a][:, b * THALF:(b + 1) * THALF, q * P:(q + 1) * P]

        def act_p_hi(e, i, j, b):
            e.wait_ge(p_turned, i * (2 * NJ) + (2 * j + b + 1))
            e.activation(p_place(HI, b, j), ps[:, 4 + b].rearrange("p (k q) -> p k q", q=P), ACT.Copy).then_inc(p_hi, 1)

        def dve_p_lo(e, i, j, b):
            e.wait_ge(p_hi, i * (2 * NJ) + (2 * j + b + 1))
            e.tensor_tensor(p_place(LO, b, j), ps[:, 4 + b].rearrange("p (k q) -> p k q", q=P),
                            p_place(HI, b, j).bitcast(F32), ALU.subtract).then_inc(p_lo, 1)

        def act_pv_low(e, i, j):
            m = i * 4 + (j // THALF - 1)
            e.wait_ge(pv_mm, m + 1)
            e.activation(grow[0:VH, 0:HALF], ps[VH:2 * VH, 6], ACT.Copy).then_inc(pv_low, 1)

        def dve_pv_out(e, i, j):
            m = i * 4 + (j // THALF - 1)
            hp, h = divmod((j // THALF - 1) % 4, 2)
            chunk = i if j > 0 else i - 1
            e.wait_ge(pv_low, m + 1)
            dst = att[hp * VH:(hp + 1) * VH, bass.ds(chunk, 1), h * HALF:(h + 1) * HALF].rearrange("p a q -> p (a q)")
            e.tensor_tensor(dst, ps[0:VH, 6], grow[0:VH, 0:HALF], ALU.add).then_inc(pv_out, 1)

        def act_prod(e, i, j, first):
            c, k = 2 + j % 2, 1 + j // 2
            if not (first and j < 2):
                e.wait_ge(conv_add, i * NJ + (j - 1))
            e.activation(prod[:, j % 2], ac[:, c, bass.ds(i * NT + k, S)], ACT.Copy,
                         scale=cw[:, c, bass.ds(i * NT + k, 1)]).then_inc(prod_ok, 1)

        def pool_conv(e, i, j, first):
            c = 2 + j % 2
            e.wait_ge(prod_ok, i * NJ + (j + 1))
            if not (first and j < 2):
                e.wait_ge(conv_add, i * NJ + (j - 1))
            e.tensor_tensor(cv[:, c], cv[:, c], prod[:, j % 2], ALU.add).then_inc(conv_add, 1)

        def dve_conv(e, a, b):
            with e.Fori(a, b) as i:
                for c in range(2):
                    e.wait_ge(conv, i * 2 + (c - 1))
                    e.scalar_tensor_tensor(out=cv[:, c], in0=ac[:, c, bass.ds(i, S)], scalar=cw[:, c, bass.ds(i, 1)],
                                           in1=cv[:, c], op0=ALU.mult, op1=ALU.add).then_inc(conv, 1)

        def dve_tap0(e, c, count):
            e.tensor_scalar(cv[:, c], ac[:, c, 0:S], cw[:, c, 0:1], vect[:, V_CB + c:V_CB + c + 1], ALU.mult, ALU.add)\
                .then_inc(count, 1)

        HEAD_UNIT_AT = {1: 0, 2: 1, 3: 2, 4: 3}

        def run_steps(e, step):
            for j in range(NJ):
                step(0, j, True, False)
            with e.Fori(1, TURNS - 1) as i:
                for j in range(NJ):
                    step(i, j, False, False)
            for j in range(NJ):
                step(TURNS - 1, j, False, True)

        def mix_src(part, t):
            return (cv, att)[part][:, :, t * P:(t + 1) * P]

        MB = 3

        block = ctx.enter_context(nc.Block())

        @block.sync
        def _(e):
            e.wait_ge(consts, 1)
            rows = ((A["b_ada"], V_BADA, N_MOD * KC), (A["c"], V_C, KC), (A["conv_b"], V_CB, CC), (A["g_conv_ln"], V_LG, CC),
                    (A["b_conv_ln"], V_LB, CC), (A["g_q_lat"], V_GQ, QL // P), (A["g_kv_lat"], V_GKV, KVL // P))
            for a, to, n in rows:
                e.dma_start(vec[to:to + n, :], a.rearrange("a (r q) -> (a r) q", q=P)).then_inc(vec_in, 16)
            for m, g in enumerate(("g_q_head", "g_k_head")):
                e.dma_start(gains[0:NOPE, m:m + 1], A[g][:, 0:NOPE].rearrange("a d -> d a")).then_inc(vec_in, 16)
            for t in range(NT):
                e.dma_start(H[:, t], x_d[:, t]).then_inc(x_in[t], 16)
            for v in range(2):
                for k in range(KC // 2):
                    two = slice(2 * k, 2 * k + 2)
                    e.dma_start(ada01[:, v, two], ada_d[:, two, v * D:(v + 1) * D]).then_inc(ada01_in[v][k], 16)
            e.wait_ge(vec_ok, 1)
            sp_load_gu(e, fs[0], ffn_w[0], 0)
            for kc in range(KC):
                sp_ada_piece(e, G1, kc)
            sp_load_d(e, fs[0], ffn_w[0], 0)
            sp_load_gu(e, fs[0], ffn_w[0], 1)
            for kc in range(KC):
                sp_ada_piece(e, SHM, kc)
            sp_ffn(e, fs[0], ffn_w[0], True)

            e.wait_ge(fs[0].gu_lo, 2 * CPG * GROUPS)
            sp_load_gu(e, U, glu_w, 0)
            e.wait_ge(mod_ok, N_MOD)
            e.dma_start(lata[:], win_d[:, :, 2 * CH:2 * CH + NZ]).then_inc(lat_in[0], 16)
            e.dma_start(cwr[0:CONV_K, :], A["conv_w"][0].rearrange("k a c -> k (a c)")).then_inc(small_in, 16)
            e.dma_start(posr[:], A["positions"].rearrange("a (t q) -> (a t) q", q=P)).then_inc(small_in, 16)
            e.wait_ge(fs[0].d_lo, CPG * GROUPS)
            e.dma_start(latb[:], win_d[:, :, 2 * CH + NZ:2 * CH + W_IN_L]).then_inc(lat_in[1], 16)
            for t in range(NT):
                e.wait_ge(ns[1].scaled, t + 1)
                e.dma_start(h_dram[:, t], H[:, t]).then_inc(h_saved, 16)
            sp_load_gu(e, U, glu_w, 1)
            e.wait_ge(h_saved, 16 * NT)
            for m, g in enumerate(("g_q_head", "g_k_head")):
                e.dma_start(grot[:, m], A[g][:, NOPE:QK].broadcast_to([P, ROPE])).then_inc(grot_in, 16)
            e.wait_ge(U.gu_lo, 2 * 2 * CPG)
            e.dma_start(wqr[:, :, 0:NHD * QK], A["w_q_up"][0].rearrange("(k p) n -> p k n", p=P)).then_inc(up_in[0], 16)
            e.dma_start(wkr, A["w_kv_up"][0]).then_inc(up_in[1], 16)
            e.wait_ge(qk_turned, 4 * NHD)
            for c in range(KC):
                if c >= 2:
                    e.wait_ge(wo_lo, c - 1)
                e.dma_start(wor[:, c % 2], A["w_out"][0][c * P:(c + 1) * P, :]).then_inc(wo_in[c % 2], 16)
            e.wait_ge(ln_step, LN_VAR)
            for n in range(2):
                half = slice(n * THALF, (n + 1) * THALF)
                e.dma_start(H[:, half], h_dram[:, half]).then_inc(h_back[n], 16)
            e.wait_ge(wo_lo, KC)
            e.wait_ge(mix_lo, 2 * NT)
            f = fs[1]
            sp_load_gu(e, f, ffn_w[1], 0)
            sp_load_d(e, f, ffn_w[1], 0)
            sp_load_gu(e, f, ffn_w[1], 1)
            sp_ffn(e, f, ffn_w[1], False)
            e.wait_ge(f.d_scaled, CPG * GROUPS)
            e.dma_start(grow[:], A["g_final"].broadcast_to([P, D])).then_inc(gfin_in, 16)
            for t in range(NT):
                e.wait_ge(o_ok, t + 1)
                e.dma_start(out_d[:, t], H[:, t]).then_inc(final_out, 16)
            e.wait_ge(final_out, 16 * NT)

        @block.gpsimd
        def _(e):
            e.memset(gains[:], 1.0)
            e.memset(vec[:], 0.0).then_inc(consts, 1)
            e.memset(ident[:], 0.0).then_inc(consts, 1)
            e.wait_ge(consts, 2)
            e.affine_select(out=ident[:], in_=ident[:], compare_op=ALU.not_equal, fill=1.0, base=0,
                            pattern=[[-1, P]], channel_multiplier=1).then_inc(consts, 1)
            e.memset(ones[:], 1.0).then_inc(consts, 1)
            e.memset(mhalf[:], -0.5).then_inc(consts, 1)
            e.wait_ge(consts, 5)
            pool_rstd(e, ns[0].base)
            pool_rstd(e, ns[1].base)
            e.wait_ge(ns[1].scaled, NT)
            for j in range(ROPE // 2):
                e.memset(trig[:, 2, 0, j:ROPE:ROPE // 2], INV_FREQ[j])
            e.wait_ge(h_saved, 16 * NT)
            e.memset(ac[:, :, 0:CONV_PAD], 0.0)
            e.memset(ac[:, :, CONV_PAD + S:ACW], 0.0)
            e.memset(cw[:, :, CONV_K:CONV_K + 2], 0.0).then_inc(pads, 1)
            e.wait_ge(z_sq, 2 * NT)
            e.tensor_scalar(zstat[:, 2 * NT:3 * NT], zstat[:, 0:NT], 1.0 / QL, EPS, ALU.mult, ALU.add)
            e.tensor_scalar(zstat[:, 3 * NT:4 * NT], zstat[:, NT:2 * NT], 1.0 / KVL, EPS, ALU.mult, ALU.add)\
                .then_inc(z_rstd, 1)
            e.wait_ge(z_rstd, 1)
            e.tensor_tensor(zstat[:, 4 * NT:6 * NT], zstat[:, 2 * NT:4 * NT], mhalf[:], ALU.pow).then_inc(z_rstd, 1)
            e.wait_ge(qk_sum, 1)
            e.tensor_scalar(qs[:], qs[:], 1.0 / QK, EPS, ALU.mult, ALU.add).then_inc(qk_rstd, 1)
            e.wait_ge(qk_rstd, 1)
            e.tensor_tensor(rqk[:], qs[:], qh[:], ALU.pow).then_inc(qk_rstd, 1)
            e.wait_ge(qk_rstd, 2)
            e.wait_ge(rope, 2)
            pool_slots(e, 0, 0, True)
            e.wait_ge(tap0, 2)

            def step(i, j, first, last):
                pool_conv(e, i, j, first)
                hp, t = divmod(j, NT)
                if t == 0 and not (last and hp == 1):
                    pool_slots(e, *((i, 1) if hp == 0 else (i + 1, 0)))

            run_steps(e, step)
            e.wait_ge(ln_step, LN_VAR)
            e.tensor_tensor(stat[:, NT:2 * NT], stat[:, 0:NT], mhalf[:, 0:NT], ALU.pow).then_inc(ln_pool, 1)
            pool_rstd(e, ns[2].base)
            pool_rstd(e, FINAL)

        @block.scalar
        def _(e):
            e.wait_ge(vec_ok, 2)
            e.activation(silu_c[:], vect[:, V_C:V_C + KC], ACT.Silu).then_inc(silu_ok, 1)
            act_norm_tiles(e, ns[0], range(NT), lambda e, t: e.wait_ge(x_in[t], 16))
            for c in range(CPG):
                act_hi_gu(e, fs[0], 0, c, None)
            e.wait_ge(mod_ok, 2)
            for h in range(NH):
                act_modulate(e, ns[0], SH1, S1, h)
            act_ffn(e, fs[0], ns[0])

            f, n = fs[0], ns[1]

            def done(e, t):
                e.wait_ge(f.added, (GROUPS - 1) * 2 * NT + 2 * t + 2)

            e.wait_ge(f.gu_mm, 4 * GROUPS)
            for c in range(CPG):
                act_hi_gu(e, U, 0, c, None)

            def safe(e, t):
                done(e, t)
                if t == 0:
                    e.wait_ge(f.down_mm, 2 * NT * GROUPS)

            act_norm_tiles(e, n, range(THALF), safe)
            e.wait_ge(mod_ok, N_MOD + 2)
            act_modulate(e, n, SHM, SMX, 0)
            act_norm_tiles(e, n, range(THALF, NT), done)
            act_modulate(e, n, SHM, SMX, 1)
            for b in range(2):
                e.wait_ge(lat_in[b], 16)
                e.activation(wl[:, HI, :, b * NZ:(b + 1) * NZ], (lata, latb)[b][:], ACT.Copy).then_inc(wl_hi, 1)
            e.wait_ge(h_saved, 16 * NT)
            e.wait_ge(trig_ok, 1)
            e.activation(cs[:], trig[:, 3], ACT.Sin).then_inc(cs_ok, 1)

            def sigmoid(s):
                e.wait_ge(U.gu_mm, s + 1)
                if s >= 2:
                    e.wait_ge(U.mul, s - 1)
                else:
                    e.wait_ge(n.x_lo, NH * KC)
                e.activation(tmp[:, s % 2], ps[:, 2 * (s % 2)], ACT.Sigmoid).then_inc(U.silu, 1)

            for s in range(3):
                sigmoid(s)
            act_hi_gu(e, U, 1, 0, 3)
            sigmoid(3)
            act_hi_gu(e, U, 1, 1, 4)
            e.wait_ge(U.mul, 4)
            for t in range(NT):
                e.wait_ge(lat_mm, t + 1)
                b = ps[:, 4 + t % 3]
                if t == 0:
                    e.wait_ge(wl_lo, 2)
                    e.wait_ge(cw_ok, 1)
                e.activation(zz[:, t], b[:, 0:QL + KVL], ACT.Copy)
                e.activation(kr[:, t], b[:, QL + KVL:W_IN_L], ACT.Copy)
                if t >= 1:
                    e.wait_ge(z_sq, 2 * t)
                e.activation(tmp[:, 0, 0:QL], b[:, 0:QL], ACT.Square, accum_out=zstat[:, t:t + 1]).then_inc(z_sq, 1)
                e.activation(tmp[:, 1, 0:KVL], b[:, QL:QL + KVL], ACT.Square, accum_out=zstat[:, NT + t:NT + t + 1])\
                    .then_inc(z_sq, 1)
            e.wait_ge(z_sq, 2 * NT)
            sigmoid(4)
            for v in range(6):
                e.wait_ge(z_turned, v + 1)
                c, h = divmod(v, 2)
                e.activation(CZ[HI][:, c, h * HALF:(h + 1) * HALF], ps[:, 4 + v % 3], ACT.Copy).then_inc(z_hi, 1)
            sigmoid(5)
            e.wait_ge(up_scaled, QL // P)
            e.activation(wq[:, HI], wqr[:, :, 0:NHD * QK], ACT.Copy).then_inc(up_hi, 1)
            e.wait_ge(up_scaled, QL // P + 1)
            e.activation(wkv[:, HI], wkr, ACT.Copy).then_inc(up_hi, 1)
            sigmoid(6)
            sigmoid(7)
            e.wait_ge(z_rstd, 2)
            e.wait_ge(U.mul, 8)
            for t in range(NT):
                e.wait_ge(up_mm, t + 1)
                b = 4 * (t % 2)
                e.activation(qn[:, t].rearrange("p (b h) d -> p b (h d)", b=2), ps[:, b:b + 2, 0:NHD // 2 * QK], ACT.Copy,
                             scale=zstat[:, 4 * NT + t:4 * NT + t + 1]).then_inc(up_out, 1)
                kv = ps[:, b + 2:b + 4].rearrange("p b (h d) -> p (b h) d", d=NOPE + VH)
                e.activation(kn[:, t], kv[:, :, 0:NOPE], ACT.Copy, scale=zstat[:, 5 * NT + t:5 * NT + t + 1])
                e.activation(vn[:, t], kv[:, :, NOPE:NOPE + VH], ACT.Copy, scale=zstat[:, 5 * NT + t:5 * NT + t + 1])\
                    .then_inc(up_out, 1)
                e.wait_ge(up_out, 2 * t + 2)
                if t >= 2:
                    e.wait_ge(qk_sum_t, t)
                sl = sq[:, t % 2]
                e.activation(sl[:, 0:NHD * QK], qn[:, t].rearrange("p h d -> p (h d)"), ACT.Square)
                e.activation(sl[:, NHD * QK:NHD * (QK + NOPE)], kn[:, t].rearrange("p h d -> p (h d)"), ACT.Square)\
                    .then_inc(qk_sq, 1)

            for u in range(4):
                act_head_unit(e, 0, 0, u, True)
            act_exp(e, 0, 0)

            def step(i, j, first, last):
                hp, t = divmod(j, NT)
                if j % THALF == 0 and not (first and j == 0):
                    act_pv_low(e, i, j)
                act_p_hi(e, i, j, 0)
                act_p_hi(e, i, j, 1)
                if not (last and j == NJ - 1):
                    act_exp(e, i, j + 1)
                act_prod(e, i, j, first)
                if t in HEAD_UNIT_AT and not (last and hp == 1):
                    act_head_unit(e, *((i, 1) if hp == 0 else (i + 1, 0)), HEAD_UNIT_AT[t])

            run_steps(e, step)
            act_pv_low(e, TURNS, 0)

            e.wait_ge(ln_step, 3 + CC)
            e.wait_ge(ln_mm, 1)
            for c in range(CC):
                e.activation((prod, pp)[c // 2][:, c % 2], cv[:, c], ACT.Square).then_inc(ln_act, 1)
            for c in range(CC):
                e.wait_ge(ln_step, LN_VAR + 2 + c)
                e.activation(cv[:, c], cv[:, c], ACT.Silu, bias=vect[:, V_LB + c:V_LB + c + 1],
                             scale=vect[:, V_LG + c:V_LG + c + 1]).then_inc(ln_act, 1)
            for c in range(KC):
                e.wait_ge(wo_scaled, c + 1)
                e.activation(wo[:, c, HI], wor[:, c % 2], ACT.Copy).then_inc(wo_hi, 1)
            f, n = fs[1], ns[2]
            act_norm_tiles(e, n, range(THALF), lambda e, t: e.wait_ge(mix_added, 2 * t + 2))
            for c in range(CPG):
                act_hi_gu(e, f, 0, c, None)
            act_norm_tiles(e, n, range(THALF, NT), lambda e, t: e.wait_ge(mix_added, 2 * NT))
            act_modulate(e, n, SH2, S2, 0)
            act_modulate(e, n, SH2, S2, 1)
            act_ffn(e, f, n)
            for t in range(NT):
                e.wait_ge(f.added, (GROUPS - 1) * 2 * NT + 2 * t + 2)
                if t >= 2:
                    e.wait_ge(sumsq, FINAL + t - 1)
                e.activation(ada_raw[:, t % 2], H[:, t], ACT.Square, accum_out=stat[:, t:t + 1]).then_inc(sumsq, 1)

        @block.vector
        def _(e):
            e.wait_ge(vec_tr, 1)
            e.tensor_copy(vect[:], ps[:, MISC, 0:NV]).then_inc(vec_ok, 2)
            e.wait_ge(vec_ok, 2)
            e.tensor_scalar(half_b[:], vect[:, 0:N_MOD * KC], 0.5, None, ALU.mult).then_inc(vec_ok, 1)
            e.wait_ge(vec_in, 16 * 9)
            e.tensor_scalar(gains[0:QK, 0:1], gains[0:QK, 0:1], float(QK) ** -0.5, None, ALU.mult).then_inc(vec_ok, 1)
            e.wait_ge(silu_ok, 1)
            for v in range(2):
                for kc in range(KC):
                    e.wait_ge(ada01_in[v][kc // 2], 16)
                    dve_ada_piece(e, v, kc, ada01[:, v, kc])
                dve_ada_column(e, v, KIND.get(v))
            f = fs[0]
            for c in range(CPG):
                for m in range(2):
                    dve_lo_gu(e, f, 0, c, m)
            for h in range(NH):
                dve_cut_x(e, ns[0], h)
            e.wait_ge(vec_ok, 3)
            for kc in range(KC):
                dve_ada_piece(e, G1, kc)

            def before_row():
                dve_ada_column(e, G1, "half")
                e.wait_ge(mod_ok, G1 + 1)
                dve_row_diag(e, 0, G1)

            dve_first(e, f, 0, before_row, lambda: dve_row_copy(e, 0))
            for kc in range(KC):
                dve_ada_piece(e, SHM, kc)
            dve_ada_column(e, SHM, None)
            e.wait_ge(row_ok, 2)
            dve_turns(e, f, True)
            e.wait_ge(mod_ok, N_MOD)
            for v, op, by in ((SMX, ALU.add, 1.0), (S2, ALU.add, 1.0), (G2, ALU.mult, 0.5)):
                e.tensor_scalar(modc[:, v * KC:(v + 1) * KC], modc[:, v * KC:(v + 1) * KC], by, None, op)\
                    .then_inc(mod_ok, 1)

            for c in range(CPG):
                for m in range(2):
                    dve_lo_gu(e, U, 0, c, m)
            dve_add(e, f, GROUPS - 1, range(2 * NT))
            for h in range(NH):
                dve_cut_x(e, ns[1], h)

            k = [0]

            def link(ins):
                k[0] += 1
                ins.then_inc(dve_step, 1)
                e.wait_ge(dve_step, k[0])

            def glu(s):
                g, (c, h) = s // 4, (FIRST_STEPS if s < 4 else STEPS)[s % 4]
                e.wait_ge(U.silu, s + 1)
                if s == 0:
                    e.wait_ge(h_saved, 16 * NT)
                e.tensor_tensor(ac[:, 2 * g + c, CONV_PAD + h * HALF:CONV_PAD + (h + 1) * HALF],
                                ps[:, 2 * (s % 2) + 1], tmp[:, s % 2], ALU.mult).then_inc(U.mul, 1)

            e.wait_ge(small_in, 32)
            e.tensor_copy(posf[:], posr[:]).then_inc(pos_ok, 1)
            for b in range(2):
                e.wait_ge(wl_hi, b + 1)
                part = slice(b * NZ, (b + 1) * NZ)
                e.tensor_tensor(wl[:, LO, :, part], (lata, latb)[b][:], wl[:, HI, :, part].bitcast(F32), ALU.subtract)\
                    .then_inc(wl_lo, 1)
            e.wait_ge(pos_ok, 2)
            link(e.tensor_copy(posc[:], ps[:, MISC, 0:NT]))
            e.wait_ge(h_saved, 16 * NT)
            e.tensor_copy(cw[:, :, 0:CONV_K], ps[:, MISC, 64:64 + 32 * CC].rearrange("p (c k) -> p c k", k=32)[:, :, 0:CONV_K])\
                .then_inc(cw_ok, 1)
            RH = ROPE // 2
            e.wait_ge(pads, 1)
            link(e.tensor_tensor(trig[:, 0], posc[:].unsqueeze(2).broadcast_to([P, NT, ROPE]),
                                 trig[:, 2, 0:1].broadcast_to([P, NT, ROPE]), ALU.mult))
            for h in range(2):
                part = slice(h * RH, (h + 1) * RH)
                e.tensor_scalar(trig[:, 1, :, part], trig[:, 0, :, part], 1.0 / (2 * np.pi), (0.25, 0.0)[h], ALU.mult, ALU.add)\
                    .then_inc(dve_step, 1)
                k[0] += 1
            e.wait_ge(dve_step, k[0])
            link(e.tensor_scalar(trig[:, 1], trig[:, 1], ROUND, ROUND, ALU.add, ALU.subtract))
            for part in TWO_PI:
                link(e.scalar_tensor_tensor(out=trig[:, 0], in0=trig[:, 1], scalar=-part, in1=trig[:, 0], op0=ALU.mult,
                                            op1=ALU.add))
            link(e.tensor_scalar(trig[:, 0, :, 0:RH], trig[:, 0, :, 0:RH], float(np.pi / 2), None, ALU.add))
            e.tensor_scalar(trig[:, 3], trig[:, 0], PI_IN, -PI_IN, ALU.min, ALU.max).then_inc(trig_ok, 1)
            for s in range(3):
                glu(s)
            dve_lo_gu(e, U, 1, 0, 0)
            dve_lo_gu(e, U, 1, 0, 1)
            glu(3)
            dve_lo_gu(e, U, 1, 1, 0)
            dve_lo_gu(e, U, 1, 1, 1)
            e.wait_ge(cw_ok, 1)
            e.wait_ge(U.mul, 4)
            e.wait_ge(cs_ok, 1)
            dve_tap0(e, 0, conv)
            dve_tap0(e, 1, conv)
            dve_conv(e, 1, 14)
            glu(4)
            for v in range(6):
                e.wait_ge(z_hi, v + 1)
                c, h = divmod(v, 2)
                tok = slice(h * HALF, (h + 1) * HALF)
                e.tensor_tensor(CZ[LO][:, c, tok], ps[:, 4 + v % 3], CZ[HI][:, c, tok].bitcast(F32), ALU.subtract)\
                    .then_inc(z_lo, 1)
            e.wait_ge(up_in[0], 16)
            for c in range(QL // P):
                w = wqr[:, c, 0:NHD * QK]
                e.tensor_scalar(w, w, vect[:, V_GQ + c:V_GQ + c + 1], None, ALU.mult).then_inc(up_scaled, 1)
            e.wait_ge(up_in[1], 16)
            e.tensor_scalar(wkr, wkr, vect[:, V_GKV:V_GKV + 1], None, ALU.mult).then_inc(up_scaled, 1)
            glu(5)
            e.wait_ge(up_hi, 1)
            e.tensor_tensor(wq[:, LO], wqr[:, :, 0:NHD * QK], wq[:, HI].bitcast(F32), ALU.subtract).then_inc(up_lo, 1)
            e.wait_ge(up_hi, 2)
            e.tensor_tensor(wkv[:, LO], wkr, wkv[:, HI].bitcast(F32), ALU.subtract).then_inc(up_lo, 1)
            dve_conv(e, 14, 18)
            glu(6)
            dve_conv(e, 18, 22)
            glu(7)
            e.wait_ge(U.mul, 8)
            dve_tap0(e, 2, tap0)
            dve_tap0(e, 3, tap0)
            krs = rt[:, 3, :, 0, 0:1].rearrange("p t a -> p (t a)")
            flat = rt[:, 0:2].rearrange("p a t h d -> p (a t h d)")
            k2 = flat[:, 0:NT * ROPE].rearrange("p (t d) -> p t d", t=NT)
            link(e.tensor_tensor(k2, kr[:], kr[:], ALU.mult))
            e.tensor_reduce(krs, k2, AX_X, ALU.add)
            e.wait_ge(grot_in, 32)
            link(e.tensor_tensor(kr[:], kr[:], grot[:, 1:2].broadcast_to([P, NT, ROPE]), ALU.mult))
            cos, sin = cs[:, :, 0:RH], cs[:, :, RH:ROPE]
            part = [rt[:, 2, n].rearrange("p h d -> p (h d)")[:, 0:NT * RH].rearrange("p (t d) -> p t d", t=NT) for n in range(4)]
            x1, x2 = kr[:, :, 0:RH], kr[:, :, RH:ROPE]
            for to, a, b in ((part[0], x1, cos), (part[1], x2, sin), (part[2], x2, cos), (part[3], x1, sin)):
                link(e.tensor_tensor(to, a, b, ALU.mult))
            link(e.tensor_tensor(x1, part[0], part[1], ALU.subtract))
            e.tensor_tensor(x2, part[2], part[3], ALU.add).then_inc(rope, 1)
            e.memset(qh[:], -0.5).then_inc(qk_sum_t, 1)
            for t in range(NT):
                e.wait_ge(qk_sq, t + 1)
                sl = sq[:, t % 2]
                e.tensor_reduce(qs[:, t, 0:NHD], sl[:, 0:NHD * QK].rearrange("p (h d) -> p h d", d=QK), AX_X, ALU.add)
                e.tensor_reduce(qs[:, t, NHD:2 * NHD], sl[:, NHD * QK:NHD * (QK + NOPE)].rearrange("p (h d) -> p h d", d=NOPE),
                                AX_X, ALU.add).then_inc(qk_sum_t, 1)
            e.wait_ge(qk_sum_t, NT + 1)
            e.tensor_tensor(qs[:, :, NHD:2 * NHD], qs[:, :, NHD:2 * NHD],
                            krs.unsqueeze(2).broadcast_to([P, NT, NHD]), ALU.add).then_inc(qk_sum, 1)
            rot = qn[:, :, :, NOPE:QK]
            link(e.tensor_tensor(rot.rearrange("p t h d -> p (t h) d"), rot.rearrange("p t h d -> p (t h) d"),
                                 grot[:, 0:1].broadcast_to([P, NT * NHD, ROPE]), ALU.mult))
            x1, x2 = qn[:, :, :, NOPE:NOPE + RH], qn[:, :, :, NOPE + RH:QK]
            cosb = cos.unsqueeze(2).broadcast_to([P, NT, NHD, RH])
            sinb = sin.unsqueeze(2).broadcast_to([P, NT, NHD, RH])
            e.wait_ge(qk_sum, 1)
            for m, (a, b) in enumerate(((x1, cosb), (x2, sinb), (x2, cosb), (x1, sinb))):
                link(e.tensor_tensor(rt[:, m], a, b, ALU.mult))
            link(e.tensor_tensor(x1, rt[:, 0], rt[:, 1], ALU.subtract))
            e.tensor_tensor(x2, rt[:, 2], rt[:, 3], ALU.add).then_inc(rope, 1)
            dve_v(e, 0, 0, True)
            e.wait_ge(rope, 2)

            for u in range(4):
                dve_head_unit(e, 0, 0, u)
            dve_max(e, 0, 0)

            def step(i, j, first, last):
                hp, t = divmod(j, NT)
                dve_norm_p(e, i, j)
                if not (last and j == NJ - 1):
                    dve_max(e, i, j + 1)
                if j % THALF == 0 and not (first and j == 0):
                    dve_pv_out(e, i, j)
                dve_p_lo(e, i, j, 0)
                dve_p_lo(e, i, j, 1)
                if t - 1 in HEAD_UNIT_AT and not (last and hp == 1):
                    dve_head_unit(e, *((i, 1) if hp == 0 else (i + 1, 0)), HEAD_UNIT_AT[t - 1])
                if t == NT - 2 and not (last and hp == 1):
                    dve_v(e, *((i, 1) if hp == 0 else (i + 1, 0)), first=first and hp == 0)

            run_steps(e, step)
            dve_pv_out(e, TURNS, 0)
            e.wait_ge(pv_out, 2 * NHD)
            dve_conv(e, 22, CONV_K)

            e.wait_ge(conv, 2 * CONV_K)
            e.wait_ge(conv_add, NHD * NT)
            e.tensor_tensor(pp[:, 0], cv[:, 0], cv[:, 1], ALU.add).then_inc(ln_step, 1)
            e.tensor_tensor(pp[:, 1], cv[:, 2], cv[:, 3], ALU.add).then_inc(ln_step, 1)
            e.wait_ge(ln_step, 2)
            e.tensor_tensor(pp[:, 0], pp[:, 0], pp[:, 1], ALU.add).then_inc(ln_step, 1)
            e.wait_ge(ln_mm, 1)
            mean = ps[:, 0:2].rearrange("p b n -> p (b n)")
            for c in range(CC):
                e.scalar_tensor_tensor(out=cv[:, c], in0=mean, scalar=-1.0 / CH, in1=cv[:, c], op0=ALU.mult, op1=ALU.add)\
                    .then_inc(ln_step, 1)
            e.wait_ge(ln_act, 4)
            e.tensor_tensor(pp[:, 0], pp[:, 0], pp[:, 1], ALU.add).then_inc(ln_step, 1)
            e.wait_ge(ln_step, 8)
            e.tensor_tensor(pp[:, 0], pp[:, 0], prod[:, 0], ALU.add).then_inc(ln_step, 1)
            e.wait_ge(ln_step, 9)
            e.tensor_tensor(pp[:, 0], pp[:, 0], prod[:, 1], ALU.add).then_inc(ln_step, 1)
            e.wait_ge(ln_mm, 2)
            e.tensor_scalar(stat[:, 0:NT], ps[:, MISC, 0:NT], 1.0 / CH, 1e-5, ALU.mult, ALU.add).then_inc(ln_step, 1)
            e.wait_ge(ln_pool, 1)
            diag = pp[:, 1].rearrange("p (k j) -> p k j", k=NT)
            e.tensor_tensor(diag, ident[:].unsqueeze(1).broadcast_to([P, NT, P]),
                            stat[:, NT:2 * NT].unsqueeze(2).broadcast_to([P, NT, P]), ALU.mult).then_inc(ln_step, 1)
            e.wait_ge(ln_mm, 3)
            rstd = ps[:, 2:4].rearrange("p b n -> p (b n)")
            for c in range(CC):
                e.tensor_tensor(cv[:, c], cv[:, c], rstd, ALU.mult).then_inc(ln_step, 1)
            dve_row_diag(e, 1, GM)
            dve_row_copy(e, 1)
            e.wait_ge(row_ok, 4)
            for c in range(KC):
                e.wait_ge(wo_in[c % 2], 16 * (c // 2 + 1))
                e.tensor_tensor(wor[:, c % 2], wor[:, c % 2], grow[:], ALU.mult).then_inc(wo_scaled, 1)
                e.wait_ge(wo_hi, c + 1)
                e.tensor_tensor(wo[:, c, LO], wor[:, c % 2], wo[:, c, HI].bitcast(F32), ALU.subtract).then_inc(wo_lo, 1)
            e.wait_ge(ln_act, 8)

            def cut_mix(t):
                for part in range(2):
                    if t >= 2:
                        e.wait_ge(mix_mm, 2 * t - 2)
                    dst = mixT[:, t % 2, HI, part * CC:(part + 1) * CC]
                    e.tensor_copy(dst, mix_src(part, t)).then_inc(mix_hi, 1)
                for part in range(2):
                    e.wait_ge(mix_hi, 2 * t + part + 1)
                    dst = mixT[:, t % 2, LO, part * CC:(part + 1) * CC]
                    e.tensor_tensor(dst, mix_src(part, t), mixT[:, t % 2, HI, part * CC:(part + 1) * CC].bitcast(F32),
                                    ALU.subtract).then_inc(mix_lo, 1)

            cut_mix(0)
            for t in range(NT):
                if t + 1 < NT:
                    cut_mix(t + 1)
                for h in range(2):
                    e.wait_ge(mix_mm, 2 * t + h + 1)
                    e.wait_ge(h_back[t // THALF], 16)
                    dst = H[:, t, h * HALF:(h + 1) * HALF]
                    e.tensor_tensor(dst, ps[:, 4 + (2 * t + h) % MB], dst, ALU.add).then_inc(mix_added, 1)

            f, n = fs[1], ns[2]
            for c in range(CPG):
                for m in range(2):
                    dve_lo_gu(e, f, 0, c, m)
            for h in range(NH):
                dve_cut_x(e, n, h)
            dve_first(e, f, 2, lambda: dve_row_diag(e, 2, G2), lambda: dve_row_copy(e, 2))
            e.wait_ge(row_ok, 6)
            dve_turns(e, f, False)
            dve_add(e, f, GROUPS - 1, range(2 * NT))
            e.wait_ge(gfin_in, 16)
            for t in range(NT):
                e.wait_ge(rms_inv, FINAL + t + 1)
                e.scalar_tensor_tensor(out=H[:, t], in0=H[:, t], scalar=stat[:, 2 * NT + t:2 * NT + t + 1], in1=grow[:],
                                       op0=ALU.mult, op1=ALU.mult).then_inc(o_ok, 1)

        @block.tensor
        def _(e):
            e.wait_ge(consts, 5)
            e.wait_ge(vec_in, 16 * 9)
            e.transpose(ps[:, MISC, 0:NV], vec[0:NV], ident[0:NV, 0:NV]).then_inc(vec_tr, 1)
            e.wait_ge(vec_ok, 2)
            for v in range(2):
                pe_ada_sum(e, v)
            e.wait_ge(mod_ok, 2)
            for h in range(NH):
                pe_turn(e, ns[0], h)
            f = fs[0]
            pe_gateup(e, f, ns[0], 0, first=True, after={
                1: lambda: pe_ada_sum(e, G1),
                2: lambda: pe_row(e, 0)})
            e.wait_ge(row_ok, 2)
            pe_ada_sum(e, SHM)
            pe_turns(e, f, ns[0], True)
            pe_down(e, f, GROUPS - 1, 0, range(2 * NT))

            n = ns[1]
            pe_turn(e, n, 0)
            pe_turn(e, n, 1)

            def small_turns():
                e.wait_ge(n.modulated, 2 * KC)
                e.wait_ge(small_in, 32)
                e.wait_ge(pos_ok, 1)
                for c in range(CC):
                    e.transpose(ps[:, MISC, 64 + 32 * c:64 + 32 * c + CONV_K], cwr[0:CONV_K, c * P:(c + 1) * P],
                                ident[0:CONV_K, 0:CONV_K])
                e.transpose(ps[:, MISC, 0:NT], posf[:], ident[0:NT, 0:NT]).then_inc(pos_ok, 1)

            small_turns()
            pe_gateup(e, U, n, 0, first=True)
            e.wait_ge(wl_lo, 2)
            for t in range(NT):
                if t >= 3:
                    e.wait_ge(z_sq, 2 * (t - 2))
                k = 0
                for kc in range(KC):
                    for wx, xx in PASSES:
                        mm = e.matmul(ps[:, 4 + t % 3, 0:W_IN_L], X[xx][:, kc, t * P:(t + 1) * P], wl[:, wx, kc],
                                      start=(k == 0), stop=(k == 3 * KC - 1))
                        k += 1
                mm.then_inc(lat_mm, 1)

            def turn_latents():
                e.wait_ge(z_sq, 2 * NT)
                for v in range(6):
                    c, h = divmod(v, 2)
                    if v >= 3:
                        e.wait_ge(z_lo, v - 2)
                    for k in range(THALF):
                        mm = e.transpose(ps[:, 4 + v % 3, k * P:(k + 1) * P], zz[:, h * THALF + k, c * P:(c + 1) * P],
                                         ident[:])
                    mm.then_inc(z_turned, 1)

            pe_gateup(e, U, n, 1, after={0: turn_latents})
            e.wait_ge(z_lo, 6)
            e.wait_ge(up_lo, 2)
            e.wait_ge(U.mul, 8)
            for t in range(NT):
                b = 4 * (t % 2)
                if t >= 2:
                    e.wait_ge(up_out, 2 * t - 2)
                tok = slice(t * P, (t + 1) * P)
                for h in range(2):
                    k = 0
                    for c in range(QL // P):
                        for wx, xx in PASSES:
                            e.matmul(ps[:, b + h, 0:NHD // 2 * QK], CZ[xx][:, c, tok],
                                     wq[:, wx, c, h * (NHD // 2 * QK):(h + 1) * (NHD // 2 * QK)], start=(k == 0),
                                     stop=(k == 3 * (QL // P) - 1))
                            k += 1
                for h in range(2):
                    for k, (wx, xx) in enumerate(PASSES):
                        mm = e.matmul(ps[:, b + 2 + h], CZ[xx][:, QL // P, tok], wkv[:, wx, h * HALF:(h + 1) * HALF],
                                      start=(k == 0), stop=(k == 2))
                mm.then_inc(up_mm, 1)

            e.wait_ge(up_out, 2 * NT)
            for u in range(4):
                pe_turn_head(e, 0, 0, u, True)
            pe_scores(e, 0, 0)
            pe_scores(e, 0, 1)

            def step(i, j, first, last):
                hp, t = divmod(j, NT)
                if not (last and j >= NJ - 2):
                    pe_scores(e, i, j + 2)
                if j % THALF == 0 and not (first and j == 0):
                    pe_pv(e, i, j)
                pe_turn_p(e, i, j, first)
                if t in HEAD_UNIT_AT and not (last and hp == 1):
                    pe_turn_head(e, *((i, 1) if hp == 0 else (i + 1, 0)), HEAD_UNIT_AT[t])

            run_steps(e, step)
            pe_pv(e, TURNS, 0)
            e.wait_ge(ln_step, 3)
            for h in range(2):
                mm = e.matmul(ps[:, h], ones[:], pp[:, 0, h * HALF:(h + 1) * HALF], start=True, stop=True)
            mm.then_inc(ln_mm, 1)
            e.wait_ge(ln_step, 10)
            for t in range(NT):
                mm = e.matmul(ps[:, MISC, t:t + 1], pp[:, 0, t * P:(t + 1) * P], ones[:, 0:1], start=True, stop=True)
            mm.then_inc(ln_mm, 1)
            e.wait_ge(ln_step, LN_VAR + 1)
            for h in range(2):
                mm = e.matmul(ps[:, 2 + h], ones[:], pp[:, 1, h * HALF:(h + 1) * HALF], start=True, stop=True)
            mm.then_inc(ln_mm, 1)
            e.wait_ge(pv_out, 2 * NHD)
            pe_row(e, 1)
            e.wait_ge(row_ok, 4)
            e.wait_ge(wo_lo, KC)
            for t in range(NT):
                e.wait_ge(mix_lo, 2 * t + 2)
                for h in range(2):
                    m = 2 * t + h
                    if m >= MB:
                        e.wait_ge(mix_added, m - MB + 1)
                    k = 0
                    for c in range(KC):
                        for wx, xx in PASSES:
                            mm = e.matmul(ps[:, 4 + m % MB], mixT[:, t % 2, xx, c], wo[:, c, wx, h * HALF:(h + 1) * HALF],
                                          start=(k == 0), stop=(k == 3 * KC - 1))
                            k += 1
                    mm.then_inc(mix_mm, 1)
            f, n = fs[1], ns[2]
            pe_turn(e, n, 0)
            pe_turn(e, n, 1)
            pe_gateup(e, f, n, 0, first=True, after={2: lambda: pe_row(e, 2)})
            pe_turns(e, f, n, False)
            pe_down(e, f, GROUPS - 1, 0, range(2 * NT))


_INS = ["x", "c", "positions", "w_ada", "b_ada", "ffn1_wg", "ffn1_wu", "ffn1_wd", "w_in", "g_q_lat", "g_kv_lat",
        "w_q_up", "w_kv_up", "g_q_head", "g_k_head", "conv_w", "conv_b", "g_conv_ln", "b_conv_ln", "w_out",
        "ffn2_wg", "ffn2_wu", "ffn2_wd", "g_final"]


def kernel(**inputs):
    import concourse.bacc as bacc
    from concourse.bass_utils import run_bass_kernel_spmd as run

    nc = bacc.Bacc("TRN2", target_bir_lowering=False, num_devices=1, dynamic_dma_scratch_size=1024)
    arrays, A = {}, {}
    for name in _INS:
        a = np.ascontiguousarray(inputs[name])
        arrays[f"in_{name}"] = a
        A[name] = nc.dram_tensor(f"in_{name}", a.shape, mybir.dt.from_np(a.dtype), kind="ExternalInput").ap()
    out = nc.dram_tensor("out", inputs["x"].shape, F32, kind="ExternalOutput").ap()
    build(nc, A, out)
    r = run(nc, [arrays], core_ids=[0])
    return r.results[0]["out"]
```

```python
from contextlib import ExitStack

import numpy as np

import concourse.bass as bass
from concourse import mybir
from concourse.alu_op_type import AluOpType as ALU

ACT = mybir.ActivationFunctionType
AX_X = mybir.AxisListType.X
F32 = mybir.dt.float32
F32R = mybir.dt.float32r
I32 = mybir.dt.int32

P = 128
HALF = 512
EPS = 1e-6

HI, LO = 0, 1
PASSES = ((HI, HI), (HI, LO), (LO, HI))


def build(nc, A, out, dump=None, stop=99):
    D = A["x"].shape[2]
    S = A["x"].shape[1]
    FF = A["ffn1_wg"].shape[2]
    KC = D // P
    NT = S // P
    NH = S // HALF
    THALF = NT // NH
    CPG = 2
    GROUPS = FF // (CPG * P)
    GW = CPG * P
    CH = A["conv_b"].shape[1]
    CONV_K = A["conv_w"].shape[1]
    QL, KVL = A["g_q_lat"].shape[1], A["g_kv_lat"].shape[1]
    QK = A["g_q_head"].shape[1]
    NHD = A["w_q_up"].shape[2] // QK
    VH = (D - CH) // NHD
    NOPE = A["w_kv_up"].shape[2] // NHD - VH
    ROPE = QK - NOPE
    W_IN_L = QL + KVL + ROPE
    N_MOD = A["w_ada"].shape[2] // D
    SH1, S1, G1, SHM, SMX, GM, SH2, S2, G2 = range(N_MOD)

    x_d = A["x"][0].rearrange("(t p) d -> p t d", p=P)
    out_d = out[0].rearrange("(t p) d -> p t d", p=P)
    ada_d = A["w_ada"][0].rearrange("(k p) n -> p k n", p=P)
    ffn_w = []
    for n in (1, 2):
        ffn_w.append(tuple(A[f"ffn{n}_{w}"][0].rearrange("(k p) n -> p k n", p=P) for w in ("wg", "wu", "wd")))

    win_d = A["w_in"][0].rearrange("(k p) n -> p k n", p=P)
    glu_w = (win_d[:, :, CH:2 * CH], win_d[:, :, 0:CH])
    CONV_PAD = CONV_K // 2
    INV_FREQ = [float(np.float32(1) / np.float32(np.float32(10000.0) ** np.float32(j / ROPE))) for j in range(0, ROPE, 2)]
    ROUND = 12582912.0
    TWO_PI = (6.28125, 0.0019354820251464844, 2 * np.pi - 6.28125 - 0.0019354820251464844)
    PI_IN = 3.1415925

    with ExitStack() as ctx:
        def sem(name):
            return ctx.enter_context(nc.semaphore(name))

        def region(size, *variants):
            made = []
            for v in variants:
                with ExitStack() as inner:
                    used = 0
                    for name, shape, dt in v:
                        used += int(np.prod(shape[1:])) * 4
                        made.append(inner.enter_context(nc.sbuf_tensor(name, shape, dt)))
                    assert used <= size, (v, used, size)
            ctx.enter_context(nc.sbuf_tensor(f"region_{made[0].name}", [P, size // 4], F32))
            return made

        def sb(name, shape, dt=F32):
            return ctx.enter_context(nc.sbuf_tensor(name, shape, dt))

        KB = 1024
        ident = sb("ident", [P, P])
        ones = sb("ones", [P, P])
        CC = CH // P
        V_BADA, V_C = 0, N_MOD * KC
        V_CB = V_C + KC
        V_LG, V_LB = V_CB + CC, V_CB + 2 * CC
        V_GQ, V_GKV = V_CB + 3 * CC, V_CB + 3 * CC + QL // P
        NV = V_GKV + KVL // P
        vect = sb("vect", [P, NV])
        silu_c = sb("silu_c", [P, KC])
        half_b = sb("half_b", [P, N_MOD * KC])
        modc = sb("modc", [P, N_MOD * KC])
        stat = sb("stat", [P, 4 * NT])
        zstat = sb("zstat", [P, 6 * NT])
        mhalf = sb("mhalf", [P, 2 * NT])
        gains = sb("gains", [P, 2])
        negmax = sb("negmax", [P, 2, THALF])
        NZ = W_IN_L // 2
        ACW = S + CONV_K + 1
        H, ac, wq, kr, cs, cw, grot, rqk, _ac2, prod = region(
            32 * KB, [("H", [P, NT, D], F32)],
            [("ac", [P, CC, ACW], F32), ("wq", [P, 2, QL // P, NHD * QK], F32R), ("kr", [P, NT, ROPE], F32),
             ("cs", [P, NT, ROPE], F32), ("cw", [P, CC, CONV_K + 2], F32), ("grot", [P, 2, ROPE], F32),
             ("rqk", [P, NT, 2 * NHD], F32)],
            [("_ac2", [P, CC, ACW], F32), ("prod", [P, 2, S], F32)])
        xh, xl, ada01, qn, kn, vn, vs, wo = region(
            64 * KB, [("xh", [P, KC, S], F32R), ("xl", [P, KC, S], F32R)],
            [("ada01", [P, 2, KC, D], F32)],
            [("qn", [P, NT, NHD, QK], F32), ("kn", [P, NT, NHD, NOPE], F32), ("vn", [P, NT, NHD, VH], F32),
             ("vs", [P, 2, NT, 2 * VH], F32)],
            [("wo", [P, KC, 2, D], F32R)])
        X = (xh, xl)
        W1, E0, E1, sq, rt, qs, qh = region(
            32 * KB, [("W1", [P, CPG, 2, 2, KC, P], F32R)],
            [("E0", [P, NT, HALF], F32), ("E1", [P, NT, HALF], F32)],
            [("sq", [P, 2, NHD * (QK + NOPE)], F32), ("rt", [P, 4, NT, NHD, ROPE // 2], F32),
             ("qs", [P, NT, 2 * NHD], F32), ("qh", [P, NT, 2 * NHD], F32)])
        EX = (E0, E1)
        AT, XS, wl, czh, czl, qkT, _x4, mixT = region(
            32 * KB, [("AT", [P, 2, CPG, 2, S], F32R)], [("XS", [P, NT, D], F32)],
            [("wl", [P, 2, KC, W_IN_L], F32R)],
            [("czh", [P, 3, S], F32R), ("czl", [P, 3, S], F32R)],
            [("qkT", [P, 2, 2, 2, S], F32R)],
            [("_x4", [P, NT // 2, D], F32), ("mixT", [P, 2, 2, KC, P], F32R)])
        CZ = (czh, czl)
        rawg, rawu, rawd, vec, wqr, _u2, latb, _g3, _u3, wkv, slot, _s2, att, wor = region(
            24 * KB, [("rawg", [P, KC, GW], F32), ("rawu", [P, KC, GW], F32), ("rawd", [P, CPG, D], F32)],
            [("vec", [NV, P], F32)],
            [("wqr", [P, QL // P, 1024], F32), ("_u2", [P, KC, GW], F32), ("latb", [P, KC, NZ], F32)],
            [("_g3", [P, KC, GW], F32), ("_u3", [P, KC, GW], F32), ("wkv", [P, 2, NHD * 2 * NOPE], F32R)],
            [("slot", [P, 2, NT, QK], F32), ("_s2", [P, 512], F32), ("att", [P, CC, S], F32)],
            [("wor", [P, 2, D], F32)])
        wkr = rawu[:].rearrange("p k n -> p (k n)")[:, 0:NHD * 2 * NOPE]
        WD, cv, trig = region(16 * KB, [("WD", [P, CPG, 2, D], F32R)], [("cv", [P, CC, S], F32)],
                              [("trig", [P, 4, NT, ROPE], F32)])
        ada_raw, ada_acc, lata, cwr, posr, posf, posc, zz, pp, gm_row = region(
            12 * KB, [("ada_raw", [P, 2, D], F32), ("ada_acc", [P, D], F32)],
            [("lata", [P, KC, NZ], F32), ("cwr", [P, CH], F32), ("posr", [NT, P], I32), ("posf", [NT, P], F32),
             ("posc", [P, NT], F32)],
            [("zz", [P, NT, QL + KVL], F32)],
            [("pp", [P, 2, S], F32), ("gm_row", [P, D], F32)])
        tmp = sb("tmp", [P, 2, HALF])
        grow = sb("grow", [P, D])
        ps = ctx.enter_context(nc.psum_tensor("ps", [P, 8, HALF], F32))
        MISC = 7

        vec_in = sem("vec_in")
        x_in = [sem(f"x_in{t}") for t in range(NT)]
        ada_in = [sem(f"ada_in{n}") for n in range(2)]
        consts = sem("consts")
        vec_tr = sem("vec_tr")
        vec_ok = sem("vec_ok")
        silu_ok = sem("silu_ok")
        ada01_in = [[sem(f"ada{v}_in{k}") for k in range(KC // 2)] for v in range(2)]
        acc_used = sem("acc_used")
        mod_ok = sem("mod_ok")
        ada_step = sem("ada_step")
        row_src = sem("row_src")
        row_mm = sem("row_mm")
        row_ok = sem("row_ok")
        final_out = sem("final_out")
        h_dram = nc.dram_tensor("h_saved_rows", (P, NT, D), F32).ap()

        class Sems:
            pass

        sumsq, mean_sq, rms_inv = sem("sumsq"), sem("mean_sq"), sem("rms_inv")

        def norm_sems(n, before):
            g = Sems()
            g.base = before * NT
            g.scaled, g.turned, g.modulated, g.x_hi, g.x_lo = (sem(f"{n}_{what}") for what in (
                "scaled", "turned", "modulated", "x_hi", "x_lo"))
            return g

        def gate_up_sems(n):
            g = Sems()
            g.g_in, g.u_in, g.gu_hi, g.gu_lo, g.gu_mm, g.silu, g.mul = (sem(f"{n}_{what}") for what in (
                "g_in", "u_in", "gu_hi", "gu_lo", "gu_mm", "silu", "mul"))
            return g

        def ffn_sems(n):
            g = gate_up_sems(n)
            g.d_in, g.d_scaled, g.d_hi, g.d_lo, g.a_hi, g.a_lo, g.down_mm, g.added = (sem(f"{n}_{what}") for what in (
                "d_in", "d_scaled", "d_hi", "d_lo", "a_hi", "a_lo", "down_mm", "added"))
            return g

        ns = [norm_sems("norm1", 0), norm_sems("norm_mix", 1), norm_sems("norm2", 2)]
        FINAL = 3 * NT
        fs = [ffn_sems("ffn1"), ffn_sems("ffn2")]
        U = gate_up_sems("glu")
        h_saved, h_back = sem("h_saved"), [sem(f"h_back{n}") for n in range(2)]
        small_in, lat_in = sem("small_in"), [sem("lat_in0"), sem("lat_in1")]
        up_in = [sem("wq_in"), sem("wkv_in")]
        pads, pos_ok, trig_ok, cw_ok = sem("pads"), sem("pos_ok"), sem("trig_ok"), sem("cw_ok")
        wl_hi, wl_lo, lat_mm, z_sq, z_rstd = (sem(n) for n in (
            "wl_hi", "wl_lo", "lat_mm", "z_sq", "z_rstd"))
        z_turned, z_hi, z_lo = sem("z_turned"), sem("z_hi"), sem("z_lo")
        up_scaled, up_hi, up_lo, up_mm, up_out = (sem(n) for n in ("up_scaled", "up_hi", "up_lo", "up_mm", "up_out"))
        qk_sq, qk_sum_t, qk_sum, qk_rstd, rope = (sem(n) for n in ("qk_sq", "qk_sum_t", "qk_sum", "qk_rstd", "rope"))
        grot_in, dve_step, cs_ok, tap0 = sem("grot_in"), sem("dve_step"), sem("cs_ok"), sem("tap0")
        conv = sem("conv")
        prod_ok, conv_add = sem("prod_ok"), sem("conv_add")
        slot_q, slot_k, k_ones = sem("slot_q"), sem("slot_k"), sem("k_ones")
        qk_turned, qk_y, qk_hi, qk_lo = sem("qk_turned"), sem("qk_y"), sem("qk_hi"), sem("qk_lo")
        max_mm, s_max, m_row, m_hi, m_lo = (sem(n) for n in ("max_mm", "s_max", "m_row", "m_hi", "m_lo"))
        s_mm, s_exp, pv_mm, pv_rec, pv_out = (sem(n) for n in ("s_mm", "s_exp", "pv_mm", "pv_rec", "pv_out"))
        v_ok, pv_copied = sem("v_ok"), sem("pv_copied")
        ln_mean, ln_mm, ln_act, ln_pool, ln_dve = (sem(n) for n in ("ln_mean", "ln_mm", "ln_act", "ln_pool", "ln_dve"))
        wo_in, wo_scaled, wo_hi, wo_lo = [sem("wo_in0"), sem("wo_in1")], sem("wo_scaled"), sem("wo_hi"), sem("wo_lo")
        mix_hi, mix_lo, mix_mm, mix_added = sem("mix_hi"), sem("mix_lo"), sem("mix_mm"), sem("mix_added")
        gfin_in, o_ok = sem("gfin_in"), sem("o_ok")

        def sp_load_gu(e, f, w, g):
            if isinstance(g, int) and g == 0:
                pass
            else:
                e.wait_ge(f.gu_lo, g * (2 * CPG))
            e.dma_start(rawg[:], w[0][:, :, bass.ds(g * GW, GW)]).then_inc(f.g_in, 16)
            e.dma_start(rawu[:], w[1][:, :, bass.ds(g * GW, GW)]).then_inc(f.u_in, 16)

        def sp_load_d(e, f, w, g):
            if not (isinstance(g, int) and g == 0):
                e.wait_ge(f.d_lo, g * CPG)
            e.dma_start(rawd[:], w[2][:, bass.ds(g * CPG, CPG), :]).then_inc(f.d_in, 16)

        def act_hi_gu(e, f, g, c, gate_free):
            for m, (raw, arrived) in enumerate(((rawg, f.g_in), (rawu, f.u_in))):
                e.wait_ge(arrived, g * 16 + 16)
                if m == 0 and gate_free is not None:
                    e.wait_ge(f.gu_mm, gate_free)
                e.activation(W1[:, c, m, HI], raw[:, :, c * P:(c + 1) * P], ACT.Copy).then_inc(f.gu_hi, 1)

        def dve_lo_gu(e, f, g, c, m):
            raw = (rawg, rawu)[m]
            e.wait_ge(f.gu_hi, g * (2 * CPG) + (2 * c + m + 1))
            e.tensor_tensor(W1[:, c, m, LO], raw[:, :, c * P:(c + 1) * P], W1[:, c, m, HI].bitcast(F32),
                            ALU.subtract).then_inc(f.gu_lo, 1)

        def dve_scale_d(e, f, g):
            e.wait_ge(f.d_in, g * 16 + 16)
            for c in range(CPG):
                e.tensor_tensor(rawd[:, c], rawd[:, c], grow[:], ALU.mult).then_inc(f.d_scaled, 1)

        def act_hi_d(e, f, g):
            for c in range(CPG):
                e.wait_ge(f.d_scaled, g * CPG + c + 1)
                e.activation(WD[:, c, HI], rawd[:, c], ACT.Copy).then_inc(f.d_hi, 1)

        def dve_lo_d(e, f, g):
            for c in range(CPG):
                e.wait_ge(f.d_hi, g * CPG + c + 1)
                e.tensor_tensor(WD[:, c, LO], rawd[:, c], WD[:, c, HI].bitcast(F32), ALU.subtract).then_inc(f.d_lo, 1)

        STEPS = [(0, 0), (0, 1), (1, 0), (1, 1)]
        FIRST_STEPS = [(0, 0), (1, 0), (0, 1), (1, 1)]

        def pe_gateup(e, f, n, g, first=False, after={}):
            for s, (c, h) in enumerate(FIRST_STEPS if first else STEPS):
                if first and s in (0, 2):
                    e.wait_ge(n.x_lo, KC * (h + 1))
                e.wait_ge(f.gu_lo, g * (2 * CPG) + 2 * c + 2)
                if not (first and s < 2):
                    e.wait_ge(f.mul, g * 4 + s - 1)
                for m in range(2):
                    bank = 2 * (s % 2) + m
                    k = 0
                    for kc in range(KC):
                        for wx, xx in PASSES:
                            mm = e.matmul(ps[:, bank], W1[:, c, m, wx, kc], X[xx][:, kc, h * HALF:(h + 1) * HALF],
                                          start=(k == 0), stop=(k == 3 * KC - 1))
                            k += 1
                mm.then_inc(f.gu_mm, 1)
                if s in after:
                    after[s]()

        def act_silu(e, f, n, g, s):
            e.wait_ge(f.gu_mm, g * 4 + s + 1)
            if not (isinstance(g, int) and g == 0 and s < 2):
                e.wait_ge(f.a_lo, g * 4 + s - 1)
            else:
                e.wait_ge(n.x_lo, NH * KC)
            e.activation(tmp[:, s % 2], ps[:, 2 * (s % 2)], ACT.Silu).then_inc(f.silu, 1)

        def dve_hidden(e, f, g, par, s, steps=STEPS):
            c, h = steps[s]
            tok = slice(h * HALF, (h + 1) * HALF)
            e.wait_ge(f.silu, g * 4 + s + 1)
            e.tensor_tensor(tmp[:, s % 2], ps[:, 2 * (s % 2) + 1], tmp[:, s % 2], ALU.mult).then_inc(f.mul, 1)
            e.wait_ge(f.mul, g * 4 + s + 1)
            e.tensor_copy(AT[:, par, c, HI, tok], tmp[:, s % 2]).then_inc(f.a_hi, 1)
            e.wait_ge(f.a_hi, g * 4 + s + 1)
            e.tensor_tensor(AT[:, par, c, LO, tok], tmp[:, s % 2], AT[:, par, c, HI, tok].bitcast(F32),
                            ALU.subtract).then_inc(f.a_lo, 1)

        DB = 3

        def pe_down(e, f, g, par, ks):
            for k in ks:
                t, h = divmod(k, 2)
                if k == 0:
                    e.wait_ge(f.a_lo, g * 4 + 4)
                    e.wait_ge(f.d_lo, g * CPG + CPG)
                if k >= DB:
                    e.wait_ge(f.added, g * (2 * NT) + k - DB + 1)
                n = 0
                for c in range(CPG):
                    for wx, ax in PASSES:
                        mm = e.matmul(ps[:, 4 + k % DB], AT[:, par, c, ax, t * P:(t + 1) * P],
                                      WD[:, c, wx, h * HALF:(h + 1) * HALF], start=(n == 0), stop=(n == 3 * CPG - 1))
                        n += 1
                mm.then_inc(f.down_mm, 1)

        def dve_add(e, f, g, ks):
            for k in ks:
                t, h = divmod(k, 2)
                e.wait_ge(f.down_mm, g * (2 * NT) + k + 1)
                dst = H[:, t, h * HALF:(h + 1) * HALF]
                e.tensor_tensor(dst, ps[:, 4 + k % DB], dst, ALU.add).then_inc(f.added, 1)

        def act_norm_tiles(e, n, tiles, ready):
            def square(t):
                ready(e, t)
                e.activation(XS[:, t], H[:, t], ACT.Square, accum_out=stat[:, t:t + 1]).then_inc(sumsq, 1)

            def scale(t):
                e.wait_ge(rms_inv, n.base + t + 1)
                e.activation(XS[:, t], H[:, t], ACT.Copy, scale=stat[:, 2 * NT + t:2 * NT + t + 1]).then_inc(n.scaled, 1)

            square(tiles[0])
            for t in tiles[1:]:
                square(t)
                scale(t - 1)
            scale(tiles[-1])

        def pool_rstd(e, base):
            for t in range(NT):
                e.wait_ge(sumsq, base + t + 1)
                e.tensor_scalar(stat[:, NT + t:NT + t + 1], stat[:, t:t + 1], 1.0 / D, EPS, ALU.mult, ALU.add)\
                    .then_inc(mean_sq, 1)
                e.wait_ge(mean_sq, base + t + 1)
                e.tensor_tensor(stat[:, 2 * NT + t:2 * NT + t + 1], stat[:, NT + t:NT + t + 1], mhalf[:, t:t + 1],
                                ALU.pow).then_inc(rms_inv, 1)

        TB = 4

        def pe_turn(e, n, h):
            e.wait_ge(n.scaled, THALF * (h + 1))
            for kc in range(KC):
                u = h * KC + kc
                if kc >= TB:
                    e.wait_ge(n.modulated, u - TB + 1)
                for j in range(THALF):
                    mm = e.transpose(ps[:, h * TB + kc % TB, j * P:(j + 1) * P],
                                     XS[:, h * THALF + j, kc * P:(kc + 1) * P], ident[:])
                mm.then_inc(n.turned, 1)

        def act_modulate(e, n, shift, scale, h):
            for kc in range(KC):
                u = h * KC + kc
                e.wait_ge(n.turned, u + 1)
                if u >= 2:
                    e.wait_ge(n.x_lo, u - 1)
                e.activation(tmp[:, u % 2], ps[:, h * TB + kc % TB], ACT.Identity, bias=modc[:, shift * KC + kc:shift * KC + kc + 1],
                             scale=modc[:, scale * KC + kc:scale * KC + kc + 1]).then_inc(n.modulated, 1)

        def dve_cut_x(e, n, h, kcs=range(KC)):
            for kc in kcs:
                u = h * KC + kc
                tok = slice(h * HALF, (h + 1) * HALF)
                e.wait_ge(n.modulated, u + 1)
                e.tensor_copy(xh[:, kc, tok], tmp[:, u % 2]).then_inc(n.x_hi, 1)
                e.wait_ge(n.x_hi, u + 1)
                e.tensor_tensor(xl[:, kc, tok], tmp[:, u % 2], xh[:, kc, tok].bitcast(F32), ALU.subtract)\
                    .then_inc(n.x_lo, 1)

        def sp_ada_piece(e, v, kc):
            j = (v - 2) * KC + kc
            if not (isinstance(v, int) and v == 2 and kc < 2):
                e.wait_ge(ada_step, v * KC + kc - 1)
            e.dma_start(ada_raw[:, kc % 2], ada_d[:, kc, bass.ds(v * D, D)]).then_inc(ada_in[kc % 2], 16)

        def dve_ada_piece(e, v, kc, src=None):
            if src is None:
                src = ada_raw[:, kc % 2]
                e.wait_ge(ada_in[kc % 2], (v - 2) * (16 * KC // 2) + (kc // 2) * 16 + 16)
            if kc == 0:
                if not (isinstance(v, int) and v == 0):
                    e.wait_ge(acc_used, v)
                e.tensor_scalar(ada_acc[:], src, silu_c[:, kc:kc + 1], None, ALU.mult).then_inc(ada_step, 1)
            else:
                e.wait_ge(ada_step, v * KC + kc)
                e.scalar_tensor_tensor(out=ada_acc[:], in0=src, scalar=silu_c[:, kc:kc + 1], in1=ada_acc[:],
                                       op0=ALU.mult, op1=ALU.add).then_inc(ada_step, 1)

        def pe_ada_sum(e, v):
            e.wait_ge(ada_step, v * KC + KC)
            if not (isinstance(v, int) and v == 0):
                e.wait_ge(mod_ok, v)
            for j in range(KC):
                mm = e.matmul(ps[:, MISC, j:j + 1], ada_acc[:, j * P:(j + 1) * P], ones[:, 0:1], start=True, stop=True)
            mm.then_inc(acc_used, 1)

        def dve_ada_column(e, v, kind):
            e.wait_ge(acc_used, v + 1)
            cols = bass.ds(v * KC, KC)
            src = ps[:, MISC, 0:KC]
            if kind == "scale":
                e.scalar_tensor_tensor(out=modc[:, cols], in0=src, scalar=1.0, in1=vect[:, cols], op0=ALU.add,
                                       op1=ALU.add).then_inc(mod_ok, 1)
            elif kind == "half":
                e.scalar_tensor_tensor(out=modc[:, cols], in0=src, scalar=0.5, in1=half_b[:, cols], op0=ALU.mult,
                                       op1=ALU.add).then_inc(mod_ok, 1)
            else:
                e.tensor_tensor(modc[:, cols], src, vect[:, cols], ALU.add).then_inc(mod_ok, 1)

        KIND = {S1: "scale", SMX: "scale", S2: "scale", G1: "half", G2: "half"}

        def dve_row_diag(e, r, v, row=grow):
            e.tensor_tensor(row[:].rearrange("p (k j) -> p k j", k=KC), ident[:].unsqueeze(1).broadcast_to([P, KC, P]),
                            modc[:, v * KC:(v + 1) * KC].unsqueeze(2).broadcast_to([P, KC, P]), ALU.mult).then_inc(row_src, 1)

        ROW_BANKS = (MISC, 4)

        def pe_row(e, r, row=grow):
            e.wait_ge(row_src, r + 1)
            for h in range(2):
                mm = e.matmul(ps[:, ROW_BANKS[h]], ones[:], row[:, h * HALF:(h + 1) * HALF], start=True, stop=True)
            mm.then_inc(row_mm, 1)

        def dve_row_copy(e, r, row=grow):
            e.wait_ge(row_mm, r + 1)
            for h in range(2):
                e.tensor_copy(row[:, h * HALF:(h + 1) * HALF], ps[:, ROW_BANKS[h]]).then_inc(row_ok, 1)

        LAST = (GROUPS - 1) // 2 - 1

        def sp_ffn(e, f, w, ada):
            def turn(i, last):
                for j in (1, 2):
                    g = i * 2 + j
                    sp_load_d(e, f, w, g)
                    if ada:
                        for kc in range(KC // 2 * (j - 1), KC // 2 * j):
                            sp_ada_piece(e, i + SMX, kc)
                    if not (last and j == 2):
                        sp_load_gu(e, f, w, g + 1)

            with e.Fori(0, LAST) as i:
                turn(i, False)
            turn(LAST, True)

        def act_ffn(e, f, n):
            def period(g, first, last):
                if not first:
                    act_hi_d(e, f, g - 1)
                act_silu(e, f, n, g, 0)
                act_silu(e, f, n, g, 1)
                if not last and not first:
                    act_hi_gu(e, f, g + 1, 0, g * 4 + 2)
                act_silu(e, f, n, g, 2)
                act_silu(e, f, n, g, 3)
                if not last:
                    if first:
                        act_hi_gu(e, f, g + 1, 0, g * 4 + 3)
                    act_hi_gu(e, f, g + 1, 1, g * 4 + 4)

            period(0, True, False)
            with e.Fori(0, LAST) as i:
                period(i * 2 + 1, False, False)
                period(i * 2 + 2, False, False)
            period(2 * LAST + 1, False, False)
            period(2 * LAST + 2, False, True)
            act_hi_d(e, f, GROUPS - 1)

        def dve_period(e, f, g, par, last, pieces):
            pieces = list(pieces)

            def some(k):
                for _ in range(min(k, len(pieces))):
                    dve_ada_piece(e, *pieces.pop(0))

            dve_scale_d(e, f, g - 1)
            dve_lo_d(e, f, g - 1)
            dve_hidden(e, f, g, par, 0)
            some(2)
            dve_hidden(e, f, g, par, 1)
            if not last:
                dve_lo_gu(e, f, g + 1, 0, 0)
                dve_lo_gu(e, f, g + 1, 0, 1)
            dve_hidden(e, f, g, par, 2)
            some(2)
            dve_hidden(e, f, g, par, 3)
            dve_add(e, f, g - 1, range(0, 4))
            if not last:
                dve_lo_gu(e, f, g + 1, 1, 0)
            dve_add(e, f, g - 1, range(4, 8))
            if not last:
                dve_lo_gu(e, f, g + 1, 1, 1)
            dve_add(e, f, g - 1, range(8, 2 * NT))

        def dve_first(e, f, row, before_row, after_row):
            dve_hidden(e, f, 0, 0, 0, FIRST_STEPS)
            dve_hidden(e, f, 0, 0, 1, FIRST_STEPS)
            before_row()
            dve_hidden(e, f, 0, 0, 2, FIRST_STEPS)
            after_row()
            for m in range(2):
                dve_lo_gu(e, f, 1, 0, m)
            dve_hidden(e, f, 0, 0, 3, FIRST_STEPS)
            for m in range(2):
                dve_lo_gu(e, f, 1, 1, m)

        def dve_turns(e, f, ada):
            def turn(i, last):
                for j, par in ((1, 1), (2, 0)):
                    half = range(KC // 2 * (j - 1), KC // 2 * j)
                    dve_period(e, f, i * 2 + j, par, last and j == 2, [(i + SMX, kc) for kc in half] if ada else [])
                if ada:
                    dve_ada_column(e, i + SMX, None)

            with e.Fori(0, LAST) as i:
                turn(i, False)
            turn(LAST, True)
            dve_scale_d(e, f, GROUPS - 1)
            dve_lo_d(e, f, GROUPS - 1)

        def pe_turns(e, f, n, ada):
            def turn(i):
                for j, par in ((1, 1), (2, 0)):
                    g = i * 2 + j
                    pe_gateup(e, f, n, g)
                    pe_down(e, f, g - 1, 1 - par, range(2 * NT))
                if ada:
                    pe_ada_sum(e, i + SMX)

            with e.Fori(0, LAST) as i:
                turn(i)
            turn(LAST)

        def dve_last_adds_and_cut(e, f, n):
            dve_add(e, f, GROUPS - 1, range(0, 12))
            for k in range(4):
                dve_cut_x(e, n, 0, range(2 * k, 2 * k + 2))
                dve_add(e, f, GROUPS - 1, [12 + k])

        NU = 2 * NH
        TURNS = NHD // 2
        AUG = QK + 1

        def at(i, m):
            return (i + m // NU, m % NU)

        def pe_max(e, i, m, p):
            i, m = at(i, m)
            hp, h = divmod(m, NH)
            t = h * THALF + p
            if p == 0 and h == 0:
                e.wait_ge(qk_lo, i * 8 + (hp * 4 + 4))
            if not (isinstance(i, int) and i == 0 and m == 0 and p == 0):
                e.wait_ge(s_max, i * 16 + (m * 4 + p))
            for b in range(NH):
                mm = e.matmul(ps[:, b], qkT[0:QK, hp, 0, HI, t * P:(t + 1) * P],
                              qkT[0:QK, hp, 1, HI, b * HALF:(b + 1) * HALF], start=True, stop=True)
            mm.then_inc(max_mm, 1)

        def dve_max(e, i, m, p):
            i, m = at(i, m)
            e.wait_ge(max_mm, i * 16 + (m * 4 + p + 1))
            e.tensor_reduce(negmax[:, m % 2, p:p + 1], ps[:, 0:NH].rearrange("p b k -> p (b k)"), AX_X, ALU.max,
                            negate=True).then_inc(s_max, 1)

        def pe_max_row(e, i, m, first=False):
            i, m = at(i, m)
            e.wait_ge(s_max, i * 16 + (m * 4 + 4))
            if not first:
                e.wait_ge(m_lo, i * 4 + m)
            ahead = m % NH == 1 and not (isinstance(i, int) and i == TURNS - 1 and m // NH == 1)
            e.wait_ge(qk_y, i * 8 + (4 * (m // NH) + (8 if ahead else 4)))
            if isinstance(i, int) and (i, m) == (TURNS - 1, 2):
                e.wait_ge(ln_mean, 2 * CC)
            for p in range(THALF):
                mm = e.matmul(ps[0:1, MISC, p * P:(p + 1) * P], negmax[:, m % 2, p:p + 1], ident[:], start=True, stop=True)
            mm.then_inc(m_row, 1)

        def max_place(m, a):
            hp, h = divmod(m, NH)
            return qkT[QK:AUG, hp, 0, a, h * HALF:(h + 1) * HALF]

        def act_max_hi(e, i, m):
            i, m = at(i, m)
            e.wait_ge(m_row, i * 4 + (m + 1))
            e.activation(max_place(m, HI), ps[0:1, MISC], ACT.Copy).then_inc(m_hi, 1)

        def dve_max_lo(e, i, m):
            i, m = at(i, m)
            e.wait_ge(m_hi, i * 4 + (m + 1))
            e.tensor_tensor(max_place(m, LO), ps[0:1, MISC], max_place(m, HI).bitcast(F32), ALU.subtract).then_inc(m_lo, 1)

        def pe_scores(e, i, m, p):
            hp, h = divmod(m, NH)
            if p == 0:
                e.wait_ge(m_lo, i * 4 + (m + 1))
            if not (isinstance(i, int) and i == 0 and m == 0 and p < 2):
                e.wait_ge(s_exp, i * 16 + (m * 4 + p - 1))
            for b in range(2):
                kt = 2 * p + b
                for k, (x, y) in enumerate(PASSES):
                    mm = e.matmul(ps[:, 2 + 2 * (p % 2) + b], qkT[0:AUG, hp, 1, x, kt * P:(kt + 1) * P],
                                  qkT[0:AUG, hp, 0, y, h * HALF:(h + 1) * HALF], start=(k == 0), stop=(k == 2))
            mm.then_inc(s_mm, 1)

        def act_exp(e, i, m, p):
            e.wait_ge(s_mm, i * 16 + (m * 4 + p + 1))
            if p == 0 and not (isinstance(i, int) and i == 0 and m < 2):
                e.wait_ge(pv_mm, i * 4 + (m - 1))
            b = 2 + 2 * (p % 2)
            e.activation(EX[m % 2][:, 2 * p:2 * p + 2], ps[:, b:b + 2], ACT.Exp).then_inc(s_exp, 1)

        def pe_pv(e, i, m, p):
            hp = (m - 1) % NU // NH
            if p == 0:
                e.wait_ge(s_exp, i * 16 + m * 4)
                if m % NH == 1:
                    e.wait_ge(v_ok, i * 2 + (hp + 1))
                if not (isinstance(i, int) and i == 0 and m == 1):
                    e.wait_ge(pv_copied, i * 4 + (m - 1))
            for kt in (2 * p, 2 * p + 1):
                mm = e.matmul(ps[:, 6], vs[:, hp, kt], EX[(m - 1) % 2][:, kt], start=(kt == 0), stop=(kt == NT - 1))
            if p == THALF - 1:
                mm.then_inc(pv_mm, 1)

        def act_pv_copy(e, i, m):
            e.wait_ge(pv_mm, i * 4 + m)
            if not (isinstance(i, int) and i == 0 and m == 1):
                e.wait_ge(pv_out, i * 4 + (m - 1))
            e.activation(grow[:, 0:HALF], ps[:, 6], ACT.Copy).then_inc(pv_copied, 1)

        def dve_pv_out(e, i, m):
            hp, h = (m - 1) % NU // NH, (m - 1) % NH
            chunk = i if m >= 1 else i - 1
            e.wait_ge(pv_copied, i * 4 + m)
            e.reciprocal(grow[0:VH, HALF:D], grow[VH:2 * VH, 0:HALF]).then_inc(pv_rec, 1)
            e.wait_ge(pv_rec, i * 4 + m)
            dst = att[hp * VH:(hp + 1) * VH, bass.ds(chunk, 1), h * HALF:(h + 1) * HALF].rearrange("p a q -> p (a q)")
            e.tensor_tensor(dst, grow[0:VH, 0:HALF], grow[0:VH, HALF:D], ALU.mult).then_inc(pv_out, 1)

        def act_v(e, i, hp, first=False):
            hd = i * 2 + hp
            if not first:
                e.wait_ge(pv_mm, hd * 2 - 2)
            e.activation(vs[:, hp, :, 0:VH], vn[:, :, bass.ds(hd, 1), :].rearrange("p t a d -> p t (a d)"), ACT.Copy)\
                .then_inc(v_ok, 1)

        def pe_turn_head(e, i, hp, u, first=False):
            e.wait_ge((slot_q, slot_k)[u // 2], i * 2 + (hp + 1))
            if not (first and u == 0):
                e.wait_ge(qk_y, i * 8 + (hp * 4 + u))
            if not first and u == 0:
                e.wait_ge(m_lo, i * 4 + (hp * 2 - 1))
            for k in range(THALF):
                mm = e.transpose(ps[0:QK, 7, k * P:(k + 1) * P], slot[:, u // 2, (u % 2) * THALF + k], ident[:])
            mm.then_inc(qk_turned, 1)

        def act_head_unit(e, i, hp, u, first=False):
            e.wait_ge(qk_turned, i * 8 + (hp * 4 + u + 1))
            if not (first and u < 2):
                e.wait_ge(qk_lo, i * 8 + (hp * 4 + u - 1))
            e.activation(tmp[0:QK, u % 2], ps[0:QK, 7], ACT.Copy, scale=gains[0:QK, u // 2:u // 2 + 1]).then_inc(qk_y, 1)

        def dve_head_unit(e, i, hp, u):
            qk, h = divmod(u, 2)
            tok = slice(h * HALF, (h + 1) * HALF)
            e.wait_ge(qk_y, i * 8 + (hp * 4 + u + 1))
            e.tensor_copy(qkT[0:QK, hp, qk, HI, tok], tmp[0:QK, u % 2]).then_inc(qk_hi, 1)
            e.wait_ge(qk_hi, i * 8 + (hp * 4 + u + 1))
            e.tensor_tensor(qkT[0:QK, hp, qk, LO, tok], tmp[0:QK, u % 2], qkT[0:QK, hp, qk, HI, tok].bitcast(F32),
                            ALU.subtract).then_inc(qk_lo, 1)

        def pool_slots(e, i, hp, first=False):
            hd = i * 2 + hp
            r = rqk[:, :, bass.ds(hd, 1)]
            if not first:
                e.wait_ge(qk_turned, hd * 4 - 2)
            e.tensor_tensor(slot[:, 0], qn[:, :, bass.ds(hd, 1), :].rearrange("p t a d -> p t (a d)"),
                            r.broadcast_to([P, NT, QK]), ALU.mult).then_inc(slot_q, 1)
            if not first:
                e.wait_ge(qk_turned, hd * 4)
            r = rqk[:, :, bass.ds(hd + NHD, 1)]
            e.tensor_tensor(slot[:, 1, :, 0:NOPE], kn[:, :, bass.ds(hd, 1), :].rearrange("p t a d -> p t (a d)"),
                            r.broadcast_to([P, NT, NOPE]), ALU.mult)
            e.tensor_tensor(slot[:, 1, :, NOPE:QK], kr[:], r.broadcast_to([P, NT, ROPE]), ALU.mult).then_inc(slot_k, 1)

        CT = TURNS - 1
        TT = (CONV_K - 1) // CT

        def act_prod(e, i, n, first):
            c, k = 2 + n % 2, 1 + n // 2
            if not (first and n < 2):
                e.wait_ge(conv_add, i * (2 * TT) + (n - 1))
            e.activation(prod[:, n % 2], ac[:, c, bass.ds(i * TT + k, S)], ACT.Copy,
                         scale=cw[:, c, bass.ds(i * TT + k, 1)]).then_inc(prod_ok, 1)

        def pool_conv(e, i, n, first):
            c = 2 + n % 2
            e.wait_ge(prod_ok, i * (2 * TT) + (n + 1))
            if not (first and n < 2):
                e.wait_ge(conv_add, i * (2 * TT) + (n - 1))
            e.tensor_tensor(cv[:, c], cv[:, c], prod[:, n % 2], ALU.add).then_inc(conv_add, 1)

        DTT = 4
        DT = CONV_K - DTT * CT

        def dve_tap(e, i):
            for c in range(2):
                e.wait_ge(conv, i * 2 + (c - 1))
                e.scalar_tensor_tensor(out=cv[:, c], in0=ac[:, c, bass.ds(i, S)], scalar=cw[:, c, bass.ds(i, 1)],
                                       in1=cv[:, c], op0=ALU.mult, op1=ALU.add).then_inc(conv, 1)

        def dve_conv(e, a, b):
            with e.Fori(a, b) as i:
                dve_tap(e, i)

        def dve_tap0(e, c, count):
            e.tensor_scalar(cv[:, c], ac[:, c, 0:S], cw[:, c, 0:1], vect[:, V_CB + c:V_CB + c + 1], ALU.mult, ALU.add)\
                .then_inc(count, 1)

        squares = (prod[:, 0], prod[:, 1], pp[:, 0], pp[:, 1])

        def pool_pair_sums(e, pairs, done):
            for n, (dst, a, b) in enumerate(pairs):
                if n == 2:
                    e.wait_ge(ln_pool, done + 2)
                e.tensor_tensor(dst, a, b, ALU.add).then_inc(ln_pool, 1)

        def pe_ln_mean(e, h):
            if h == 0:
                e.wait_ge(ln_pool, 3)
                e.wait_ge(m_lo, NU * (TURNS - 1) + 2)
                e.wait_ge(qk_y, 4 * NHD)
            else:
                e.wait_ge(ln_mean, CC)
            e.matmul(ps[:, MISC], ones[:], pp[:, 0, h * HALF:(h + 1) * HALF], start=True, stop=True).then_inc(ln_mm, 1)

        def dve_ln_mean(e, h):
            e.wait_ge(ln_mm, h + 1)
            for c in range(CC):
                x = cv[:, c, h * HALF:(h + 1) * HALF]
                e.scalar_tensor_tensor(out=x, in0=ps[:, MISC], scalar=-1.0 / CH, in1=x, op0=ALU.mult, op1=ALU.add)\
                    .then_inc(ln_mean, 1)

        def act_ln_square(e, c):
            e.wait_ge(ln_mean, 2 * CC)
            e.activation(squares[c], cv[:, c], ACT.Square).then_inc(ln_act, 1)

        def pe_ln_var(e):
            e.wait_ge(ln_pool, 6)
            e.wait_ge(m_lo, NU * TURNS)
            for t in range(NT):
                mm = e.matmul(ps[:, MISC, t:t + 1], pp[:, 0, t * P:(t + 1) * P], ones[:, 0:1], start=True, stop=True)
            mm.then_inc(ln_mm, 1)

        def dve_ln_var(e):
            e.wait_ge(ln_mm, 3)
            e.tensor_scalar(stat[:, 0:NT], ps[:, MISC, 0:NT], 1.0 / CH, 1e-5, ALU.mult, ALU.add).then_inc(ln_dve, 1)

        def dve_ln_diag(e):
            e.wait_ge(ln_pool, 7)
            e.tensor_tensor(pp[:, 1].rearrange("p (k j) -> p k j", k=NT), ident[:].unsqueeze(1).broadcast_to([P, NT, P]),
                            stat[:, NT:2 * NT].unsqueeze(2).broadcast_to([P, NT, P]), ALU.mult).then_inc(ln_dve, 1)

        def pe_ln_rstd(e):
            e.wait_ge(ln_dve, 2)
            e.wait_ge(s_max, 4 * NU * TURNS)
            for h in range(2):
                mm = e.matmul(ps[:, h], ones[:], pp[:, 1, h * HALF:(h + 1) * HALF], start=True, stop=True)
            mm.then_inc(ln_mm, 1)

        def dve_ln_scale(e):
            e.wait_ge(ln_mm, 4)
            for c in range(CC):
                e.tensor_tensor(cv[:, c], cv[:, c], ps[:, 0:2].rearrange("p b n -> p (b n)"), ALU.mult).then_inc(ln_dve, 1)

        def act_ln_swish(e):
            for c in range(CC):
                e.wait_ge(ln_dve, 3 + c)
                e.activation(cv[:, c], cv[:, c], ACT.Silu, bias=vect[:, V_LB + c:V_LB + c + 1],
                             scale=vect[:, V_LG + c:V_LG + c + 1]).then_inc(ln_act, 1)

        WO_AT = {(1, 3): 0, (2, 0): 1, (2, 2): 2, (2, 3): 3, (3, 0): 4, (3, 1): 5, (3, 2): 6}

        def pool_wo_scale(e, c):
            e.wait_ge(wo_in[c % 2], 16 * (c // 2 + 1))
            e.tensor_tensor(wor[:, c % 2], wor[:, c % 2], gm_row[:], ALU.mult).then_inc(wo_scaled, 1)

        def act_wo_hi(e, c):
            e.wait_ge(wo_scaled, c + 1)
            if c == 0:
                e.wait_ge(slot_k, NHD)
            if c == 5:
                e.wait_ge(v_ok, NHD)
            if c == 7:
                e.wait_ge(pv_mm, 2 * NHD)
            e.activation(wo[:, c, HI], wor[:, c % 2], ACT.Copy).then_inc(wo_hi, 1)

        def dve_wo_lo(e, c):
            e.wait_ge(wo_hi, c + 1)
            e.tensor_tensor(wo[:, c, LO], wor[:, c % 2], wo[:, c, HI].bitcast(F32), ALU.subtract).then_inc(wo_lo, 1)

        def run_units(e, unit):
            for m in range(NU):
                unit(0, m, True, False)
            with e.Fori(1, TURNS - 1) as i:
                for m in range(NU):
                    unit(i, m, False, False)
            for m in range(NU):
                unit(TURNS - 1, m, False, True)

        def next_head(i, m):
            return (i, 1) if m // NH == 0 else (i + 1, 0)

        def mix_src(part, t):
            return (cv, att)[part][:, :, t * P:(t + 1) * P]

        MB = 3

        block = ctx.enter_context(nc.Block())

        @block.sync
        def _(e):
            e.wait_ge(consts, 1)
            rows = ((A["b_ada"], V_BADA, N_MOD * KC), (A["c"], V_C, KC), (A["conv_b"], V_CB, CC), (A["g_conv_ln"], V_LG, CC),
                    (A["b_conv_ln"], V_LB, CC), (A["g_q_lat"], V_GQ, QL // P), (A["g_kv_lat"], V_GKV, KVL // P))
            for a, to, n in rows:
                e.dma_start(vec[to:to + n, :], a.rearrange("a (r q) -> (a r) q", q=P)).then_inc(vec_in, 16)
            for m, g in enumerate(("g_q_head", "g_k_head")):
                e.dma_start(gains[0:NOPE, m:m + 1], A[g][:, 0:NOPE].rearrange("a d -> d a")).then_inc(vec_in, 16)
            for t in range(NT):
                e.dma_start(H[:, t], x_d[:, t]).then_inc(x_in[t], 16)
            for v in range(2):
                for k in range(KC // 2):
                    two = slice(2 * k, 2 * k + 2)
                    e.dma_start(ada01[:, v, two], ada_d[:, two, v * D:(v + 1) * D]).then_inc(ada01_in[v][k], 16)
            e.wait_ge(vec_ok, 1)
            sp_load_gu(e, fs[0], ffn_w[0], 0)
            for kc in range(KC):
                sp_ada_piece(e, G1, kc)
            sp_load_d(e, fs[0], ffn_w[0], 0)
            sp_load_gu(e, fs[0], ffn_w[0], 1)
            for kc in range(KC):
                sp_ada_piece(e, SHM, kc)
            sp_ffn(e, fs[0], ffn_w[0], True)

            e.wait_ge(fs[0].gu_lo, 2 * CPG * GROUPS)
            sp_load_gu(e, U, glu_w, 0)
            e.wait_ge(mod_ok, N_MOD)
            e.dma_start(lata[:], win_d[:, :, 2 * CH:2 * CH + NZ]).then_inc(lat_in[0], 16)
            e.dma_start(cwr[0:CONV_K, :], A["conv_w"][0].rearrange("k a c -> k (a c)")).then_inc(small_in, 16)
            e.dma_start(posr[:], A["positions"].rearrange("a (t q) -> (a t) q", q=P)).then_inc(small_in, 16)
            e.wait_ge(fs[0].d_lo, CPG * GROUPS)
            e.dma_start(latb[:], win_d[:, :, 2 * CH + NZ:2 * CH + W_IN_L]).then_inc(lat_in[1], 16)
            for t in range(NT):
                e.wait_ge(ns[1].scaled, t + 1)
                e.dma_start(h_dram[:, t], H[:, t]).then_inc(h_saved, 16)
            sp_load_gu(e, U, glu_w, 1)
            e.wait_ge(h_saved, 16 * NT)
            for m, g in enumerate(("g_q_head", "g_k_head")):
                e.dma_start(grot[:, m], A[g][:, NOPE:QK].broadcast_to([P, ROPE])).then_inc(grot_in, 16)
            e.wait_ge(U.gu_lo, 2 * 2 * CPG)
            e.dma_start(wqr[:, :, 0:NHD * QK], A["w_q_up"][0].rearrange("(k p) n -> p k n", p=P)).then_inc(up_in[0], 16)
            e.dma_start(wkr, A["w_kv_up"][0]).then_inc(up_in[1], 16)
            e.wait_ge(qk_turned, 4 * NHD)
            for c in range(KC):
                if c >= 2:
                    e.wait_ge(wo_lo, c - 1)
                e.dma_start(wor[:, c % 2], A["w_out"][0][c * P:(c + 1) * P, :]).then_inc(wo_in[c % 2], 16)
            e.wait_ge(ln_pool, 6)
            for n in range(2):
                half = slice(n * THALF, (n + 1) * THALF)
                e.dma_start(H[:, half], h_dram[:, half]).then_inc(h_back[n], 16)
            e.wait_ge(wo_lo, KC)
            e.wait_ge(mix_lo, 2 * NT)
            f = fs[1]
            sp_load_gu(e, f, ffn_w[1], 0)
            sp_load_d(e, f, ffn_w[1], 0)
            sp_load_gu(e, f, ffn_w[1], 1)
            sp_ffn(e, f, ffn_w[1], False)
            e.wait_ge(f.d_scaled, CPG * GROUPS)
            e.dma_start(grow[:], A["g_final"].broadcast_to([P, D])).then_inc(gfin_in, 16)
            for t in range(NT):
                e.wait_ge(o_ok, t + 1)
                e.dma_start(out_d[:, t], H[:, t]).then_inc(final_out, 16)
            e.wait_ge(final_out, 16 * NT)

        @block.gpsimd
        def _(e):
            e.memset(gains[:], 1.0)
            e.memset(vec[:], 0.0).then_inc(consts, 1)
            e.memset(ident[:], 0.0).then_inc(consts, 1)
            e.wait_ge(consts, 2)
            e.affine_select(out=ident[:], in_=ident[:], compare_op=ALU.not_equal, fill=1.0, base=0,
                            pattern=[[-1, P]], channel_multiplier=1).then_inc(consts, 1)
            e.memset(ones[:], 1.0).then_inc(consts, 1)
            e.memset(mhalf[:], -0.5).then_inc(consts, 1)
            e.wait_ge(consts, 5)
            pool_rstd(e, ns[0].base)
            pool_rstd(e, ns[1].base)
            e.wait_ge(ns[1].scaled, NT)
            for j in range(ROPE // 2):
                e.memset(trig[:, 2, 0, j:ROPE:ROPE // 2], INV_FREQ[j])
            e.wait_ge(h_saved, 16 * NT)
            e.memset(ac[:, :, 0:CONV_PAD], 0.0)
            e.memset(ac[:, :, CONV_PAD + S:ACW], 0.0)
            e.memset(cw[:, :, CONV_K:CONV_K + 2], 0.0).then_inc(pads, 1)
            e.wait_ge(z_sq, 2 * NT)
            e.tensor_scalar(zstat[:, 2 * NT:3 * NT], zstat[:, 0:NT], 1.0 / QL, EPS, ALU.mult, ALU.add)
            e.tensor_scalar(zstat[:, 3 * NT:4 * NT], zstat[:, NT:2 * NT], 1.0 / KVL, EPS, ALU.mult, ALU.add)\
                .then_inc(z_rstd, 1)
            e.wait_ge(z_rstd, 1)
            e.tensor_tensor(zstat[:, 4 * NT:6 * NT], zstat[:, 2 * NT:4 * NT], mhalf[:], ALU.pow).then_inc(z_rstd, 1)
            e.wait_ge(qk_sum, 1)
            e.tensor_scalar(qs[:], qs[:], 1.0 / QK, EPS, ALU.mult, ALU.add).then_inc(qk_rstd, 1)
            e.wait_ge(qk_rstd, 1)
            e.tensor_tensor(rqk[:], qs[:], qh[:], ALU.pow).then_inc(qk_rstd, 1)
            e.wait_ge(qk_rstd, 2)
            e.wait_ge(rope, 2)
            pool_slots(e, 0, 0, True)
            e.wait_ge(tap0, 2)

            pool_slots(e, 0, 1)

            def unit(i, m, first, last):
                if m % NH == 1 and not last:
                    pool_slots(e, i + 1, m // NH)
                if not last:
                    for n in range(m * TT // 2, (m + 1) * TT // 2):
                        pool_conv(e, i, n, first)

            run_units(e, unit)
            e.wait_ge(conv_add, 2 * (CONV_K - 1))
            e.wait_ge(conv, 2 * CONV_K)
            pool_pair_sums(e, ((pp[:, 0], cv[:, 0], cv[:, 1]), (pp[:, 1], cv[:, 2], cv[:, 3]), (pp[:, 0], pp[:, 0], pp[:, 1])), 0)
            for c in range(3):
                pool_wo_scale(e, c)
            e.wait_ge(ln_act, CC)
            pool_pair_sums(e, ((squares[0], squares[0], squares[1]), (squares[2], squares[2], squares[3]),
                               (pp[:, 0], squares[0], squares[2])), 3)
            for c in range(3, 6):
                pool_wo_scale(e, c)
            e.wait_ge(ln_dve, 1)
            e.tensor_tensor(stat[:, NT:2 * NT], stat[:, 0:NT], mhalf[:, 0:NT], ALU.pow).then_inc(ln_pool, 1)
            for c in range(6, KC):
                pool_wo_scale(e, c)
            pool_rstd(e, ns[2].base)
            pool_rstd(e, FINAL)

        @block.scalar
        def _(e):
            e.wait_ge(vec_ok, 2)
            e.activation(silu_c[:], vect[:, V_C:V_C + KC], ACT.Silu).then_inc(silu_ok, 1)
            act_norm_tiles(e, ns[0], range(NT), lambda e, t: e.wait_ge(x_in[t], 16))
            for c in range(CPG):
                act_hi_gu(e, fs[0], 0, c, None)
            e.wait_ge(mod_ok, 2)
            for h in range(NH):
                act_modulate(e, ns[0], SH1, S1, h)
            act_ffn(e, fs[0], ns[0])

            f, n = fs[0], ns[1]

            def done(e, t):
                e.wait_ge(f.added, (GROUPS - 1) * 2 * NT + 2 * t + 2)

            e.wait_ge(f.gu_mm, 4 * GROUPS)
            for c in range(CPG):
                act_hi_gu(e, U, 0, c, None)

            def safe(e, t):
                done(e, t)
                if t == 0:
                    e.wait_ge(f.down_mm, 2 * NT * GROUPS)

            act_norm_tiles(e, n, range(THALF), safe)
            e.wait_ge(mod_ok, N_MOD + 2)
            act_modulate(e, n, SHM, SMX, 0)
            act_norm_tiles(e, n, range(THALF, NT), done)
            act_modulate(e, n, SHM, SMX, 1)
            for b in range(2):
                e.wait_ge(lat_in[b], 16)
                e.activation(wl[:, HI, :, b * NZ:(b + 1) * NZ], (lata, latb)[b][:], ACT.Copy).then_inc(wl_hi, 1)
            e.wait_ge(h_saved, 16 * NT)
            e.wait_ge(trig_ok, 1)
            e.activation(cs[:], trig[:, 3], ACT.Sin).then_inc(cs_ok, 1)

            def sigmoid(s):
                e.wait_ge(U.gu_mm, s + 1)
                if s >= 2:
                    e.wait_ge(U.mul, s - 1)
                else:
                    e.wait_ge(n.x_lo, NH * KC)
                e.activation(tmp[:, s % 2], ps[:, 2 * (s % 2)], ACT.Sigmoid).then_inc(U.silu, 1)

            for s in range(3):
                sigmoid(s)
            act_hi_gu(e, U, 1, 0, 3)
            sigmoid(3)
            act_hi_gu(e, U, 1, 1, 4)
            e.wait_ge(U.mul, 4)
            for t in range(NT):
                e.wait_ge(lat_mm, t + 1)
                b = ps[:, 4 + t % 3]
                if t == 0:
                    e.wait_ge(wl_lo, 2)
                    e.wait_ge(cw_ok, 1)
                e.activation(zz[:, t], b[:, 0:QL + KVL], ACT.Copy)
                e.activation(kr[:, t], b[:, QL + KVL:W_IN_L], ACT.Copy)
                if t >= 1:
                    e.wait_ge(z_sq, 2 * t)
                e.activation(tmp[:, 0, 0:QL], b[:, 0:QL], ACT.Square, accum_out=zstat[:, t:t + 1]).then_inc(z_sq, 1)
                e.activation(tmp[:, 1, 0:KVL], b[:, QL:QL + KVL], ACT.Square, accum_out=zstat[:, NT + t:NT + t + 1])\
                    .then_inc(z_sq, 1)
            e.wait_ge(z_sq, 2 * NT)
            sigmoid(4)
            for v in range(6):
                e.wait_ge(z_turned, v + 1)
                c, h = divmod(v, 2)
                e.activation(CZ[HI][:, c, h * HALF:(h + 1) * HALF], ps[:, 4 + v % 3], ACT.Copy).then_inc(z_hi, 1)
            sigmoid(5)
            e.wait_ge(up_scaled, QL // P)
            e.activation(wq[:, HI], wqr[:, :, 0:NHD * QK], ACT.Copy).then_inc(up_hi, 1)
            e.wait_ge(up_scaled, QL // P + 1)
            e.activation(wkv[:, HI], wkr, ACT.Copy).then_inc(up_hi, 1)
            sigmoid(6)
            sigmoid(7)
            e.wait_ge(z_rstd, 2)
            e.wait_ge(U.mul, 8)
            for t in range(NT):
                e.wait_ge(up_mm, t + 1)
                b = 4 * (t % 2)
                e.activation(qn[:, t].rearrange("p (b h) d -> p b (h d)", b=2), ps[:, b:b + 2, 0:NHD // 2 * QK], ACT.Copy,
                             scale=zstat[:, 4 * NT + t:4 * NT + t + 1]).then_inc(up_out, 1)
                kv = ps[:, b + 2:b + 4].rearrange("p b (h d) -> p (b h) d", d=NOPE + VH)
                e.activation(kn[:, t], kv[:, :, 0:NOPE], ACT.Copy, scale=zstat[:, 5 * NT + t:5 * NT + t + 1])
                e.activation(vn[:, t], kv[:, :, NOPE:NOPE + VH], ACT.Copy, scale=zstat[:, 5 * NT + t:5 * NT + t + 1])\
                    .then_inc(up_out, 1)
                e.wait_ge(up_out, 2 * t + 2)
                if t >= 2:
                    e.wait_ge(qk_sum_t, t)
                sl = sq[:, t % 2]
                e.activation(sl[:, 0:NHD * QK], qn[:, t].rearrange("p h d -> p (h d)"), ACT.Square)
                e.activation(sl[:, NHD * QK:NHD * (QK + NOPE)], kn[:, t].rearrange("p h d -> p (h d)"), ACT.Square)\
                    .then_inc(qk_sq, 1)

            for u in range(4):
                act_head_unit(e, 0, 0, u, True)
            act_max_hi(e, 0, 0)
            act_v(e, 0, 0, True)

            def unit(i, m, first, last):
                for p in range(THALF):
                    if p == 0 and not (first and m < 2):
                        act_pv_copy(e, *at(i, m - 1))
                    if m % NH == 0 and not (last and m // NH == 1):
                        act_head_unit(e, *next_head(i, m), p)
                    if p == 3 and not (last and m == NU - 1):
                        act_max_hi(e, i, m + 1)
                    if last and m == 2 and p < 2:
                        act_ln_square(e, 2 * p)
                        act_ln_square(e, 2 * p + 1)
                    if p == 3 and m % NH == 1 and not (last and m // NH == 1):
                        act_v(e, *next_head(i, m), first=first and m == 1)
                    act_exp(e, i, m, p)
                    if last and (m, p) in WO_AT:
                        act_wo_hi(e, WO_AT[m, p])
                    if not last:
                        for n in range(TT // 2 * p // THALF, TT // 2 * (p + 1) // THALF):
                            act_prod(e, i, m * TT // 2 + n, first)

            run_units(e, unit)
            act_pv_copy(e, TURNS, -1)
            act_ln_swish(e)
            act_pv_copy(e, TURNS, 0)
            act_wo_hi(e, KC - 1)
            f, n = fs[1], ns[2]
            act_norm_tiles(e, n, range(THALF), lambda e, t: e.wait_ge(mix_added, 2 * t + 2))
            for c in range(CPG):
                act_hi_gu(e, f, 0, c, None)
            act_norm_tiles(e, n, range(THALF, NT), lambda e, t: e.wait_ge(mix_added, 2 * NT))
            act_modulate(e, n, SH2, S2, 0)
            act_modulate(e, n, SH2, S2, 1)
            act_ffn(e, f, n)
            for t in range(NT):
                e.wait_ge(f.added, (GROUPS - 1) * 2 * NT + 2 * t + 2)
                if t >= 2:
                    e.wait_ge(sumsq, FINAL + t - 1)
                e.activation(ada_raw[:, t % 2], H[:, t], ACT.Square, accum_out=stat[:, t:t + 1]).then_inc(sumsq, 1)

        @block.vector
        def _(e):
            e.wait_ge(vec_tr, 1)
            e.tensor_copy(vect[:], ps[:, MISC, 0:NV]).then_inc(vec_ok, 2)
            e.wait_ge(vec_ok, 2)
            e.tensor_scalar(half_b[:], vect[:, 0:N_MOD * KC], 0.5, None, ALU.mult).then_inc(vec_ok, 1)
            e.wait_ge(vec_in, 16 * 9)
            e.tensor_scalar(gains[0:QK, 0:1], gains[0:QK, 0:1], float(QK) ** -0.5, None, ALU.mult).then_inc(vec_ok, 1)
            e.wait_ge(silu_ok, 1)
            for v in range(2):
                for kc in range(KC):
                    e.wait_ge(ada01_in[v][kc // 2], 16)
                    dve_ada_piece(e, v, kc, ada01[:, v, kc])
                dve_ada_column(e, v, KIND.get(v))
            f = fs[0]
            for c in range(CPG):
                for m in range(2):
                    dve_lo_gu(e, f, 0, c, m)
            for h in range(NH):
                dve_cut_x(e, ns[0], h)
            e.wait_ge(vec_ok, 3)
            for kc in range(KC):
                dve_ada_piece(e, G1, kc)

            def before_row():
                dve_ada_column(e, G1, "half")
                e.wait_ge(mod_ok, G1 + 1)
                dve_row_diag(e, 0, G1)

            dve_first(e, f, 0, before_row, lambda: dve_row_copy(e, 0))
            for kc in range(KC):
                dve_ada_piece(e, SHM, kc)
            dve_ada_column(e, SHM, None)
            e.wait_ge(row_ok, 2)
            dve_turns(e, f, True)
            e.wait_ge(mod_ok, N_MOD)
            for v, op, by in ((SMX, ALU.add, 1.0), (S2, ALU.add, 1.0), (G2, ALU.mult, 0.5)):
                e.tensor_scalar(modc[:, v * KC:(v + 1) * KC], modc[:, v * KC:(v + 1) * KC], by, None, op)\
                    .then_inc(mod_ok, 1)

            for c in range(CPG):
                for m in range(2):
                    dve_lo_gu(e, U, 0, c, m)
            dve_add(e, f, GROUPS - 1, range(2 * NT))
            for h in range(NH):
                dve_cut_x(e, ns[1], h)

            k = [0]

            def link(ins):
                k[0] += 1
                ins.then_inc(dve_step, 1)
                e.wait_ge(dve_step, k[0])

            def glu(s):
                g, (c, h) = s // 4, (FIRST_STEPS if s < 4 else STEPS)[s % 4]
                e.wait_ge(U.silu, s + 1)
                if s == 0:
                    e.wait_ge(h_saved, 16 * NT)
                e.tensor_tensor(ac[:, 2 * g + c, CONV_PAD + h * HALF:CONV_PAD + (h + 1) * HALF],
                                ps[:, 2 * (s % 2) + 1], tmp[:, s % 2], ALU.mult).then_inc(U.mul, 1)

            e.wait_ge(small_in, 32)
            e.tensor_copy(posf[:], posr[:]).then_inc(pos_ok, 1)
            for b in range(2):
                e.wait_ge(wl_hi, b + 1)
                part = slice(b * NZ, (b + 1) * NZ)
                e.tensor_tensor(wl[:, LO, :, part], (lata, latb)[b][:], wl[:, HI, :, part].bitcast(F32), ALU.subtract)\
                    .then_inc(wl_lo, 1)
            e.wait_ge(pos_ok, 2)
            link(e.tensor_copy(posc[:], ps[:, MISC, 0:NT]))
            e.wait_ge(h_saved, 16 * NT)
            e.tensor_copy(cw[:, :, 0:CONV_K], ps[:, MISC, 64:64 + 32 * CC].rearrange("p (c k) -> p c k", k=32)[:, :, 0:CONV_K])\
                .then_inc(cw_ok, 1)
            RH = ROPE // 2
            e.wait_ge(pads, 1)
            link(e.tensor_tensor(trig[:, 0], posc[:].unsqueeze(2).broadcast_to([P, NT, ROPE]),
                                 trig[:, 2, 0:1].broadcast_to([P, NT, ROPE]), ALU.mult))
            for h in range(2):
                part = slice(h * RH, (h + 1) * RH)
                e.tensor_scalar(trig[:, 1, :, part], trig[:, 0, :, part], 1.0 / (2 * np.pi), (0.25, 0.0)[h], ALU.mult, ALU.add)\
                    .then_inc(dve_step, 1)
                k[0] += 1
            e.wait_ge(dve_step, k[0])
            link(e.tensor_scalar(trig[:, 1], trig[:, 1], ROUND, ROUND, ALU.add, ALU.subtract))
            for part in TWO_PI:
                link(e.scalar_tensor_tensor(out=trig[:, 0], in0=trig[:, 1], scalar=-part, in1=trig[:, 0], op0=ALU.mult,
                                            op1=ALU.add))
            link(e.tensor_scalar(trig[:, 0, :, 0:RH], trig[:, 0, :, 0:RH], float(np.pi / 2), None, ALU.add))
            e.tensor_scalar(trig[:, 3], trig[:, 0], PI_IN, -PI_IN, ALU.min, ALU.max).then_inc(trig_ok, 1)
            for s in range(3):
                glu(s)
            dve_lo_gu(e, U, 1, 0, 0)
            dve_lo_gu(e, U, 1, 0, 1)
            glu(3)
            dve_lo_gu(e, U, 1, 1, 0)
            dve_lo_gu(e, U, 1, 1, 1)
            e.wait_ge(cw_ok, 1)
            e.wait_ge(U.mul, 4)
            e.wait_ge(cs_ok, 1)
            dve_tap0(e, 0, conv)
            dve_tap0(e, 1, conv)
            dve_conv(e, 1, 14)
            glu(4)
            for v in range(6):
                e.wait_ge(z_hi, v + 1)
                c, h = divmod(v, 2)
                tok = slice(h * HALF, (h + 1) * HALF)
                e.tensor_tensor(CZ[LO][:, c, tok], ps[:, 4 + v % 3], CZ[HI][:, c, tok].bitcast(F32), ALU.subtract)\
                    .then_inc(z_lo, 1)
            dve_row_diag(e, 1, GM, gm_row)
            e.wait_ge(up_in[0], 16)
            for c in range(QL // P):
                w = wqr[:, c, 0:NHD * QK]
                e.tensor_scalar(w, w, vect[:, V_GQ + c:V_GQ + c + 1], None, ALU.mult).then_inc(up_scaled, 1)
            e.wait_ge(up_in[1], 16)
            e.tensor_scalar(wkr, wkr, vect[:, V_GKV:V_GKV + 1], None, ALU.mult).then_inc(up_scaled, 1)
            glu(5)
            e.wait_ge(up_hi, 1)
            e.tensor_tensor(wq[:, LO], wqr[:, :, 0:NHD * QK], wq[:, HI].bitcast(F32), ALU.subtract).then_inc(up_lo, 1)
            e.wait_ge(up_hi, 2)
            e.tensor_tensor(wkv[:, LO], wkr, wkv[:, HI].bitcast(F32), ALU.subtract).then_inc(up_lo, 1)
            dve_conv(e, 14, DT)
            glu(6)
            glu(7)
            dve_row_copy(e, 1, gm_row)
            e.wait_ge(U.mul, 8)
            e.memset(vs[:, :, :, VH:2 * VH], 1.0).then_inc(k_ones, 1)
            dve_tap0(e, 2, tap0)
            dve_tap0(e, 3, tap0)
            krs = rt[:, 3, :, 0, 0:1].rearrange("p t a -> p (t a)")
            flat = rt[:, 0:2].rearrange("p a t h d -> p (a t h d)")
            k2 = flat[:, 0:NT * ROPE].rearrange("p (t d) -> p t d", t=NT)
            link(e.tensor_tensor(k2, kr[:], kr[:], ALU.mult))
            e.tensor_reduce(krs, k2, AX_X, ALU.add)
            e.wait_ge(grot_in, 32)
            link(e.tensor_tensor(kr[:], kr[:], grot[:, 1:2].broadcast_to([P, NT, ROPE]), ALU.mult))
            cos, sin = cs[:, :, 0:RH], cs[:, :, RH:ROPE]
            part = [rt[:, 2, n].rearrange("p h d -> p (h d)")[:, 0:NT * RH].rearrange("p (t d) -> p t d", t=NT) for n in range(4)]
            x1, x2 = kr[:, :, 0:RH], kr[:, :, RH:ROPE]
            for to, a, b in ((part[0], x1, cos), (part[1], x2, sin), (part[2], x2, cos), (part[3], x1, sin)):
                link(e.tensor_tensor(to, a, b, ALU.mult))
            link(e.tensor_tensor(x1, part[0], part[1], ALU.subtract))
            e.tensor_tensor(x2, part[2], part[3], ALU.add).then_inc(rope, 1)
            e.memset(qh[:], -0.5).then_inc(qk_sum_t, 1)
            for t in range(NT):
                e.wait_ge(qk_sq, t + 1)
                sl = sq[:, t % 2]
                e.tensor_reduce(qs[:, t, 0:NHD], sl[:, 0:NHD * QK].rearrange("p (h d) -> p h d", d=QK), AX_X, ALU.add)
                e.tensor_reduce(qs[:, t, NHD:2 * NHD], sl[:, NHD * QK:NHD * (QK + NOPE)].rearrange("p (h d) -> p h d", d=NOPE),
                                AX_X, ALU.add).then_inc(qk_sum_t, 1)
            e.wait_ge(qk_sum_t, NT + 1)
            e.tensor_copy(qkT[QK:AUG, :, 1, HI], ones[QK:AUG, 0:1].unsqueeze(2).broadcast_to([1, 2, S])).then_inc(k_ones, 1)
            e.tensor_scalar(qkT[QK:AUG, :, 1, LO], ones[QK:AUG, 0:1].unsqueeze(2).broadcast_to([1, 2, S]), 0.0, None,
                            ALU.mult).then_inc(k_ones, 1)
            e.tensor_tensor(qs[:, :, NHD:2 * NHD], qs[:, :, NHD:2 * NHD],
                            krs.unsqueeze(2).broadcast_to([P, NT, NHD]), ALU.add).then_inc(qk_sum, 1)
            rot = qn[:, :, :, NOPE:QK]
            link(e.tensor_tensor(rot.rearrange("p t h d -> p (t h) d"), rot.rearrange("p t h d -> p (t h) d"),
                                 grot[:, 0:1].broadcast_to([P, NT * NHD, ROPE]), ALU.mult))
            x1, x2 = qn[:, :, :, NOPE:NOPE + RH], qn[:, :, :, NOPE + RH:QK]
            cosb = cos.unsqueeze(2).broadcast_to([P, NT, NHD, RH])
            sinb = sin.unsqueeze(2).broadcast_to([P, NT, NHD, RH])
            e.wait_ge(qk_sum, 1)
            for m, (a, b) in enumerate(((x1, cosb), (x2, sinb), (x2, cosb), (x1, sinb))):
                link(e.tensor_tensor(rt[:, m], a, b, ALU.mult))
            link(e.tensor_tensor(x1, rt[:, 0], rt[:, 1], ALU.subtract))
            e.tensor_tensor(x2, rt[:, 2], rt[:, 3], ALU.add).then_inc(rope, 1)
            e.wait_ge(rope, 2)

            for u in range(4):
                dve_head_unit(e, 0, 0, u)
            for p in range(THALF):
                dve_max(e, 0, 0, p)
            dve_max_lo(e, 0, 0)

            def unit(i, m, first, last):
                for p in range(THALF):
                    if not (last and m == NU - 1):
                        dve_max(e, i, m + 1, p)
                    if p == 3 and not (last and m == NU - 1):
                        dve_max_lo(e, i, m + 1)
                    if m % NH == 0:
                        if not (last and m // NH == 1):
                            dve_head_unit(e, *next_head(i, m), p)
                    elif p in (1, 2) and not last:
                        dve_tap(e, i * DTT + (DT + m // NH * 2 + p - 1))
                    if p == 0 and not (first and m < 2):
                        dve_pv_out(e, *at(i, m - 1))
                    if last and m == 1 and p in (1, 2):
                        dve_ln_mean(e, p - 1)
                    if last and m == 3 and p == 1:
                        dve_ln_var(e)
                    if last and (m, p) in WO_AT:
                        dve_wo_lo(e, WO_AT[m, p])
                    if last and m == 3 and p == 2:
                        dve_ln_diag(e)

            run_units(e, unit)
            dve_ln_scale(e)
            dve_pv_out(e, TURNS, -1)

            def cut_mix(t, part):
                if t == 0 and part == 0:
                    e.wait_ge(ln_act, 2 * CC)
                    e.wait_ge(s_mm, 4 * NU * TURNS)
                if t == 0 and part == 1:
                    e.wait_ge(pv_out, NU * TURNS)
                if t >= 2:
                    e.wait_ge(mix_mm, 2 * t - 2)
                dst = mixT[:, t % 2, HI, part * CC:(part + 1) * CC]
                e.tensor_copy(dst, mix_src(part, t)).then_inc(mix_hi, 1)
                e.wait_ge(mix_hi, 2 * t + part + 1)
                dst = mixT[:, t % 2, LO, part * CC:(part + 1) * CC]
                e.tensor_tensor(dst, mix_src(part, t), mixT[:, t % 2, HI, part * CC:(part + 1) * CC].bitcast(F32),
                                ALU.subtract).then_inc(mix_lo, 1)

            cut_mix(0, 0)
            dve_pv_out(e, TURNS, 0)
            cut_mix(0, 1)
            dve_wo_lo(e, KC - 1)
            for t in range(NT):
                if t + 1 < NT:
                    cut_mix(t + 1, 0)
                    cut_mix(t + 1, 1)
                for h in range(2):
                    e.wait_ge(mix_mm, 2 * t + h + 1)
                    e.wait_ge(h_back[t // THALF], 16)
                    dst = H[:, t, h * HALF:(h + 1) * HALF]
                    e.tensor_tensor(dst, ps[:, 4 + (2 * t + h) % MB], dst, ALU.add).then_inc(mix_added, 1)

            f, n = fs[1], ns[2]
            for c in range(CPG):
                for m in range(2):
                    dve_lo_gu(e, f, 0, c, m)
            for h in range(NH):
                dve_cut_x(e, n, h)
            dve_first(e, f, 2, lambda: dve_row_diag(e, 2, G2), lambda: dve_row_copy(e, 2))
            e.wait_ge(row_ok, 6)
            dve_turns(e, f, False)
            dve_add(e, f, GROUPS - 1, range(2 * NT))
            e.wait_ge(gfin_in, 16)
            for t in range(NT):
                e.wait_ge(rms_inv, FINAL + t + 1)
                e.scalar_tensor_tensor(out=H[:, t], in0=H[:, t], scalar=stat[:, 2 * NT + t:2 * NT + t + 1], in1=grow[:],
                                       op0=ALU.mult, op1=ALU.mult).then_inc(o_ok, 1)

        @block.tensor
        def _(e):
            e.wait_ge(consts, 5)
            e.wait_ge(vec_in, 16 * 9)
            e.transpose(ps[:, MISC, 0:NV], vec[0:NV], ident[0:NV, 0:NV]).then_inc(vec_tr, 1)
            e.wait_ge(vec_ok, 2)
            for v in range(2):
                pe_ada_sum(e, v)
            e.wait_ge(mod_ok, 2)
            for h in range(NH):
                pe_turn(e, ns[0], h)
            f = fs[0]
            pe_gateup(e, f, ns[0], 0, first=True, after={
                1: lambda: pe_ada_sum(e, G1),
                2: lambda: pe_row(e, 0)})
            e.wait_ge(row_ok, 2)
            pe_ada_sum(e, SHM)
            pe_turns(e, f, ns[0], True)
            pe_down(e, f, GROUPS - 1, 0, range(2 * NT))

            n = ns[1]
            pe_turn(e, n, 0)
            pe_turn(e, n, 1)

            def small_turns():
                e.wait_ge(n.modulated, 2 * KC)
                e.wait_ge(small_in, 32)
                e.wait_ge(pos_ok, 1)
                for c in range(CC):
                    e.transpose(ps[:, MISC, 64 + 32 * c:64 + 32 * c + CONV_K], cwr[0:CONV_K, c * P:(c + 1) * P],
                                ident[0:CONV_K, 0:CONV_K])
                e.transpose(ps[:, MISC, 0:NT], posf[:], ident[0:NT, 0:NT]).then_inc(pos_ok, 1)

            small_turns()
            pe_gateup(e, U, n, 0, first=True)
            e.wait_ge(wl_lo, 2)
            for t in range(NT):
                if t >= 3:
                    e.wait_ge(z_sq, 2 * (t - 2))
                k = 0
                for kc in range(KC):
                    for wx, xx in PASSES:
                        mm = e.matmul(ps[:, 4 + t % 3, 0:W_IN_L], X[xx][:, kc, t * P:(t + 1) * P], wl[:, wx, kc],
                                      start=(k == 0), stop=(k == 3 * KC - 1))
                        k += 1
                mm.then_inc(lat_mm, 1)

            def turn_latents():
                e.wait_ge(z_sq, 2 * NT)
                for v in range(6):
                    c, h = divmod(v, 2)
                    if v >= 3:
                        e.wait_ge(z_lo, v - 2)
                    for k in range(THALF):
                        mm = e.transpose(ps[:, 4 + v % 3, k * P:(k + 1) * P], zz[:, h * THALF + k, c * P:(c + 1) * P],
                                         ident[:])
                    mm.then_inc(z_turned, 1)

            pe_gateup(e, U, n, 1, after={0: turn_latents})
            e.wait_ge(z_lo, 6)
            pe_row(e, 1, gm_row)
            e.wait_ge(up_lo, 2)
            e.wait_ge(U.mul, 8)
            for t in range(NT):
                b = 4 * (t % 2)
                if t == 1:
                    e.wait_ge(row_ok, 4)
                if t >= 2:
                    e.wait_ge(up_out, 2 * t - 2)
                tok = slice(t * P, (t + 1) * P)
                for h in range(2):
                    k = 0
                    for c in range(QL // P):
                        for wx, xx in PASSES:
                            e.matmul(ps[:, b + h, 0:NHD // 2 * QK], CZ[xx][:, c, tok],
                                     wq[:, wx, c, h * (NHD // 2 * QK):(h + 1) * (NHD // 2 * QK)], start=(k == 0),
                                     stop=(k == 3 * (QL // P) - 1))
                            k += 1
                for h in range(2):
                    for k, (wx, xx) in enumerate(PASSES):
                        mm = e.matmul(ps[:, b + 2 + h], CZ[xx][:, QL // P, tok], wkv[:, wx, h * HALF:(h + 1) * HALF],
                                      start=(k == 0), stop=(k == 2))
                mm.then_inc(up_mm, 1)

            e.wait_ge(up_out, 2 * NT)
            for u in range(4):
                pe_turn_head(e, 0, 0, u, True)
            for p in range(THALF):
                pe_max(e, 0, 0, p)
            pe_max_row(e, 0, 0, True)
            e.wait_ge(k_ones, 3)

            def unit(i, m, first, last):
                for p in range(THALF):
                    if m % NH == 0 and not (last and m // NH == 1):
                        pe_turn_head(e, *next_head(i, m), p)
                    if not (last and m == NU - 1):
                        pe_max(e, i, m + 1, p)
                    pe_scores(e, i, m, p)
                    if p == THALF - 1 and not (last and m == NU - 1):
                        pe_max_row(e, i, m + 1)
                    if last and m == 1 and p in (1, 2):
                        pe_ln_mean(e, p - 1)
                    if last and m == 3 and p == 1:
                        pe_ln_var(e)
                    if not (first and m == 0):
                        pe_pv(e, i, m, p)

            run_units(e, unit)
            for p in range(THALF):
                if p == 1:
                    pe_ln_rstd(e)
                pe_pv(e, TURNS, 0, p)
            for t in range(NT):
                for h in range(2):
                    m = 2 * t + h
                    if m >= MB:
                        e.wait_ge(mix_added, m - MB + 1)
                    elif m == 2:
                        e.wait_ge(pv_copied, NU * TURNS)
                    k = 0
                    for c in range(KC):
                        if h == 0 and c % CC == 0:
                            e.wait_ge(mix_lo, 2 * t + 1 + c // CC)
                        if m == 0 and c in (0, KC - 1):
                            e.wait_ge(wo_lo, KC - 1 if c == 0 else KC)
                        for wx, xx in PASSES:
                            mm = e.matmul(ps[:, 4 + m % MB], mixT[:, t % 2, xx, c], wo[:, c, wx, h * HALF:(h + 1) * HALF],
                                          start=(k == 0), stop=(k == 3 * KC - 1))
                            k += 1
                    mm.then_inc(mix_mm, 1)
            f, n = fs[1], ns[2]
            pe_turn(e, n, 0)
            pe_turn(e, n, 1)
            pe_gateup(e, f, n, 0, first=True, after={2: lambda: pe_row(e, 2)})
            pe_turns(e, f, n, False)
            pe_down(e, f, GROUPS - 1, 0, range(2 * NT))


_INS = ["x", "c", "positions", "w_ada", "b_ada", "ffn1_wg", "ffn1_wu", "ffn1_wd", "w_in", "g_q_lat", "g_kv_lat",
        "w_q_up", "w_kv_up", "g_q_head", "g_k_head", "conv_w", "conv_b", "g_conv_ln", "b_conv_ln", "w_out",
        "ffn2_wg", "ffn2_wu", "ffn2_wd", "g_final"]


def kernel(**inputs):
    import concourse.bacc as bacc
    from concourse.bass_utils import run_bass_kernel_spmd as run

    nc = bacc.Bacc("TRN2", target_bir_lowering=False, num_devices=1, dynamic_dma_scratch_size=1024)
    arrays, A = {}, {}
    for name in _INS:
        a = np.ascontiguousarray(inputs[name])
        arrays[f"in_{name}"] = a
        A[name] = nc.dram_tensor(f"in_{name}", a.shape, mybir.dt.from_np(a.dtype), kind="ExternalInput").ap()
    out = nc.dram_tensor("out", inputs["x"].shape, F32, kind="ExternalOutput").ap()
    build(nc, A, out)
    r = run(nc, [arrays], core_ids=[0])
    return r.results[0]["out"]
```

```python
from contextlib import ExitStack

import numpy as np

import concourse.bass as bass
from concourse import mybir
from concourse.alu_op_type import AluOpType as ALU

ACT = mybir.ActivationFunctionType
AX_X = mybir.AxisListType.X
F32 = mybir.dt.float32
F32R = mybir.dt.float32r
I32 = mybir.dt.int32

P = 128
HALF = 512
EPS = 1e-6

HI, LO = 0, 1
PASSES = ((HI, HI), (HI, LO), (LO, HI))


def build(nc, A, out):
    D = A["x"].shape[2]
    S = A["x"].shape[1]
    FF = A["ffn1_wg"].shape[2]
    KC = D // P
    NT = S // P
    NH = S // HALF
    THALF = NT // NH
    CPG = 2
    GROUPS = FF // (CPG * P)
    GW = CPG * P
    CH = A["conv_b"].shape[1]
    CONV_K = A["conv_w"].shape[1]
    QL, KVL = A["g_q_lat"].shape[1], A["g_kv_lat"].shape[1]
    QK = A["g_q_head"].shape[1]
    NHD = A["w_q_up"].shape[2] // QK
    VH = (D - CH) // NHD
    NOPE = A["w_kv_up"].shape[2] // NHD - VH
    ROPE = QK - NOPE
    W_IN_L = QL + KVL + ROPE
    N_MOD = A["w_ada"].shape[2] // D
    SH1, S1, G1, SHM, SMX, GM, SH2, S2, G2 = range(N_MOD)

    x_d = A["x"][0].rearrange("(t p) d -> p t d", p=P)
    out_d = out[0].rearrange("(t p) d -> p t d", p=P)
    ada_d = A["w_ada"][0].rearrange("(k p) n -> p k n", p=P)
    ffn_w = []
    for n in (1, 2):
        ffn_w.append(tuple(A[f"ffn{n}_{w}"][0].rearrange("(k p) n -> p k n", p=P) for w in ("wg", "wu", "wd")))

    win_d = A["w_in"][0].rearrange("(k p) n -> p k n", p=P)
    glu_w = (win_d[:, :, CH:2 * CH], win_d[:, :, 0:CH])
    CONV_PAD = CONV_K // 2
    INV_FREQ = [float(np.float32(1) / np.float32(np.float32(10000.0) ** np.float32(j / ROPE))) for j in range(0, ROPE, 2)]
    ROUND = 12582912.0
    TWO_PI = (6.28125, 0.0019354820251464844, 2 * np.pi - 6.28125 - 0.0019354820251464844)
    PI_IN = 3.1415925

    with ExitStack() as ctx:
        def sem(name):
            return ctx.enter_context(nc.semaphore(name))

        def region(size, *variants):
            made = []
            for v in variants:
                with ExitStack() as inner:
                    used = 0
                    for name, shape, dt in v:
                        used += int(np.prod(shape[1:])) * 4
                        made.append(inner.enter_context(nc.sbuf_tensor(name, shape, dt)))
                    assert used <= size, (v, used, size)
            ctx.enter_context(nc.sbuf_tensor(f"region_{made[0].name}", [P, size // 4], F32))
            return made

        def sb(name, shape, dt=F32):
            return ctx.enter_context(nc.sbuf_tensor(name, shape, dt))

        KB = 1024
        ident = sb("ident", [P, P])
        ones = sb("ones", [P, P])
        CC = CH // P
        V_BADA, V_C = 0, N_MOD * KC
        V_CB = V_C + KC
        V_LG, V_LB = V_CB + CC, V_CB + 2 * CC
        V_GQ, V_GKV = V_CB + 3 * CC, V_CB + 3 * CC + QL // P
        NV = V_GKV + KVL // P
        vect = sb("vect", [P, NV])
        silu_c = sb("silu_c", [P, KC])
        modc = sb("modc", [P, N_MOD * KC])
        stat = sb("stat", [P, 4 * NT])
        zstat = sb("zstat", [P, 6 * NT])
        mhalf = sb("mhalf", [P, 2 * NT])
        gains = sb("gains", [P, 2])
        negmax = sb("negmax", [P, 2, THALF])
        NZ = W_IN_L // 2
        ACW = S + CONV_K + 1
        H, ac, wq, kr, cs, cw, grot, rqk, _ac2, prod = region(
            32 * KB, [("H", [P, NT, D], F32)],
            [("ac", [P, CC, ACW], F32), ("wq", [P, 2, QL // P, NHD * QK], F32R), ("kr", [P, NT, ROPE], F32),
             ("cs", [P, NT, ROPE], F32), ("cw", [P, CC, CONV_K + 2], F32), ("grot", [P, 2, ROPE], F32),
             ("rqk", [P, NT, 2 * NHD], F32)],
            [("_ac2", [P, CC, ACW], F32), ("prod", [P, 2, S], F32)])
        xh, xl, ada01, qn, kn, vn, vs, wo = region(
            64 * KB, [("xh", [P, KC, S], F32R), ("xl", [P, KC, S], F32R)],
            [("ada01", [P, 2, KC, D], F32)],
            [("qn", [P, NT, NHD, QK], F32), ("kn", [P, NT, NHD, NOPE], F32), ("vn", [P, NT, NHD, VH], F32),
             ("vs", [P, 2, NT, 2 * VH], F32)],
            [("wo", [P, KC, 2, D], F32R)])
        X = (xh, xl)
        W1, _w0, WDL, E0, E1, sq, rt = region(
            32 * KB, [("W1", [P, CPG, 2, 2, KC, P], F32R)],
            [("_w0", [P, 2, 2, KC, P], F32R), ("WDL", [P, CPG, 2, D], F32R)],
            [("E0", [P, NT, HALF], F32), ("E1", [P, NT, HALF], F32)],
            [("sq", [P, 2, NHD * (QK + NOPE)], F32), ("rt", [P, 4, NT, NHD, ROPE // 2], F32),
            ])
        EX = (E0, E1)
        AT, XS, wl, czh, czl, qkT, _x4, mixT = region(
            32 * KB, [("AT", [P, 2, CPG, 2, S], F32R)], [("XS", [P, NT, D], F32)],
            [("wl", [P, 2, KC, W_IN_L], F32R)],
            [("czh", [P, 3, S], F32R), ("czl", [P, 3, S], F32R)],
            [("qkT", [P, 2, 2, 2, S], F32R)],
            [("_x4", [P, NT // 2, D], F32), ("mixT", [P, 2, 2, KC, P], F32R)])
        CZ = (czh, czl)
        rawg, rawu, rawd, vec, wqr, _u2, latb, _g3, _u3, wkv, slot, qs, _s2, att, wor = region(
            24 * KB, [("rawg", [P, KC, GW], F32), ("rawu", [P, KC, GW], F32), ("rawd", [P, CPG, D], F32)],
            [("vec", [NV, P], F32)],
            [("wqr", [P, QL // P, 1024], F32), ("_u2", [P, KC, GW], F32), ("latb", [P, KC, NZ], F32)],
            [("_g3", [P, KC, GW], F32), ("_u3", [P, KC, GW], F32), ("wkv", [P, 2, NHD * 2 * NOPE], F32R)],
            [("slot", [P, 2, NT, QK], F32), ("qs", [P, NT, 2 * NHD], F32), ("_s2", [P, 384], F32), ("att", [P, CC, S], F32)],
            [("wor", [P, 2, D], F32)])
        wkr = rawu[:].rearrange("p k n -> p (k n)")[:, 0:NHD * 2 * NOPE]
        WD, cv, trig = region(16 * KB, [("WD", [P, CPG, 2, D], F32R)], [("cv", [P, CC, S], F32)],
                              [("trig", [P, 4, NT, ROPE], F32)])
        ada_raw, ada_acc, lata, cwr, posr, posf, posc, zz, pp, gm_row = region(
            12 * KB, [("ada_raw", [P, 2, D], F32), ("ada_acc", [P, D], F32)],
            [("lata", [P, KC, NZ], F32), ("cwr", [P, CH], F32), ("posr", [NT, P], I32), ("posf", [NT, P], F32),
             ("posc", [P, NT], F32)],
            [("zz", [P, NT, QL + KVL], F32)],
            [("pp", [P, 2, S], F32), ("gm_row", [P, D], F32)])
        tmp = sb("tmp", [P, 2, HALF])
        grow = sb("grow", [P, D])
        ps = ctx.enter_context(nc.psum_tensor("ps", [P, 8, HALF], F32))
        MISC = 7

        vec_in = sem("vec_in")
        x_in = [sem(f"x_in{t}") for t in range(NT)]
        first_in = [sem("first_gate_in"), sem("first_up_in")]
        ada_in = [sem(f"ada_in{n}") for n in range(2)]
        consts = sem("consts")
        vec_tr = sem("vec_tr")
        vec_ok = sem("vec_ok")
        silu_ok = sem("silu_ok")
        ada01_in = [[sem(f"ada{v}_in{k}") for k in range(KC // 2)] for v in range(2)]
        acc_used = sem("acc_used")
        col_half, col_sum = sem("col_half"), sem("col_sum")
        mod_ok = sem("mod_ok")
        ada_step = sem("ada_step")
        row_src = sem("row_src")
        row_mm = sem("row_mm")
        row_ok = sem("row_ok")
        final_out = sem("final_out")
        h_dram = nc.dram_tensor("h_saved_rows", (P, NT, D), F32).ap()

        class Sems:
            pass

        sumsq, mean_sq, rms_inv, scaled = sem("sumsq"), sem("mean_sq"), sem("rms_inv"), sem("scaled")
        turned, modulated, x_hi, x_lo = sem("turned"), sem("modulated"), sem("x_hi"), sem("x_lo")

        class Norm:
            def __init__(self, before, banks, first_slot=0):
                self.tiles, self.units = before * NT, before * NH * KC
                self.banks = banks
                self.first_slot = first_slot

            def slot(self, t):
                return (t + self.first_slot) % NT

        def gate_up_sems(n):
            g = Sems()
            g.g_in, g.u_in, g.gu_hi, g.gu_lo, g.gu_mm, g.silu, g.mul = (sem(f"{n}_{what}") for what in (
                "g_in", "u_in", "gu_hi", "gu_lo", "gu_mm", "silu", "mul"))
            return g

        def ffn_sems(n):
            g = gate_up_sems(n)
            g.d_in, g.d_scaled, g.d_hi, g.d_lo, g.a_hi, g.a_lo, g.down_mm, g.added = (sem(f"{n}_{what}") for what in (
                "d_in", "d_scaled", "d_hi", "d_lo", "a_hi", "a_lo", "down_mm", "added"))
            return g

        ns = [Norm(0, ((2, 3, 4, 5, 6), (4, 5, 6))), Norm(1, ((2, 3, 7), (4, 5, 6)), THALF), Norm(2, ((2, 3, 7), (4, 5, 6)))]
        FINAL = 3 * NT
        fs = [ffn_sems("ffn1"), ffn_sems("ffn2")]
        U = gate_up_sems("glu")
        h_saved, h_back = sem("h_saved"), [sem(f"h_back{n}") for n in range(2)]
        small_in, lat_in = sem("small_in"), [sem("lat_in0"), sem("lat_in1")]
        up_in = [sem("wq_in"), sem("wkv_in")]
        pads, pos_ok, trig_ok, cw_ok = sem("pads"), sem("pos_ok"), sem("trig_ok"), sem("cw_ok")
        wl_hi, wl_lo, lat_mm, z_sq, z_rstd = (sem(n) for n in (
            "wl_hi", "wl_lo", "lat_mm", "z_sq", "z_rstd"))
        z_turned, z_hi, z_lo = sem("z_turned"), sem("z_hi"), sem("z_lo")
        up_scaled, up_hi, up_lo, up_mm, up_out = (sem(n) for n in ("up_scaled", "up_hi", "up_lo", "up_mm", "up_out"))
        qk_sq, qk_sum_t, qk_sum, qk_rstd, rope = (sem(n) for n in ("qk_sq", "qk_sum_t", "qk_sum", "qk_rstd", "rope"))
        grot_in, dve_step, cs_ok, tap0, rot_step = sem("grot_in"), sem("dve_step"), sem("cs_ok"), sem("tap0"), sem("rot_step")
        conv = sem("conv")
        prod_ok, conv_add = sem("prod_ok"), sem("conv_add")
        slot_q, slot_k, k_ones = sem("slot_q"), sem("slot_k"), sem("k_ones")
        qk_turned, qk_y, qk_hi, qk_lo = sem("qk_turned"), sem("qk_y"), sem("qk_hi"), sem("qk_lo")
        max_mm, s_max, m_row, m_hi, m_lo = (sem(n) for n in ("max_mm", "s_max", "m_row", "m_hi", "m_lo"))
        s_mm, s_exp, pv_mm, pv_rec, pv_out = (sem(n) for n in ("s_mm", "s_exp", "pv_mm", "pv_rec", "pv_out"))
        v_ok, pv_copied = sem("v_ok"), sem("pv_copied")
        ln_mean, ln_mm, ln_act, ln_pool, ln_dve = (sem(n) for n in ("ln_mean", "ln_mm", "ln_act", "ln_pool", "ln_dve"))
        wo_in, wo_scaled, wo_hi, wo_lo = [sem("wo_in0"), sem("wo_in1")], sem("wo_scaled"), sem("wo_hi"), sem("wo_lo")
        mix_hi, mix_lo, mix_mm, mix_added = sem("mix_hi"), sem("mix_lo"), sem("mix_mm"), sem("mix_added")
        gfin_in, o_ok = sem("gfin_in"), sem("o_ok")

        def sp_load_gu(e, f, w, g):
            if not (isinstance(g, int) and g == 0):
                e.wait_ge(f.gu_lo, g * (2 * CPG))
            e.dma_start(rawg[:], w[0][:, :, bass.ds(g * GW, GW)]).then_inc(f.g_in, 16)
            e.dma_start(rawu[:], w[1][:, :, bass.ds(g * GW, GW)]).then_inc(f.u_in, 16)

        def sp_load_d(e, f, w, g):
            if not (isinstance(g, int) and g == 0):
                e.wait_ge(f.d_lo, g * CPG)
            e.dma_start(rawd[:], w[2][:, bass.ds(g * CPG, CPG), :]).then_inc(f.d_in, 16)

        def act_hi_gu(e, f, g, c, gate_free, ms=(0, 1), arrived=None):
            for m in ms:
                raw = (rawg, rawu)[m]
                e.wait_ge((arrived or (f.g_in, f.u_in))[m], g * 16 + 16)
                if m == 0 and gate_free is not None:
                    e.wait_ge(f.gu_mm, gate_free)
                e.activation(W1[:, c, m, HI], raw[:, :, c * P:(c + 1) * P], ACT.Copy).then_inc(f.gu_hi, 1)

        def dve_lo_gu(e, f, g, c, m):
            raw = (rawg, rawu)[m]
            e.wait_ge(f.gu_hi, g * (2 * CPG) + (2 * c + m + 1))
            e.tensor_tensor(W1[:, c, m, LO], raw[:, :, c * P:(c + 1) * P], W1[:, c, m, HI].bitcast(F32),
                            ALU.subtract).then_inc(f.gu_lo, 1)

        def dve_scale_d(e, f, g):
            e.wait_ge(f.d_in, g * 16 + 16)
            for c in range(CPG):
                e.scalar_tensor_tensor(out=rawd[:, c], in0=rawd[:, c], scalar=0.5, in1=grow[:], op0=ALU.mult,
                                       op1=ALU.mult).then_inc(f.d_scaled, 1)

        def act_hi_d(e, f, g, wd=WD):
            for c in range(CPG):
                e.wait_ge(f.d_scaled, g * CPG + c + 1)
                e.activation(wd[:, c, HI], rawd[:, c], ACT.Copy).then_inc(f.d_hi, 1)

        def dve_lo_d(e, f, g, wd=WD, cs=range(CPG)):
            for c in cs:
                e.wait_ge(f.d_hi, g * CPG + c + 1)
                e.tensor_tensor(wd[:, c, LO], rawd[:, c], wd[:, c, HI].bitcast(F32), ALU.subtract).then_inc(f.d_lo, 1)

        STEPS = [(0, 0), (0, 1), (1, 0), (1, 1)]
        FIRST_STEPS = [(0, 0), (1, 0), (0, 1), (1, 1)]

        def pe_gateup(e, f, n, g, first=False, after={}, ahead=KC):
            for s, (c, h) in enumerate(FIRST_STEPS if first else STEPS):
                if not (first and s < 2):
                    e.wait_ge(f.mul, g * 4 + s - 1)
                for m in range(2):
                    e.wait_ge(f.gu_lo, g * (2 * CPG) + (2 * c + m + 1))
                    bank = 2 * (s % 2) + m
                    k = 0
                    for kc in range(KC):
                        if first and s % 2 == 0 and m == 0:
                            e.wait_ge(x_lo, n.units + h * KC + kc + 1)
                        for wx, xx in PASSES:
                            mm = e.matmul(ps[:, bank], W1[:, c, m, wx, kc], X[xx][:, kc, h * HALF:(h + 1) * HALF],
                                          start=(k == 0), stop=(k == 3 * KC - 1))
                            k += 1
                        if first and s == 0 and m == 0 and ahead + kc < KC:
                            pe_turn_unit(e, n, ahead + kc)
                        place = m * KC + kc
                        if first and s == 1 and place % 3 < 2 and place < 3 * KC // 2:
                            pe_turn_unit(e, n, KC + place // 3 * 2 + place % 3)
                mm.then_inc(f.gu_mm, 1)
                if s in after:
                    after[s]()

        def act_silu(e, f, n, g, s):
            e.wait_ge(f.gu_mm, g * 4 + s + 1)
            if not (isinstance(g, int) and g == 0 and s < 2):
                e.wait_ge(f.a_lo, g * 4 + s - 1)
            else:
                e.wait_ge(x_lo, n.units + NH * KC)
            e.activation(tmp[:, s % 2], ps[:, 2 * (s % 2)], ACT.Silu).then_inc(f.silu, 1)

        def dve_hidden(e, f, g, par, s, steps=STEPS):
            c, h = steps[s]
            tok = slice(h * HALF, (h + 1) * HALF)
            e.wait_ge(f.silu, g * 4 + s + 1)
            e.tensor_tensor(tmp[:, s % 2], ps[:, 2 * (s % 2) + 1], tmp[:, s % 2], ALU.mult).then_inc(f.mul, 1)
            e.wait_ge(f.mul, g * 4 + s + 1)
            e.tensor_copy(AT[:, par, c, HI, tok], tmp[:, s % 2]).then_inc(f.a_hi, 1)
            e.wait_ge(f.a_hi, g * 4 + s + 1)
            e.tensor_tensor(AT[:, par, c, LO, tok], tmp[:, s % 2], AT[:, par, c, HI, tok].bitcast(F32),
                            ALU.subtract).then_inc(f.a_lo, 1)

        DB = 3

        def pe_down(e, f, g, par, ks, wd=WD):
            for k in ks:
                t, h = divmod(k, 2)
                if k == 0:
                    e.wait_ge(f.a_lo, g * 4 + 4)
                    e.wait_ge(f.d_lo, g * CPG + CPG)
                    if wd is WDL:
                        e.wait_ge(f.added, g * (2 * NT))
                if k >= DB:
                    e.wait_ge(f.added, g * (2 * NT) + k - DB + 1)
                n = 0
                for c in range(CPG):
                    for wx, ax in PASSES:
                        mm = e.matmul(ps[:, 4 + k % DB], AT[:, par, c, ax, t * P:(t + 1) * P],
                                      wd[:, c, wx, h * HALF:(h + 1) * HALF], start=(n == 0), stop=(n == 3 * CPG - 1))
                        n += 1
                mm.then_inc(f.down_mm, 1)

        def dve_add(e, f, g, ks):
            for k in ks:
                t, h = divmod(k, 2)
                e.wait_ge(f.down_mm, g * (2 * NT) + k + 1)
                dst = H[:, t, h * HALF:(h + 1) * HALF]
                e.tensor_tensor(dst, ps[:, 4 + k % DB], dst, ALU.add).then_inc(f.added, 1)

        def act_square(e, n, t):
            aside = t >= THALF and n.tiles > 0
            if aside and t > THALF:
                e.wait_ge(sumsq, n.tiles + t)
            e.activation(grow[:] if aside else XS[:, n.slot(t)], H[:, t], ACT.Square, accum_out=stat[:, t:t + 1])\
                .then_inc(sumsq, 1)

        def act_scale_row(e, n, t):
            e.wait_ge(rms_inv, n.tiles + t + 1)
            e.activation(XS[:, n.slot(t)], H[:, t], ACT.Copy, scale=stat[:, 2 * NT + t:2 * NT + t + 1]).then_inc(scaled, 1)

        def act_norm(e, n, shift, scale, ready, before_unit, before_rows):
            for t in range(THALF):
                ready(t)
                act_square(e, n, t)
                if t >= 1:
                    act_scale_row(e, n, t - 1)
            act_scale_row(e, n, THALF - 1)
            for u in range(KC):
                before_unit(u)
                act_modulate(e, n, shift, scale, u)
                if u % 2 == 1:
                    ready(THALF + u // 2)
                    act_square(e, n, THALF + u // 2)
            before_rows()
            for t in range(THALF, NT):
                act_scale_row(e, n, t)
            for u in range(KC, 2 * KC):
                act_modulate(e, n, shift, scale, u)

        def pool_rstd(e, base):
            for t in range(NT):
                e.wait_ge(sumsq, base + t + 1)
                e.tensor_scalar(stat[:, NT + t:NT + t + 1], stat[:, t:t + 1], 1.0 / D, EPS, ALU.mult, ALU.add)\
                    .then_inc(mean_sq, 1)
                e.wait_ge(mean_sq, base + t + 1)
                e.tensor_tensor(stat[:, 2 * NT + t:2 * NT + t + 1], stat[:, NT + t:NT + t + 1], mhalf[:, t:t + 1],
                                ALU.pow).then_inc(rms_inv, 1)

        def pe_turn_unit(e, n, u):
            h, kc = divmod(u, KC)
            banks = n.banks[h]
            if kc == 0:
                e.wait_ge(scaled, n.tiles + THALF * (h + 1))
            if kc >= len(banks):
                e.wait_ge(modulated, n.units + u - len(banks) + 1)
            for j in range(THALF):
                mm = e.transpose(ps[:, banks[kc % len(banks)], j * P:(j + 1) * P],
                                 XS[:, n.slot(h * THALF + j), kc * P:(kc + 1) * P], ident[:])
            mm.then_inc(turned, 1)

        def act_modulate(e, n, shift, scale, u):
            h, kc = divmod(u, KC)
            e.wait_ge(turned, n.units + u + 1)
            if u >= 2:
                e.wait_ge(x_lo, n.units + u - 1)
            e.activation(tmp[:, u % 2], ps[:, n.banks[h][kc % len(n.banks[h])]], ACT.Identity,
                         bias=modc[:, shift * KC + kc:shift * KC + kc + 1],
                         scale=modc[:, scale * KC + kc:scale * KC + kc + 1]).then_inc(modulated, 1)

        def dve_cut_x(e, n, units):
            for u in units:
                h, kc = divmod(u, KC)
                tok = slice(h * HALF, (h + 1) * HALF)
                e.wait_ge(modulated, n.units + u + 1)
                e.tensor_copy(xh[:, kc, tok], tmp[:, u % 2]).then_inc(x_hi, 1)
                e.wait_ge(x_hi, n.units + u + 1)
                e.tensor_tensor(xl[:, kc, tok], tmp[:, u % 2], xh[:, kc, tok].bitcast(F32), ALU.subtract)\
                    .then_inc(x_lo, 1)

        def sp_ada_piece(e, v, kc):
            j = (v - 2) * KC + kc
            if not (isinstance(v, int) and v == 2 and kc < 2):
                e.wait_ge(ada_step, v * KC + kc - 1)
            e.dma_start(ada_raw[:, kc % 2], ada_d[:, kc, bass.ds(v * D, D)]).then_inc(ada_in[kc % 2], 16)

        def dve_ada_piece(e, v, kc, src=None):
            if src is None:
                src = ada_raw[:, kc % 2]
                e.wait_ge(ada_in[kc % 2], (v - 2) * (16 * KC // 2) + (kc // 2) * 16 + 16)
            if kc == 0:
                if not isinstance(v, int) or v > SHM:
                    e.wait_ge(mod_ok, v - 1)
                elif v == SHM:
                    e.wait_ge(col_half, 2)
                elif v > 0:
                    e.wait_ge(acc_used, v)
                e.tensor_scalar(ada_acc[:], src, silu_c[:, kc:kc + 1], None, ALU.mult).then_inc(ada_step, 1)
            else:
                e.wait_ge(ada_step, v * KC + kc)
                e.scalar_tensor_tensor(out=ada_acc[:], in0=src, scalar=silu_c[:, kc:kc + 1], in1=ada_acc[:],
                                       op0=ALU.mult, op1=ALU.add).then_inc(ada_step, 1)

        def pe_ada_sum(e, v):
            e.wait_ge(ada_step, v * KC + KC)
            if not (isinstance(v, int) and v == 0):
                e.wait_ge(mod_ok, v)
            for j in range(KC):
                mm = e.matmul(ps[:, MISC, j:j + 1], ada_acc[:, j * P:(j + 1) * P], ones[:, 0:1], start=True, stop=True)
            mm.then_inc(acc_used, 1)

        def dve_ada_column(e, v):
            e.wait_ge(acc_used, v + 1)
            cols = slice(v * KC, (v + 1) * KC)
            if v == S1:
                e.scalar_tensor_tensor(out=modc[:, cols], in0=ps[:, MISC, 0:KC], scalar=1.0, in1=vect[:, cols],
                                       op0=ALU.add, op1=ALU.add).then_inc(mod_ok, 1)
            else:
                e.tensor_tensor(modc[:, cols], ps[:, MISC, 0:KC], vect[:, cols], ALU.add).then_inc(mod_ok, 1)

        def pe_ada_half(e, v, h):
            if h == 0:
                e.wait_ge(ada_step, v * KC + KC)
            if isinstance(v, int) and v == G1 and h == 0:
                e.wait_ge(mod_ok, 2)
            else:
                e.wait_ge(col_half, v * 2 + (h - 4))
            e.matmul(ps[:, MISC], ones[:], ada_acc[:, h * HALF:(h + 1) * HALF], start=True, stop=True).then_inc(acc_used, 1)

        def dve_ada_half(e, v, h):
            e.wait_ge(acc_used, v * 2 + (h - 1))
            part = ada_acc[:, h * HALF:(h + 1) * HALF].rearrange("p (k j) -> p k j", j=P)
            e.tensor_tensor(part, ps[:, MISC].rearrange("p (k j) -> p k j", j=P),
                            ident[:].unsqueeze(1).broadcast_to([P, KC // 2, P]), ALU.mult).then_inc(col_half, 1)
            e.wait_ge(col_half, v * 2 + (h - 3))
            e.tensor_reduce(modc[:, bass.ds(v * KC + h * (KC // 2), KC // 2)], part, AX_X, ALU.add).then_inc(col_sum, 1)
            if h == 1:
                e.wait_ge(col_sum, v * 2 - 4)
                cols = bass.ds(v * KC, KC)
                e.tensor_tensor(modc[:, cols], modc[:, cols], vect[:, cols], ALU.add).then_inc(mod_ok, 1)

        def dve_gate1_row(e, h):
            e.wait_ge(acc_used, 2 * G1 + h - 1)
            half = grow[:, h * HALF:(h + 1) * HALF]
            e.tensor_tensor(half, ps[:, MISC], half, ALU.add).then_inc(col_half, 1)

        def dve_row_diag(e, v, row=grow):
            e.tensor_tensor(row[:].rearrange("p (k j) -> p k j", k=KC), ident[:].unsqueeze(1).broadcast_to([P, KC, P]),
                            modc[:, v * KC:(v + 1) * KC].unsqueeze(2).broadcast_to([P, KC, P]), ALU.mult).then_inc(row_src, 1)

        ROW_BANKS = (MISC, 4)

        def pe_row(e, r, row=grow):
            e.wait_ge(row_src, r + 1)
            for h in range(2):
                mm = e.matmul(ps[:, ROW_BANKS[h]], ones[:], row[:, h * HALF:(h + 1) * HALF], start=True, stop=True)
            mm.then_inc(row_mm, 1)

        def dve_row_copy(e, r, row=grow):
            e.wait_ge(row_mm, r + 1)
            for h in range(2):
                e.tensor_copy(row[:, h * HALF:(h + 1) * HALF], ps[:, ROW_BANKS[h]]).then_inc(row_ok, 1)

        LAST = (GROUPS - 1) // 2 - 1

        def run_turns(e, turn):
            turn(0, False)
            with e.Fori(1, LAST) as i:
                turn(i, False)
            turn(LAST, True)

        def ada_pieces(i, j):
            if isinstance(i, int) and i == 0:
                return [((SHM, SMX)[j - 1], kc) for kc in range(KC)]
            return [(i + SMX, kc) for kc in range(KC // 2 * (j - 1), KC // 2 * j)]

        def sp_ffn(e, f, w, ada):
            def turn(i, last):
                for j in (1, 2):
                    g = i * 2 + j
                    if not (last and j == 2):
                        sp_load_gu(e, f, w, g + 1)
                    sp_load_d(e, f, w, g)
                    for v, kc in ada_pieces(i, j) if ada else ():
                        sp_ada_piece(e, v, kc)

            run_turns(e, turn)

        def act_ffn(e, f, n):
            def period(g, first, last):
                if not first:
                    act_hi_d(e, f, g - 1)
                act_silu(e, f, n, g, 0)
                act_silu(e, f, n, g, 1)
                if not last and not first:
                    act_hi_gu(e, f, g + 1, 0, g * 4 + 2)
                act_silu(e, f, n, g, 2)
                if first:
                    act_hi_gu(e, f, g + 1, 0, g * 4 + 3)
                act_silu(e, f, n, g, 3)
                if last:
                    act_hi_d(e, f, g, WDL)
                else:
                    act_hi_gu(e, f, g + 1, 1, g * 4 + 4)

            period(0, True, False)

            def turn(i, last):
                period(i * 2 + 1, False, False)
                period(i * 2 + 2, False, last)

            run_turns(e, turn)

        def dve_period(e, f, g, par, last, pieces, made):
            def some(k):
                for v, kc in pieces[len(pieces) * k // 4:len(pieces) * (k + 1) // 4]:
                    dve_ada_piece(e, v, kc)

            dve_scale_d(e, f, g - 1)
            dve_lo_d(e, f, g - 1)
            dve_hidden(e, f, g, par, 0)
            some(0)
            dve_hidden(e, f, g, par, 1)
            if not last:
                dve_lo_gu(e, f, g + 1, 0, 0)
                dve_lo_gu(e, f, g + 1, 0, 1)
            some(1)
            dve_hidden(e, f, g, par, 2)
            some(2)
            if last:
                dve_scale_d(e, f, g)
            some(3)
            dve_hidden(e, f, g, par, 3)
            if made is not None:
                dve_ada_half(e, made, 0)
            for c in range(CPG):
                dve_add(e, f, g - 1, range(4 * c, 4 * c + 4))
                if last:
                    dve_lo_d(e, f, g, WDL, (c,))
                else:
                    dve_lo_gu(e, f, g + 1, 1, c)
            dve_add(e, f, g - 1, range(4 * CPG, 2 * NT))
            if made is not None:
                dve_ada_half(e, made, 1)

        def dve_first(e, f):
            for s in range(3):
                dve_hidden(e, f, 0, 0, s, FIRST_STEPS)
                if f is fs[0] and s < 2:
                    for kc in range(2 + 3 * s, 5 + 3 * s):
                        dve_ada_piece(e, G1, kc)
            for m in range(2):
                dve_lo_gu(e, f, 1, 0, m)
            if f is fs[0]:
                e.wait_ge(vec_in, 16 * 10)
                dve_gate1_row(e, 0)
            else:
                dve_row_diag(e, G2)
            dve_hidden(e, f, 0, 0, 3, FIRST_STEPS)
            if f is fs[0]:
                dve_gate1_row(e, 1)
            else:
                dve_row_copy(e, 1)
            for m in range(2):
                dve_lo_gu(e, f, 1, 1, m)
            if f is fs[0]:
                e.wait_ge(col_half, 2)
            else:
                e.wait_ge(row_ok, 4)

        def vector_made(i, j):
            if isinstance(i, int) and i == 0:
                return (SHM, SMX)[j - 1]
            return i + SMX if j == 2 else None

        def dve_turns(e, f, ada):
            def turn(i, last):
                for j, par in ((1, 1), (2, 0)):
                    dve_period(e, f, i * 2 + j, par, last and j == 2, ada_pieces(i, j) if ada else [],
                               vector_made(i, j) if ada else None)

            run_turns(e, turn)

        def pe_turns(e, f, n, ada):
            def turn(i, last):
                for j, par in ((1, 1), (2, 0)):
                    g = i * 2 + j
                    pe_gateup(e, f, n, g)
                    made = vector_made(i, j) if ada else None
                    if made is not None:
                        pe_ada_half(e, made, 0)
                    pe_down(e, f, g - 1, 1 - par, range(2 * NT))
                    if made is not None:
                        pe_ada_half(e, made, 1)

            run_turns(e, turn)

        NU = 2 * NH
        TURNS = NHD // 2
        AUG = QK + 1

        def at(i, m):
            return (i + m // NU, m % NU)

        def pe_max(e, i, m, p, start=False):
            i, m = at(i, m)
            hp, h = divmod(m, NH)
            t = h * THALF + p
            if p == 0:
                e.wait_ge(qk_lo, i * 8 + (hp * 4 + 3 + h))
            if not start:
                e.wait_ge(s_max, i * 16 + (m * 4 + p))
            elif p >= 2:
                e.wait_ge(s_max, p - 1)
            for b in range(NH):
                mm = e.matmul(ps[:, b + (2 * (p % 2) if start else 0)], qkT[0:QK, hp, 0, HI, t * P:(t + 1) * P],
                              qkT[0:QK, hp, 1, HI, b * HALF:(b + 1) * HALF], start=True, stop=True)
            mm.then_inc(max_mm, 1)

        def dve_max(e, i, m, p, start=False):
            i, m = at(i, m)
            e.wait_ge(max_mm, i * 16 + (m * 4 + p + 1))
            b = 2 * (p % 2) if start else 0
            e.tensor_reduce(negmax[:, m % 2, p:p + 1], ps[:, b:b + NH].rearrange("p b k -> p (b k)"), AX_X, ALU.max,
                            negate=True).then_inc(s_max, 1)

        def pe_max_row(e, i, m, first=False):
            i, m = at(i, m)
            e.wait_ge(s_max, i * 16 + (m * 4 + 4))
            if not first:
                e.wait_ge(m_lo, i * 4 + m)
            ahead = m % NH == 1 and not (isinstance(i, int) and i == TURNS - 1 and m // NH == 1)
            e.wait_ge(qk_y, i * 8 + (4 * (m // NH) + (8 if ahead else 4)))
            if isinstance(i, int) and (i, m) == (TURNS - 1, 2):
                e.wait_ge(ln_mean, 2 * CC)
            for p in range(THALF):
                mm = e.matmul(ps[0:1, MISC, p * P:(p + 1) * P], negmax[:, m % 2, p:p + 1], ident[:], start=True, stop=True)
            mm.then_inc(m_row, 1)

        def max_place(m, a):
            hp, h = divmod(m, NH)
            return qkT[QK:AUG, hp, 0, a, h * HALF:(h + 1) * HALF]

        def act_max_hi(e, i, m):
            i, m = at(i, m)
            e.wait_ge(m_row, i * 4 + (m + 1))
            e.activation(max_place(m, HI), ps[0:1, MISC], ACT.Copy).then_inc(m_hi, 1)

        def dve_max_lo(e, i, m):
            i, m = at(i, m)
            e.wait_ge(m_hi, i * 4 + (m + 1))
            e.tensor_tensor(max_place(m, LO), ps[0:1, MISC], max_place(m, HI).bitcast(F32), ALU.subtract).then_inc(m_lo, 1)

        def pe_scores(e, i, m, p):
            hp, h = divmod(m, NH)
            if p == 0:
                e.wait_ge(m_lo, i * 4 + (m + 1))
            if not (isinstance(i, int) and i == 0 and m == 0 and p < 2):
                e.wait_ge(s_exp, i * 16 + (m * 4 + p - 1))
            for b in range(2):
                kt = 2 * p + b
                for k, (x, y) in enumerate(PASSES):
                    mm = e.matmul(ps[:, 2 + 2 * (p % 2) + b], qkT[0:AUG, hp, 1, x, kt * P:(kt + 1) * P],
                                  qkT[0:AUG, hp, 0, y, h * HALF:(h + 1) * HALF], start=(k == 0), stop=(k == 2))
            mm.then_inc(s_mm, 1)

        def act_exp(e, i, m, p):
            e.wait_ge(s_mm, i * 16 + (m * 4 + p + 1))
            if p == 0 and not (isinstance(i, int) and i == 0 and m < 2):
                e.wait_ge(pv_mm, i * 4 + (m - 1))
            b = 2 + 2 * (p % 2)
            e.activation(EX[m % 2][:, 2 * p:2 * p + 2], ps[:, b:b + 2], ACT.Exp).then_inc(s_exp, 1)

        def pe_pv(e, i, m, p):
            hp = (m - 1) % NU // NH
            if p == 0:
                e.wait_ge(s_exp, i * 16 + m * 4)
                if m % NH == 1:
                    e.wait_ge(v_ok, i * 2 + (hp + 1))
                if not (isinstance(i, int) and i == 0 and m == 1):
                    e.wait_ge(pv_copied, i * 4 + (m - 1))
            for kt in (2 * p, 2 * p + 1):
                mm = e.matmul(ps[:, 6], vs[:, hp, kt], EX[(m - 1) % 2][:, kt], start=(kt == 0), stop=(kt == NT - 1))
            if p == THALF - 1:
                mm.then_inc(pv_mm, 1)

        def act_pv_copy(e, i, m):
            e.wait_ge(pv_mm, i * 4 + m)
            if not (isinstance(i, int) and i == 0 and m == 1):
                e.wait_ge(pv_out, i * 4 + (m - 1))
            e.activation(grow[:, 0:HALF], ps[:, 6], ACT.Copy).then_inc(pv_copied, 1)

        def dve_pv_recip(e, i, m, third):
            if third == 0:
                e.wait_ge(pv_copied, i * 4 + m)
            a, b = ((0, 192), (192, 352), (352, HALF))[third]
            e.reciprocal(grow[0:VH, HALF + a:HALF + b], grow[VH:2 * VH, a:b]).then_inc(pv_rec, 1)

        def dve_pv_scale(e, i, m):
            hp, h = (m - 1) % NU // NH, (m - 1) % NH
            chunk = i if m >= 1 else i - 1
            e.wait_ge(pv_rec, i * 12 + 3 * m)
            dst = att[hp * VH:(hp + 1) * VH, bass.ds(chunk, 1), h * HALF:(h + 1) * HALF].rearrange("p a q -> p (a q)")
            e.tensor_tensor(dst, grow[0:VH, 0:HALF], grow[0:VH, HALF:D], ALU.mult).then_inc(pv_out, 1)

        def act_v(e, i, hp, first=False):
            hd = i * 2 + hp
            if not first:
                e.wait_ge(pv_mm, hd * 2 - 2)
            e.activation(vs[:, hp, :, 0:VH], vn[:, :, bass.ds(hd, 1), :].rearrange("p t a d -> p t (a d)"), ACT.Copy)\
                .then_inc(v_ok, 1)

        FIRST_HEAD = (0, 2, 1, 3)
        FIRST_BANKS = (3, 2, MISC, 6)

        def head_unit(n, first):
            return (FIRST_HEAD[n], FIRST_BANKS[n]) if first else (n, MISC)

        def pe_turn_head(e, i, hp, n, first=False):
            u, bank = head_unit(n, first)
            if first:
                e.wait_ge((slot_k, slot_q)[u // 2], u % 2 + 1)
            else:
                e.wait_ge((slot_k, slot_q)[u // 2], i * 2 + (hp + 2))
                e.wait_ge(qk_y, i * 8 + (hp * 4 + n))
                if n == 0:
                    e.wait_ge(m_lo, i * 4 + (hp * 2 - 1))
            for k in range(THALF):
                mm = e.transpose(ps[0:QK, bank, k * P:(k + 1) * P], slot[:, 1 - u // 2, (u % 2) * THALF + k], ident[:])
            mm.then_inc(qk_turned, 1)

        def act_head_unit(e, i, hp, n, first=False):
            u, bank = head_unit(n, first)
            e.wait_ge(qk_turned, i * 8 + (hp * 4 + n + 1))
            if not (first and n < 2):
                e.wait_ge(qk_lo, i * 8 + (hp * 4 + n - 1))
            m = 1 - u // 2
            e.activation(tmp[0:QK, n % 2], ps[0:QK, bank], ACT.Copy, scale=gains[0:QK, m:m + 1]).then_inc(qk_y, 1)

        def dve_head_unit(e, i, hp, n, first=False):
            u, _bank = head_unit(n, first)
            qk, h = 1 - u // 2, u % 2
            tok = slice(h * HALF, (h + 1) * HALF)
            e.wait_ge(qk_y, i * 8 + (hp * 4 + n + 1))
            e.tensor_copy(qkT[0:QK, hp, qk, HI, tok], tmp[0:QK, n % 2]).then_inc(qk_hi, 1)
            e.wait_ge(qk_hi, i * 8 + (hp * 4 + n + 1))
            e.tensor_tensor(qkT[0:QK, hp, qk, LO, tok], tmp[0:QK, n % 2], qkT[0:QK, hp, qk, HI, tok].bitcast(F32),
                            ALU.subtract).then_inc(qk_lo, 1)

        def pool_inv_rms(e, hd, m, tiles, count):
            r, ms = (x[:, tiles].rearrange("p t (m h) -> p t m h", m=2)[:, :, m, bass.ds(hd, 1)] for x in (rqk, qs))
            e.tensor_tensor(r, ms, mhalf[:, tiles].unsqueeze(2), ALU.pow).then_inc(qk_rstd, 1)
            e.wait_ge(qk_rstd, count)
            return r

        def pool_slot_k(e, hd, tiles, r):
            n = tiles.stop - tiles.start
            e.tensor_tensor(slot[:, 1, tiles, 0:NOPE], kn[:, tiles, bass.ds(hd, 1), :].rearrange("p t a d -> p t (a d)"),
                            r.broadcast_to([P, n, NOPE]), ALU.mult)
            return e.tensor_tensor(slot[:, 1, tiles, NOPE:QK], kr[:, tiles], r.broadcast_to([P, n, ROPE]), ALU.mult)

        def pool_slot_q(e, hd, tiles, r):
            n = tiles.stop - tiles.start
            return e.tensor_tensor(slot[:, 0, tiles], qn[:, tiles, bass.ds(hd, 1), :].rearrange("p t a d -> p t (a d)"),
                                   r.broadcast_to([P, n, QK]), ALU.mult)

        def pool_first_slots(e):
            for h in range(NH):
                tiles = slice(h * THALF, (h + 1) * THALF)
                e.wait_ge(qk_sum, h + 1)
                e.tensor_scalar(qs[:, tiles], qs[:, tiles], 1.0 / QK, EPS, ALU.mult, ALU.add).then_inc(qk_rstd, 1)
                e.wait_ge(qk_rstd, 3 * h + 1)
                e.wait_ge(rope, 1 + (h + 1) * THALF)
                pool_slot_k(e, 0, tiles, pool_inv_rms(e, 0, 1, tiles, 3 * h + 2)).then_inc(slot_k, 1)
                pool_slot_q(e, 0, tiles, pool_inv_rms(e, 0, 0, tiles, 3 * h + 3)).then_inc(slot_q, 1)

        def pool_slots(e, i, hp):
            hd = i * 2 + hp
            tiles = slice(0, NT)
            count = hd * 2 + (3 * NH - 2)
            r = pool_inv_rms(e, hd, 1, tiles, count + 1)
            e.wait_ge(qk_turned, 3 if isinstance(hd, int) and hd == 1 else hd * 4 - 2)
            pool_slot_k(e, hd, tiles, r).then_inc(slot_k, 1)
            r = pool_inv_rms(e, hd, 0, tiles, count + 2)
            e.wait_ge(qk_turned, hd * 4)
            pool_slot_q(e, hd, tiles, r).then_inc(slot_q, 1)

        CT = TURNS - 1
        TT = (CONV_K - 1) // CT

        PRODUCTS = ((2, 1, 2, 1), (0, 1, 2, 1))

        def products(m, p0, p1):
            start = m // NH * TT + m % NH * sum(PRODUCTS[0])
            return range(start + sum(PRODUCTS[m % NH][:p0]), start + sum(PRODUCTS[m % NH][:p1]))

        def act_prod(e, i, n, first):
            c, k = 2 + n % 2, 1 + n // 2
            if not (first and n < 2):
                e.wait_ge(conv_add, i * (2 * TT) + (n - 1))
            e.activation(prod[:, n % 2], ac[:, c, bass.ds(i * TT + k, S)], ACT.Copy,
                         scale=cw[:, c, bass.ds(i * TT + k, 1)]).then_inc(prod_ok, 1)

        def pool_conv(e, i, n, first):
            c = 2 + n % 2
            e.wait_ge(prod_ok, i * (2 * TT) + (n + 1))
            if not (first and n < 2):
                e.wait_ge(conv_add, i * (2 * TT) + (n - 1))
            e.tensor_tensor(cv[:, c], cv[:, c], prod[:, n % 2], ALU.add).then_inc(conv_add, 1)

        DTT = 4
        DT = CONV_K - DTT * CT

        def dve_tap(e, i, chunks=(0, 1)):
            for c in chunks:
                e.wait_ge(conv, i * 2 + (c - 1))
                e.scalar_tensor_tensor(out=cv[:, c], in0=ac[:, c, bass.ds(i, S)], scalar=cw[:, c, bass.ds(i, 1)],
                                       in1=cv[:, c], op0=ALU.mult, op1=ALU.add).then_inc(conv, 1)

        def dve_conv(e, a, b):
            with e.Fori(a, b) as i:
                dve_tap(e, i)

        def dve_tap0(e, c, count):
            e.tensor_scalar(cv[:, c], ac[:, c, 0:S], cw[:, c, 0:1], vect[:, V_CB + c:V_CB + c + 1], ALU.mult, ALU.add)\
                .then_inc(count, 1)

        squares = (prod[:, 0], prod[:, 1], pp[:, 0], pp[:, 1])

        def pool_pair_sums(e, pairs, done):
            for n, (dst, a, b) in enumerate(pairs):
                if n == 2:
                    e.wait_ge(ln_pool, done + 2)
                e.tensor_tensor(dst, a, b, ALU.add).then_inc(ln_pool, 1)

        def pe_ln_mean(e, h):
            if h == 0:
                e.wait_ge(ln_pool, 3)
                e.wait_ge(m_lo, NU * (TURNS - 1) + 2)
                e.wait_ge(qk_y, 4 * NHD)
            else:
                e.wait_ge(ln_mean, CC)
            e.matmul(ps[:, MISC], ones[:], pp[:, 0, h * HALF:(h + 1) * HALF], start=True, stop=True).then_inc(ln_mm, 1)

        def dve_ln_mean(e, h):
            e.wait_ge(ln_mm, h + 1)
            for c in range(CC):
                x = cv[:, c, h * HALF:(h + 1) * HALF]
                e.scalar_tensor_tensor(out=x, in0=ps[:, MISC], scalar=-1.0 / CH, in1=x, op0=ALU.mult, op1=ALU.add)\
                    .then_inc(ln_mean, 1)

        def act_ln_square(e, c):
            e.wait_ge(ln_mean, 2 * CC)
            e.activation(squares[c], cv[:, c], ACT.Square).then_inc(ln_act, 1)

        def pe_ln_var(e):
            e.wait_ge(ln_pool, 6)
            e.wait_ge(m_lo, NU * TURNS)
            for t in range(NT):
                mm = e.matmul(ps[:, MISC, t:t + 1], pp[:, 0, t * P:(t + 1) * P], ones[:, 0:1], start=True, stop=True)
            mm.then_inc(ln_mm, 1)

        def dve_ln_var(e):
            e.wait_ge(ln_mm, 3)
            e.tensor_scalar(stat[:, 0:NT], ps[:, MISC, 0:NT], 1.0 / CH, 1e-5, ALU.mult, ALU.add).then_inc(ln_dve, 1)

        def dve_ln_diag(e):
            e.wait_ge(ln_pool, 7)
            e.tensor_tensor(pp[:, 1].rearrange("p (k j) -> p k j", k=NT), ident[:].unsqueeze(1).broadcast_to([P, NT, P]),
                            stat[:, NT:2 * NT].unsqueeze(2).broadcast_to([P, NT, P]), ALU.mult).then_inc(ln_dve, 1)

        def pe_ln_rstd(e):
            e.wait_ge(ln_dve, 2)
            e.wait_ge(s_max, 4 * NU * TURNS)
            for h in range(2):
                mm = e.matmul(ps[:, h], ones[:], pp[:, 1, h * HALF:(h + 1) * HALF], start=True, stop=True)
            mm.then_inc(ln_mm, 1)

        def dve_ln_scale(e):
            e.wait_ge(ln_mm, 4)
            for c in range(CC):
                e.tensor_tensor(cv[:, c], cv[:, c], ps[:, 0:2].rearrange("p b n -> p (b n)"), ALU.mult).then_inc(ln_dve, 1)

        def act_ln_swish(e):
            for c in range(CC):
                e.wait_ge(ln_dve, 3 + c)
                e.activation(cv[:, c], cv[:, c], ACT.Silu, bias=vect[:, V_LB + c:V_LB + c + 1],
                             scale=vect[:, V_LG + c:V_LG + c + 1]).then_inc(ln_act, 1)

        WO_AT = {(1, 3): 0, (2, 0): 1, (2, 2): 2, (2, 3): 3, (3, 0): 4, (3, 1): 5, (3, 2): 6}

        def pool_wo_scale(e, c):
            e.wait_ge(wo_in[c % 2], 16 * (c // 2 + 1))
            e.tensor_tensor(wor[:, c % 2], wor[:, c % 2], gm_row[:], ALU.mult).then_inc(wo_scaled, 1)

        def act_wo_hi(e, c):
            e.wait_ge(wo_scaled, c + 1)
            if c == 0:
                e.wait_ge(slot_k, NHD + 1)
            if c == 5:
                e.wait_ge(v_ok, NHD)
            if c == 7:
                e.wait_ge(pv_mm, 2 * NHD)
            e.activation(wo[:, c, HI], wor[:, c % 2], ACT.Copy).then_inc(wo_hi, 1)

        def dve_wo_lo(e, c):
            e.wait_ge(wo_hi, c + 1)
            e.tensor_tensor(wo[:, c, LO], wor[:, c % 2], wo[:, c, HI].bitcast(F32), ALU.subtract).then_inc(wo_lo, 1)

        def run_units(e, unit):
            for m in range(NU):
                unit(0, m, True, False)
            with e.Fori(1, TURNS - 1) as i:
                for m in range(NU):
                    unit(i, m, False, False)
            for m in range(NU):
                unit(TURNS - 1, m, False, True)

        def next_head(i, m):
            return (i, 1) if m // NH == 0 else (i + 1, 0)

        def mix_src(part, t):
            return (cv, att)[part][:, :, t * P:(t + 1) * P]

        MB = 3

        block = ctx.enter_context(nc.Block())

        @block.sync
        def _(e):
            e.wait_ge(consts, 1)
            rows = ((A["b_ada"], V_BADA, N_MOD * KC), (A["c"], V_C, KC), (A["conv_b"], V_CB, CC), (A["g_conv_ln"], V_LG, CC),
                    (A["b_conv_ln"], V_LB, CC), (A["g_q_lat"], V_GQ, QL // P), (A["g_kv_lat"], V_GKV, KVL // P))
            e.dma_start(grow[:], A["b_ada"][:, G1 * D:(G1 + 1) * D].broadcast_to([P, D])).then_inc(vec_in, 16)
            for a, to, n in rows:
                e.dma_start(vec[to:to + n, :], a.rearrange("a (r q) -> (a r) q", q=P)).then_inc(vec_in, 16)
            for m, g in enumerate(("g_q_head", "g_k_head")):
                e.dma_start(gains[0:NOPE, m:m + 1], A[g][:, 0:NOPE].rearrange("a d -> d a")).then_inc(vec_in, 16)
            for t in range(THALF):
                e.dma_start(H[:, t], x_d[:, t]).then_inc(x_in[t], 16)
            def load_first_gu(c, m, signal):
                e.dma_start((rawg, rawu)[m][:, :, c * P:(c + 1) * P], ffn_w[0][m][:, :, c * P:(c + 1) * P]).then_inc(signal, 16)

            e.wait_ge(vec_ok, 1)
            load_first_gu(0, 0, first_in[0])
            for v in range(2):
                for k in range(KC // 2):
                    two = slice(2 * k, 2 * k + 2)
                    e.dma_start(ada01[:, v, two], ada_d[:, two, v * D:(v + 1) * D]).then_inc(ada01_in[v][k], 16)
            load_first_gu(0, 1, first_in[1])
            for t in range(THALF, NT):
                e.dma_start(H[:, t], x_d[:, t]).then_inc(x_in[t], 16)
                if t == THALF + 1:
                    load_first_gu(1, 0, fs[0].g_in)
            load_first_gu(1, 1, fs[0].u_in)
            for kc in range(2):
                sp_ada_piece(e, G1, kc)
            sp_load_gu(e, fs[0], ffn_w[0], 1)
            for kc in range(2, KC):
                sp_ada_piece(e, G1, kc)
            sp_load_d(e, fs[0], ffn_w[0], 0)
            sp_ffn(e, fs[0], ffn_w[0], True)

            e.wait_ge(fs[0].gu_lo, 2 * CPG * GROUPS)
            sp_load_gu(e, U, glu_w, 0)
            e.wait_ge(mod_ok, N_MOD - 1)
            e.dma_start(lata[:], win_d[:, :, 2 * CH:2 * CH + NZ]).then_inc(lat_in[0], 16)
            e.dma_start(cwr[0:CONV_K, :], A["conv_w"][0].rearrange("k a c -> k (a c)")).then_inc(small_in, 16)
            e.dma_start(posr[:], A["positions"].rearrange("a (t q) -> (a t) q", q=P)).then_inc(small_in, 16)
            e.wait_ge(fs[0].d_lo, CPG * GROUPS)
            e.dma_start(latb[:], win_d[:, :, 2 * CH + NZ:2 * CH + W_IN_L]).then_inc(lat_in[1], 16)
            for t in range(NT):
                e.wait_ge(fs[0].added, (GROUPS - 1) * 2 * NT + 2 * t + 2)
                e.dma_start(h_dram[:, t], H[:, t]).then_inc(h_saved, 16)
            sp_load_gu(e, U, glu_w, 1)
            e.wait_ge(h_saved, 16 * NT)
            e.wait_ge(scaled, ns[1].tiles + NT)
            for m, g in enumerate(("g_q_head", "g_k_head")):
                e.dma_start(grot[:, m], A[g][:, NOPE:QK].broadcast_to([P, ROPE])).then_inc(grot_in, 16)
            e.wait_ge(U.gu_lo, 2 * 2 * CPG)
            e.dma_start(wqr[:, :, 0:NHD * QK], A["w_q_up"][0].rearrange("(k p) n -> p k n", p=P)).then_inc(up_in[0], 16)
            e.dma_start(wkr, A["w_kv_up"][0]).then_inc(up_in[1], 16)
            e.wait_ge(qk_turned, 4 * NHD)
            for c in range(KC):
                if c >= 2:
                    e.wait_ge(wo_lo, c - 1)
                e.dma_start(wor[:, c % 2], A["w_out"][0][c * P:(c + 1) * P, :]).then_inc(wo_in[c % 2], 16)
            e.wait_ge(ln_pool, 6)
            for n in range(2):
                half = slice(n * THALF, (n + 1) * THALF)
                e.dma_start(H[:, half], h_dram[:, half]).then_inc(h_back[n], 16)
            e.wait_ge(wo_lo, KC)
            f = fs[1]
            e.dma_start(rawg[:], ffn_w[1][0][:, :, 0:GW]).then_inc(f.g_in, 16)
            e.wait_ge(mix_lo, 2 * NT)
            e.dma_start(rawu[:], ffn_w[1][1][:, :, 0:GW]).then_inc(f.u_in, 16)
            sp_load_d(e, f, ffn_w[1], 0)
            sp_load_gu(e, f, ffn_w[1], 1)
            sp_ffn(e, f, ffn_w[1], False)
            e.wait_ge(f.d_scaled, CPG * GROUPS)
            e.dma_start(grow[:], A["g_final"].broadcast_to([P, D])).then_inc(gfin_in, 16)
            for t in range(NT):
                e.wait_ge(o_ok, t + 1)
                e.dma_start(out_d[:, t], H[:, t]).then_inc(final_out, 16)
            e.wait_ge(final_out, 16 * NT)

        @block.gpsimd
        def _(e):
            e.memset(gains[:], 1.0)
            e.memset(vec[:], 0.0).then_inc(consts, 1)
            e.memset(ident[:], 0.0).then_inc(consts, 1)
            e.wait_ge(consts, 2)
            e.affine_select(out=ident[:], in_=ident[:], compare_op=ALU.not_equal, fill=1.0, base=0,
                            pattern=[[-1, P]], channel_multiplier=1).then_inc(consts, 1)
            e.memset(ones[:], 1.0).then_inc(consts, 1)
            e.memset(mhalf[:], -0.5).then_inc(consts, 1)
            e.wait_ge(consts, 5)
            pool_rstd(e, ns[0].tiles)
            pool_rstd(e, ns[1].tiles)
            e.wait_ge(scaled, ns[1].tiles + NT)
            for j in range(ROPE // 2):
                e.memset(trig[:, 2, 0, j:ROPE:ROPE // 2], INV_FREQ[j])
            e.wait_ge(h_saved, 16 * NT)
            e.memset(ac[:, :, 0:CONV_PAD], 0.0)
            e.memset(ac[:, :, CONV_PAD + S:ACW], 0.0)
            e.memset(cw[:, :, CONV_K:CONV_K + 2], 0.0).then_inc(pads, 1)
            e.wait_ge(z_sq, 2 * NT)
            e.tensor_scalar(zstat[:, 2 * NT:3 * NT], zstat[:, 0:NT], 1.0 / QL, EPS, ALU.mult, ALU.add)
            e.tensor_scalar(zstat[:, 3 * NT:4 * NT], zstat[:, NT:2 * NT], 1.0 / KVL, EPS, ALU.mult, ALU.add)\
                .then_inc(z_rstd, 1)
            e.wait_ge(z_rstd, 1)
            e.tensor_tensor(zstat[:, 4 * NT:6 * NT], zstat[:, 2 * NT:4 * NT], mhalf[:], ALU.pow).then_inc(z_rstd, 1)
            pool_first_slots(e)
            pool_slots(e, 0, 1)
            e.wait_ge(tap0, 2)

            def unit(i, m, first, last):
                if m % NH == 1 and not last:
                    pool_slots(e, i + 1, m // NH)
                if not last:
                    for n in products(m, 0, THALF):
                        pool_conv(e, i, n, first)

            run_units(e, unit)
            e.wait_ge(conv_add, 2 * (CONV_K - 1))
            e.wait_ge(conv, 2 * CONV_K)
            pool_pair_sums(e, ((pp[:, 0], cv[:, 0], cv[:, 1]), (pp[:, 1], cv[:, 2], cv[:, 3]), (pp[:, 0], pp[:, 0], pp[:, 1])), 0)
            for c in range(3):
                pool_wo_scale(e, c)
            e.wait_ge(ln_act, CC)
            pool_pair_sums(e, ((squares[0], squares[0], squares[1]), (squares[2], squares[2], squares[3]),
                               (pp[:, 0], squares[0], squares[2])), 3)
            for c in range(3, 6):
                pool_wo_scale(e, c)
            e.wait_ge(ln_dve, 1)
            e.tensor_tensor(stat[:, NT:2 * NT], stat[:, 0:NT], mhalf[:, 0:NT], ALU.pow).then_inc(ln_pool, 1)
            for c in range(6, KC):
                pool_wo_scale(e, c)
            pool_rstd(e, ns[2].tiles)
            pool_rstd(e, FINAL)

        @block.scalar
        def _(e):
            e.wait_ge(vec_ok, 2)
            e.activation(silu_c[:], vect[:, V_C:V_C + KC], ACT.Silu).then_inc(silu_ok, 1)
            f, n = fs[0], ns[0]

            def first_weights(u):
                if u == 0:
                    act_hi_gu(e, f, 0, 0, None, (0,), first_in)
                    e.wait_ge(mod_ok, 2)
                if u == 2:
                    act_hi_gu(e, f, 0, 0, None, (1,), first_in)

            act_norm(e, n, SH1, S1, lambda t: e.wait_ge(x_in[t], 16), first_weights, lambda: act_hi_gu(e, f, 0, 1, None))
            act_ffn(e, f, n)

            n = ns[1]
            act_hi_gu(e, U, 0, 0, None)

            def second_half():
                e.wait_ge(f.down_mm, 2 * NT * GROUPS)
                act_hi_gu(e, U, 0, 1, None)

            def columns_made(u):
                if u == 0:
                    e.wait_ge(mod_ok, N_MOD + 1)

            act_norm(e, n, SHM, SMX, lambda t: e.wait_ge(f.added, (GROUPS - 1) * 2 * NT + 2 * t + 2), columns_made,
                     second_half)

            def sigmoid(s):
                e.wait_ge(U.gu_mm, s + 1)
                if s >= 2:
                    e.wait_ge(U.mul, s - 1)
                else:
                    e.wait_ge(x_lo, n.units + NH * KC)
                e.activation(tmp[:, s % 2], ps[:, 2 * (s % 2)], ACT.Sigmoid).then_inc(U.silu, 1)

            for b in range(2):
                sigmoid(b)
                e.wait_ge(lat_in[b], 16)
                e.activation(wl[:, HI, :, b * NZ:(b + 1) * NZ], (lata, latb)[b][:], ACT.Copy).then_inc(wl_hi, 1)
            sigmoid(2)
            e.wait_ge(trig_ok, 1)
            e.activation(cs[:], trig[:, 3], ACT.Sin).then_inc(cs_ok, 1)
            act_hi_gu(e, U, 1, 0, 3)
            sigmoid(3)
            act_hi_gu(e, U, 1, 1, 4)
            e.wait_ge(U.mul, 4)
            for t in range(NT):
                e.wait_ge(lat_mm, t + 1)
                b = ps[:, 4 + t % 3]
                if t == 0:
                    e.wait_ge(wl_lo, 2)
                    e.wait_ge(cw_ok, 1)
                e.activation(zz[:, t], b[:, 0:QL + KVL], ACT.Copy)
                e.activation(kr[:, t], b[:, QL + KVL:W_IN_L], ACT.Copy)
                if t >= 1:
                    e.wait_ge(z_sq, 2 * t)
                e.activation(tmp[:, 0, 0:QL], b[:, 0:QL], ACT.Square, accum_out=zstat[:, t:t + 1]).then_inc(z_sq, 1)
                e.activation(tmp[:, 1, 0:KVL], b[:, QL:QL + KVL], ACT.Square, accum_out=zstat[:, NT + t:NT + t + 1])\
                    .then_inc(z_sq, 1)
            e.wait_ge(z_sq, 2 * NT)
            sigmoid(4)
            for v in range(6):
                e.wait_ge(z_turned, v + 1)
                c, h = divmod(v, 2)
                e.activation(CZ[HI][:, c, h * HALF:(h + 1) * HALF], ps[:, 4 + v % 3], ACT.Copy).then_inc(z_hi, 1)
            sigmoid(5)
            e.wait_ge(up_scaled, QL // P)
            e.activation(wq[:, HI], wqr[:, :, 0:NHD * QK], ACT.Copy).then_inc(up_hi, 1)
            e.wait_ge(up_scaled, QL // P + 1)
            e.activation(wkv[:, HI], wkr, ACT.Copy).then_inc(up_hi, 1)
            sigmoid(6)
            sigmoid(7)
            e.wait_ge(z_rstd, 2)
            e.wait_ge(U.mul, 8)
            for t in range(NT):
                e.wait_ge(up_mm, t + 1)
                b = 4 * (t % 2)
                e.activation(qn[:, t].rearrange("p (b h) d -> p b (h d)", b=2), ps[:, b:b + 2, 0:NHD // 2 * QK], ACT.Copy,
                             scale=zstat[:, 4 * NT + t:4 * NT + t + 1]).then_inc(up_out, 1)
                kv = ps[:, b + 2:b + 4].rearrange("p b (h d) -> p (b h) d", d=NOPE + VH)
                e.activation(kn[:, t], kv[:, :, 0:NOPE], ACT.Copy, scale=zstat[:, 5 * NT + t:5 * NT + t + 1])
                e.activation(vn[:, t], kv[:, :, NOPE:NOPE + VH], ACT.Copy, scale=zstat[:, 5 * NT + t:5 * NT + t + 1])\
                    .then_inc(up_out, 1)
                e.wait_ge(up_out, 2 * t + 2)
                if t >= 2:
                    e.wait_ge(qk_sum_t, t - 1)
                sl = sq[:, t % 2]
                e.activation(sl[:, 0:NHD * QK], qn[:, t].rearrange("p h d -> p (h d)"), ACT.Square).then_inc(qk_sq, 1)
                e.activation(sl[:, NHD * QK:NHD * (QK + NOPE)], kn[:, t].rearrange("p h d -> p (h d)"), ACT.Square)\
                    .then_inc(qk_sq, 1)

            for u in range(4):
                act_head_unit(e, 0, 0, u, True)
            act_max_hi(e, 0, 0)
            act_v(e, 0, 0, True)

            def unit(i, m, first, last):
                for p in range(THALF):
                    if p == 0 and not (first and m < 2):
                        act_pv_copy(e, *at(i, m - 1))
                    if m % NH == 0 and not (last and m // NH == 1):
                        act_head_unit(e, *next_head(i, m), p)
                    if p == 3 and not (last and m == NU - 1):
                        act_max_hi(e, i, m + 1)
                    if last and m == 2 and p < 2:
                        act_ln_square(e, 2 * p)
                        act_ln_square(e, 2 * p + 1)
                    if p == 3 and m % NH == 1 and not (last and m // NH == 1):
                        act_v(e, *next_head(i, m), first=first and m == 1)
                    act_exp(e, i, m, p)
                    if last and (m, p) in WO_AT:
                        act_wo_hi(e, WO_AT[m, p])
                    if not last:
                        for n in products(m, p, p + 1):
                            act_prod(e, i, n, first)

            run_units(e, unit)
            act_pv_copy(e, TURNS, -1)
            act_ln_swish(e)
            act_pv_copy(e, TURNS, 0)
            act_wo_hi(e, KC - 1)
            f, n = fs[1], ns[2]

            def weights_between(u):
                if u == 2:
                    for c in range(CPG):
                        act_hi_gu(e, f, 0, c, None)

            act_norm(e, n, SH2, S2, lambda t: e.wait_ge(mix_added, 2 * t + 2), weights_between,
                     lambda: e.wait_ge(mix_mm, 2 * NT))
            act_ffn(e, f, n)
            for t in range(NT):
                e.wait_ge(f.added, (GROUPS - 1) * 2 * NT + 2 * t + 2)
                if t >= 2:
                    e.wait_ge(sumsq, FINAL + t - 1)
                e.activation(ada_raw[:, t % 2], H[:, t], ACT.Square, accum_out=stat[:, t:t + 1]).then_inc(sumsq, 1)

        @block.vector
        def _(e):
            e.wait_ge(vec_tr, 1)
            e.tensor_copy(vect[:], ps[:, MISC, 0:NV]).then_inc(vec_ok, 2)
            e.wait_ge(vec_ok, 2)
            e.wait_ge(vec_in, 16 * 10)
            e.tensor_scalar(gains[0:QK, 0:1], gains[0:QK, 0:1], float(QK) ** -0.5, None, ALU.mult).then_inc(vec_ok, 1)
            e.wait_ge(silu_ok, 1)
            f, n = fs[0], ns[0]
            for v in range(2):
                for kc in range(KC):
                    e.wait_ge(ada01_in[v][kc // 2], 16)
                    dve_ada_piece(e, v, kc, ada01[:, v, kc])
                dve_ada_column(e, v)
                if v == 0:
                    dve_lo_gu(e, f, 0, 0, 0)
            dve_cut_x(e, n, range(3))
            dve_lo_gu(e, f, 0, 0, 1)
            dve_cut_x(e, n, range(3, KC))
            for m in range(2):
                dve_lo_gu(e, f, 0, 1, m)
            for kc in range(2):
                dve_ada_piece(e, G1, kc)
            dve_cut_x(e, n, range(KC, 2 * KC))
            dve_first(e, f)
            dve_turns(e, f, True)
            e.wait_ge(mod_ok, N_MOD - 1)
            for v in (SMX, S2):
                e.tensor_scalar(modc[:, v * KC:(v + 1) * KC], modc[:, v * KC:(v + 1) * KC], 1.0, None, ALU.add)\
                    .then_inc(mod_ok, 1)

            n = ns[1]
            for m in range(2):
                dve_lo_gu(e, U, 0, 0, m)
            FIRST_UNIT_AT = 2 * NT - KC + 2
            for k in range(2 * NT):
                dve_add(e, f, GROUPS - 1, [k])
                if k >= FIRST_UNIT_AT:
                    dve_cut_x(e, n, [k - FIRST_UNIT_AT])
            dve_cut_x(e, n, range(2 * NT - FIRST_UNIT_AT, KC))
            for m in range(2):
                dve_lo_gu(e, U, 0, 1, m)
            e.wait_ge(small_in, 32)
            e.tensor_copy(posf[:], posr[:]).then_inc(pos_ok, 1)
            dve_cut_x(e, n, range(KC, 2 * KC))

            k = [0]

            def link(ins):
                k[0] += 1
                ins.then_inc(dve_step, 1)
                e.wait_ge(dve_step, k[0])

            def glu(s):
                g, (c, h) = s // 4, (FIRST_STEPS if s < 4 else STEPS)[s % 4]
                e.wait_ge(U.silu, s + 1)
                if s == 0:
                    e.wait_ge(h_saved, 16 * NT)
                e.tensor_tensor(ac[:, 2 * g + c, CONV_PAD + h * HALF:CONV_PAD + (h + 1) * HALF],
                                ps[:, 2 * (s % 2) + 1], tmp[:, s % 2], ALU.mult).then_inc(U.mul, 1)

            for b in range(2):
                glu(b)
                e.wait_ge(wl_hi, b + 1)
                part = slice(b * NZ, (b + 1) * NZ)
                e.tensor_tensor(wl[:, LO, :, part], (lata, latb)[b][:], wl[:, HI, :, part].bitcast(F32), ALU.subtract)\
                    .then_inc(wl_lo, 1)
            e.wait_ge(pos_ok, 2)
            link(e.tensor_copy(posc[:], ps[:, MISC, 0:NT]))
            e.wait_ge(h_saved, 16 * NT)
            e.tensor_copy(cw[:, :, 0:CONV_K], ps[:, MISC, 64:64 + 32 * CC].rearrange("p (c k) -> p c k", k=32)[:, :, 0:CONV_K])\
                .then_inc(cw_ok, 1)
            RH = ROPE // 2
            e.wait_ge(pads, 1)
            link(e.tensor_tensor(trig[:, 0], posc[:].unsqueeze(2).broadcast_to([P, NT, ROPE]),
                                 trig[:, 2, 0:1].broadcast_to([P, NT, ROPE]), ALU.mult))
            for h in range(2):
                part = slice(h * RH, (h + 1) * RH)
                e.tensor_scalar(trig[:, 1, :, part], trig[:, 0, :, part], 1.0 / (2 * np.pi), (0.25, 0.0)[h], ALU.mult, ALU.add)\
                    .then_inc(dve_step, 1)
                k[0] += 1
            e.wait_ge(dve_step, k[0])
            link(e.tensor_scalar(trig[:, 1], trig[:, 1], ROUND, ROUND, ALU.add, ALU.subtract))
            for part in TWO_PI:
                link(e.scalar_tensor_tensor(out=trig[:, 0], in0=trig[:, 1], scalar=-part, in1=trig[:, 0], op0=ALU.mult,
                                            op1=ALU.add))
            link(e.tensor_scalar(trig[:, 0, :, 0:RH], trig[:, 0, :, 0:RH], float(np.pi / 2), None, ALU.add))
            e.tensor_scalar(trig[:, 3], trig[:, 0], PI_IN, -PI_IN, ALU.min, ALU.max).then_inc(trig_ok, 1)
            glu(2)
            dve_lo_gu(e, U, 1, 0, 0)
            dve_lo_gu(e, U, 1, 0, 1)
            glu(3)
            dve_lo_gu(e, U, 1, 1, 0)
            dve_lo_gu(e, U, 1, 1, 1)
            e.wait_ge(cw_ok, 1)
            e.wait_ge(U.mul, 4)
            e.wait_ge(cs_ok, 1)
            dve_tap0(e, 0, conv)
            dve_tap0(e, 1, conv)
            dve_conv(e, 1, 14)
            glu(4)
            for v in range(6):
                e.wait_ge(z_hi, v + 1)
                c, h = divmod(v, 2)
                tok = slice(h * HALF, (h + 1) * HALF)
                e.tensor_tensor(CZ[LO][:, c, tok], ps[:, 4 + v % 3], CZ[HI][:, c, tok].bitcast(F32), ALU.subtract)\
                    .then_inc(z_lo, 1)
            dve_row_diag(e, GM, gm_row)
            e.wait_ge(up_in[0], 16)
            for c in range(QL // P):
                w = wqr[:, c, 0:NHD * QK]
                e.tensor_scalar(w, w, vect[:, V_GQ + c:V_GQ + c + 1], None, ALU.mult).then_inc(up_scaled, 1)
            e.wait_ge(up_in[1], 16)
            e.tensor_scalar(wkr, wkr, vect[:, V_GKV:V_GKV + 1], None, ALU.mult).then_inc(up_scaled, 1)
            glu(5)
            e.wait_ge(up_hi, 1)
            e.tensor_tensor(wq[:, LO], wqr[:, :, 0:NHD * QK], wq[:, HI].bitcast(F32), ALU.subtract).then_inc(up_lo, 1)
            e.wait_ge(up_hi, 2)
            e.tensor_tensor(wkv[:, LO], wkr, wkv[:, HI].bitcast(F32), ALU.subtract).then_inc(up_lo, 1)
            dve_conv(e, 14, DT)
            glu(6)
            glu(7)
            dve_row_copy(e, 0, gm_row)
            e.wait_ge(U.mul, 8)
            e.memset(vs[:, :, :, VH:2 * VH], 1.0).then_inc(k_ones, 1)
            dve_tap0(e, 2, tap0)
            dve_tap0(e, 3, tap0)
            krs = zstat[:, 0:NT]
            e.wait_ge(z_rstd, 2)
            flat = rt[:, 0:2].rearrange("p a t h d -> p (a t h d)")
            k2 = flat[:, 0:NT * ROPE].rearrange("p (t d) -> p t d", t=NT)
            link(e.tensor_tensor(k2, kr[:], kr[:], ALU.mult))
            e.tensor_reduce(krs, k2, AX_X, ALU.add)
            e.wait_ge(grot_in, 32)
            link(e.tensor_tensor(kr[:], kr[:], grot[:, 1:2].broadcast_to([P, NT, ROPE]), ALU.mult))
            cos, sin = cs[:, :, 0:RH], cs[:, :, RH:ROPE]
            part = [rt[:, 2, n].rearrange("p h d -> p (h d)")[:, 0:NT * RH].rearrange("p (t d) -> p t d", t=NT) for n in range(4)]
            x1, x2 = kr[:, :, 0:RH], kr[:, :, RH:ROPE]
            for to, a, b in ((part[0], x1, cos), (part[1], x2, sin), (part[2], x2, cos), (part[3], x1, sin)):
                link(e.tensor_tensor(to, a, b, ALU.mult))
            link(e.tensor_tensor(x1, part[0], part[1], ALU.subtract))
            e.tensor_tensor(x2, part[2], part[3], ALU.add).then_inc(rope, 1)
            def rotate_q(t, stage):
                rot = qn[:, t, :, NOPE:QK]
                pair = rot.rearrange("p h (s d) -> p h s d", s=2)
                by = [c[:, t:t + 1].unsqueeze(2).broadcast_to([P, NHD, 2, RH]) for c in (cos, sin)]
                to = [rt[:, 2 * n:2 * n + 2, t].rearrange("p s h d -> p h s d") for n in range(2)]
                if stage == 0:
                    e.tensor_tensor(rot, rot, grot[:, 0:1].broadcast_to([P, NHD, ROPE]), ALU.mult).then_inc(rot_step, 1)
                elif stage == 1:
                    e.wait_ge(rot_step, 3 * t + 1)
                    for n in range(2):
                        e.tensor_tensor(to[n], pair, by[n], ALU.mult).then_inc(rot_step, 1)
                else:
                    e.wait_ge(rot_step, 3 * t + 3)
                    e.tensor_tensor(pair[:, :, 0], to[0][:, :, 0], to[1][:, :, 1], ALU.subtract)
                    e.tensor_tensor(pair[:, :, 1], to[0][:, :, 1], to[1][:, :, 0], ALU.add).then_inc(rope, 1)

            for t in range(NT):
                e.wait_ge(qk_sq, 2 * t + 1)
                rotate_q(t, 0)
                sl = sq[:, t % 2]
                e.tensor_reduce(qs[:, t, 0:NHD], sl[:, 0:NHD * QK].rearrange("p (h d) -> p h d", d=QK), AX_X, ALU.add)
                rotate_q(t, 1)
                e.wait_ge(qk_sq, 2 * t + 2)
                e.tensor_reduce(qs[:, t, NHD:2 * NHD], sl[:, NHD * QK:NHD * (QK + NOPE)].rearrange("p (h d) -> p h d", d=NOPE),
                                AX_X, ALU.add).then_inc(qk_sum_t, 1)
                rotate_q(t, 2)
                if t % THALF == THALF - 1:
                    tiles = slice(t + 1 - THALF, t + 1)
                    e.wait_ge(qk_sum_t, t + 1)
                    e.tensor_tensor(qs[:, tiles, NHD:2 * NHD], qs[:, tiles, NHD:2 * NHD],
                                    krs[:, tiles].unsqueeze(2).broadcast_to([P, THALF, NHD]), ALU.add).then_inc(qk_sum, 1)
            for u in range(2):
                dve_head_unit(e, 0, 0, u, True)
            e.tensor_copy(qkT[QK:AUG, :, 1, HI], ones[QK:AUG, 0:1].unsqueeze(2).broadcast_to([1, 2, S])).then_inc(k_ones, 1)
            e.tensor_scalar(qkT[QK:AUG, :, 1, LO], ones[QK:AUG, 0:1].unsqueeze(2).broadcast_to([1, 2, S]), 0.0, None,
                            ALU.mult).then_inc(k_ones, 1)
            e.wait_ge(rope, 1 + NT)

            for u in range(2, 4):
                dve_head_unit(e, 0, 0, u, True)
            for p in range(THALF):
                dve_max(e, 0, 0, p, True)
            dve_max_lo(e, 0, 0)

            def unit(i, m, first, last):
                for p in range(THALF):
                    if not (last and m == NU - 1):
                        dve_max(e, i, m + 1, p)
                    if p == 3 and not (last and m == NU - 1):
                        dve_max_lo(e, i, m + 1)
                    if m % NH == 0:
                        if not (last and m // NH == 1):
                            dve_head_unit(e, *next_head(i, m), p)
                    elif not last:
                        dve_tap(e, i * DTT + (DT + m // NH * 2 + p // 2), (p % 2,))
                    if not (first and m < 2):
                        if p < 3:
                            dve_pv_recip(e, *at(i, m - 1), p)
                        else:
                            dve_pv_scale(e, *at(i, m - 1))
                    if last and m == 1 and p in (1, 2):
                        dve_ln_mean(e, p - 1)
                    if last and m == 3 and p == 1:
                        dve_ln_var(e)
                    if last and (m, p) in WO_AT:
                        dve_wo_lo(e, WO_AT[m, p])
                    if last and m == 3 and p == 2:
                        dve_ln_diag(e)

            run_units(e, unit)

            def cut_mix(t, part):
                if t == 0 and part == 0:
                    e.wait_ge(ln_act, 2 * CC)
                    e.wait_ge(s_mm, 4 * NU * TURNS)
                if t == 0 and part == 1:
                    e.wait_ge(pv_out, NU * TURNS)
                if t >= 2:
                    e.wait_ge(mix_mm, 2 * t - 2)
                dst = mixT[:, t % 2, HI, part * CC:(part + 1) * CC]
                e.tensor_copy(dst, mix_src(part, t)).then_inc(mix_hi, 1)
                e.wait_ge(mix_hi, 2 * t + part + 1)
                dst = mixT[:, t % 2, LO, part * CC:(part + 1) * CC]
                e.tensor_tensor(dst, mix_src(part, t), mixT[:, t % 2, HI, part * CC:(part + 1) * CC].bitcast(F32),
                                ALU.subtract).then_inc(mix_lo, 1)

            dve_pv_recip(e, TURNS, -1, 0)
            dve_pv_recip(e, TURNS, -1, 1)
            dve_ln_scale(e)
            dve_pv_recip(e, TURNS, -1, 2)
            dve_pv_scale(e, TURNS, -1)
            cut_mix(0, 0)
            for third in range(3):
                dve_pv_recip(e, TURNS, 0, third)
            dve_pv_scale(e, TURNS, 0)
            cut_mix(0, 1)
            dve_wo_lo(e, KC - 1)
            for t in range(NT):
                if t + 1 < NT:
                    cut_mix(t + 1, 0)
                    cut_mix(t + 1, 1)
                for h in range(2):
                    e.wait_ge(mix_mm, 2 * t + h + 1)
                    e.wait_ge(h_back[t // THALF], 16)
                    dst = H[:, t, h * HALF:(h + 1) * HALF]
                    e.tensor_tensor(dst, ps[:, 4 + (2 * t + h) % MB], dst, ALU.add).then_inc(mix_added, 1)
                    if (t, h) == (NT - 1, 0):
                        for m in range(2):
                            dve_lo_gu(e, fs[1], 0, 0, m)

            f, n = fs[1], ns[2]
            dve_cut_x(e, n, range(KC))
            for m in range(2):
                dve_lo_gu(e, f, 0, 1, m)
            dve_cut_x(e, n, range(KC, 2 * KC))
            dve_first(e, f)
            dve_turns(e, f, False)
            e.wait_ge(gfin_in, 16)

            def final(t):
                e.wait_ge(rms_inv, FINAL + t + 1)
                e.scalar_tensor_tensor(out=H[:, t], in0=H[:, t], scalar=stat[:, 2 * NT + t:2 * NT + t + 1], in1=grow[:],
                                       op0=ALU.mult, op1=ALU.mult).then_inc(o_ok, 1)

            for t in range(NT):
                dve_add(e, f, GROUPS - 1, (2 * t, 2 * t + 1))
                if t >= 2:
                    final(t - 2)
            final(NT - 2)
            final(NT - 1)

        @block.tensor
        def _(e):
            e.wait_ge(consts, 5)
            e.wait_ge(vec_in, 16 * 10)
            e.transpose(ps[:, MISC, 0:NV], vec[0:NV], ident[0:NV, 0:NV]).then_inc(vec_tr, 1)
            e.wait_ge(vec_ok, 2)
            f, n = fs[0], ns[0]
            AHEAD = len(n.banks[0])
            for u in range(AHEAD):
                pe_turn_unit(e, n, u)
            for v in range(2):
                pe_ada_sum(e, v)

            def gate1_row():
                pe_ada_half(e, G1, 0)
                pe_ada_half(e, G1, 1)

            pe_gateup(e, f, n, 0, first=True, after={3: gate1_row}, ahead=AHEAD)
            pe_turns(e, f, n, True)

            n = ns[1]
            for k in range(2 * NT):
                pe_down(e, f, GROUPS - 1, 0, [k], WDL)
                if k >= 2 * NT - KC + 1:
                    pe_turn_unit(e, n, k - (2 * NT - KC + 1))
            pe_turn_unit(e, n, KC - 1)

            def small_turns():
                e.wait_ge(small_in, 32)
                e.wait_ge(pos_ok, 1)
                for c in range(CC):
                    e.transpose(ps[:, MISC, 64 + 32 * c:64 + 32 * c + CONV_K], cwr[0:CONV_K, c * P:(c + 1) * P],
                                ident[0:CONV_K, 0:CONV_K])
                e.transpose(ps[:, MISC, 0:NT], posf[:], ident[0:NT, 0:NT]).then_inc(pos_ok, 1)

            pe_gateup(e, U, n, 0, first=True, after={2: small_turns})
            e.wait_ge(wl_lo, 2)
            for t in range(NT):
                if t >= 3:
                    e.wait_ge(z_sq, 2 * (t - 2))
                k = 0
                for kc in range(KC):
                    for wx, xx in PASSES:
                        mm = e.matmul(ps[:, 4 + t % 3, 0:W_IN_L], X[xx][:, kc, t * P:(t + 1) * P], wl[:, wx, kc],
                                      start=(k == 0), stop=(k == 3 * KC - 1))
                        k += 1
                mm.then_inc(lat_mm, 1)

            def turn_latents():
                e.wait_ge(z_sq, 2 * NT)
                for v in range(6):
                    c, h = divmod(v, 2)
                    if v >= 3:
                        e.wait_ge(z_lo, v - 2)
                    for k in range(THALF):
                        mm = e.transpose(ps[:, 4 + v % 3, k * P:(k + 1) * P], zz[:, h * THALF + k, c * P:(c + 1) * P],
                                         ident[:])
                    mm.then_inc(z_turned, 1)

            pe_gateup(e, U, n, 1, after={0: turn_latents})
            e.wait_ge(z_lo, 6)
            pe_row(e, 0, gm_row)
            e.wait_ge(up_lo, 2)
            e.wait_ge(U.mul, 8)
            for t in range(NT):
                b = 4 * (t % 2)
                if t == 1:
                    e.wait_ge(row_ok, 2)
                if t >= 2:
                    e.wait_ge(up_out, 2 * t - 2)
                tok = slice(t * P, (t + 1) * P)
                for h in range(2):
                    k = 0
                    for c in range(QL // P):
                        for wx, xx in PASSES:
                            e.matmul(ps[:, b + h, 0:NHD // 2 * QK], CZ[xx][:, c, tok],
                                     wq[:, wx, c, h * (NHD // 2 * QK):(h + 1) * (NHD // 2 * QK)], start=(k == 0),
                                     stop=(k == 3 * (QL // P) - 1))
                            k += 1
                for h in range(2):
                    for k, (wx, xx) in enumerate(PASSES):
                        mm = e.matmul(ps[:, b + 2 + h], CZ[xx][:, QL // P, tok], wkv[:, wx, h * HALF:(h + 1) * HALF],
                                      start=(k == 0), stop=(k == 2))
                mm.then_inc(up_mm, 1)

            e.wait_ge(up_out, 2 * NT - 2)
            pe_turn_head(e, 0, 0, 0, True)
            pe_turn_head(e, 0, 0, 1, True)
            e.wait_ge(up_out, 2 * NT)
            pe_turn_head(e, 0, 0, 2, True)
            pe_turn_head(e, 0, 0, 3, True)
            for p in range(THALF):
                pe_max(e, 0, 0, p, True)
            pe_max_row(e, 0, 0, True)
            e.wait_ge(k_ones, 3)

            def unit(i, m, first, last):
                for p in range(THALF):
                    if m % NH == 0 and not (last and m // NH == 1):
                        pe_turn_head(e, *next_head(i, m), p)
                    if not (last and m == NU - 1):
                        pe_max(e, i, m + 1, p)
                    pe_scores(e, i, m, p)
                    if p == THALF - 1 and not (last and m == NU - 1):
                        pe_max_row(e, i, m + 1)
                    if last and m == 1 and p in (1, 2):
                        pe_ln_mean(e, p - 1)
                    if last and m == 3 and p == 1:
                        pe_ln_var(e)
                    if not (first and m == 0):
                        pe_pv(e, i, m, p)

            run_units(e, unit)
            pe_ln_rstd(e)
            for p in range(THALF):
                pe_pv(e, TURNS, 0, p)
            def pe_mix(m, part):
                t, h = divmod(m, 2)
                if part == 0:
                    if m >= MB:
                        e.wait_ge(mix_added, m - MB + 1)
                    elif m == 2:
                        e.wait_ge(pv_copied, NU * TURNS)
                if h == 0:
                    e.wait_ge(mix_lo, 2 * t + 1 + part)
                for c in range(part * CC, (part + 1) * CC):
                    if m == 0 and c in (0, KC - 1):
                        e.wait_ge(wo_lo, KC - 1 if c == 0 else KC)
                    for k, (wx, xx) in enumerate(PASSES):
                        mm = e.matmul(ps[:, 4 + m % MB], mixT[:, t % 2, xx, c], wo[:, c, wx, h * HALF:(h + 1) * HALF],
                                      start=(c == 0 and k == 0), stop=(c == KC - 1 and k == 2))
                if part == 1:
                    mm.then_inc(mix_mm, 1)

            for m, part in ((0, 0), (1, 0), (0, 1), (1, 1)):
                pe_mix(m, part)
            for m in range(2, 2 * NT):
                pe_mix(m, 0)
                pe_mix(m, 1)
                if m == 2 * NT - 3:
                    for u in range(5):
                        pe_turn_unit(e, ns[2], u)
            f, n = fs[1], ns[2]
            pe_gateup(e, f, n, 0, first=True, after={3: lambda: pe_row(e, 1)}, ahead=5)
            pe_turns(e, f, n, False)
            pe_down(e, f, GROUPS - 1, 0, range(2 * NT), WDL)


_INS = ["x", "c", "positions", "w_ada", "b_ada", "ffn1_wg", "ffn1_wu", "ffn1_wd", "w_in", "g_q_lat", "g_kv_lat",
        "w_q_up", "w_kv_up", "g_q_head", "g_k_head", "conv_w", "conv_b", "g_conv_ln", "b_conv_ln", "w_out",
        "ffn2_wg", "ffn2_wu", "ffn2_wd", "g_final"]


def kernel(**inputs):
    import concourse.bacc as bacc
    from concourse.bass_utils import run_bass_kernel_spmd as run

    nc = bacc.Bacc("TRN2", target_bir_lowering=False, num_devices=1, dynamic_dma_scratch_size=1024)
    arrays, A = {}, {}
    for name in _INS:
        a = np.ascontiguousarray(inputs[name])
        arrays[f"in_{name}"] = a
        A[name] = nc.dram_tensor(f"in_{name}", a.shape, mybir.dt.from_np(a.dtype), kind="ExternalInput").ap()
    out = nc.dram_tensor("out", inputs["x"].shape, F32, kind="ExternalOutput").ap()
    build(nc, A, out)
    r = run(nc, [arrays], core_ids=[0])
    return r.results[0]["out"]
```
